# Optimizing a Trainium2 kernel written in Bass

```python
import math
import jax, jax.numpy as jnp
from jax import lax
import numpy as np

D_MODEL = 1024
BATCH = 1
SEQ = 1024
DEPTH = 1

EPS = 1e-6
CONV_CH = D_MODEL
CONV_WIDTH = 31
N_HEADS = 8
QK_NOPE = 128
QK_ROPE = 64
V_DIM = 128
Q_LORA = 256
KV_LORA = 128
ROPE_BASE = 10000.0
Q_BLOCK = 128
N_KEYS = 128
N_EXPERTS = N_KEYS * N_KEYS
PEER_HEADS = 8
PEER_DK = 256
PEER_TOPK = 16
TOKEN_BLOCK = 128
IN_SPLITS = (CONV_CH, 2 * CONV_CH, 2 * CONV_CH + Q_LORA, 2 * CONV_CH + Q_LORA + KV_LORA + QK_ROPE)
IN_WIDTH = 2 * CONV_CH + Q_LORA + KV_LORA + QK_ROPE + 2 * D_MODEL

kernel_name = "hybrid_conv_mla_peer_block"

def rmsnorm(x, g):
    xf = x.astype(jnp.float32)
    y = xf * lax.rsqrt(jnp.mean(xf * xf, axis=-1, keepdims=True) + EPS)
    return (y * g.astype(jnp.float32)).astype(x.dtype)

def layernorm(x, g, b):
    xf = x.astype(jnp.float32)
    mu = jnp.mean(xf, axis=-1, keepdims=True)
    var = jnp.mean(jnp.square(xf - mu), axis=-1, keepdims=True)
    y = (xf - mu) * lax.rsqrt(var + EPS)
    return (y * g.astype(jnp.float32) + b.astype(jnp.float32)).astype(x.dtype)

def apply_rope(t, positions):
    half = t.shape[-1] // 2
    inv_freq = ROPE_BASE ** (-jnp.arange(half, dtype=jnp.float32) / half)
    ang = positions.astype(jnp.float32)[..., None] * inv_freq
    cos = jnp.cos(ang)[:, :, None, :]
    sin = jnp.sin(ang)[:, :, None, :]
    tf = t.astype(jnp.float32)
    t1, t2 = tf[..., :half], tf[..., half:]
    out = jnp.concatenate([t1 * cos - t2 * sin, t2 * cos + t1 * sin], axis=-1)
    return out.astype(t.dtype)

def conformer_conv(val, gate, w_dw, b_dw, ln_g, ln_b, w_pw):
    h = val * jax.nn.sigmoid(gate)
    h = lax.conv_general_dilated(
        h, w_dw, window_strides=(1,), padding=[(CONV_WIDTH - 1, 0)],
        dimension_numbers=("NWC", "WIO", "NWC"), feature_group_count=CONV_CH) + b_dw
    h = jax.nn.silu(layernorm(h, ln_g, ln_b))
    return h @ w_pw

def mla(c_q, c_kv_full, positions, q_norm_g, w_uq, kv_norm_g, w_ukv):
    B, S, _ = c_q.shape
    c_kv, k_rope = c_kv_full[..., :KV_LORA], c_kv_full[..., KV_LORA:]
    q = (rmsnorm(c_q, q_norm_g) @ w_uq).reshape(B, S, N_HEADS, QK_NOPE + QK_ROPE)
    q_nope, q_rope = q[..., :QK_NOPE], apply_rope(q[..., QK_NOPE:], positions)
    kv = (rmsnorm(c_kv, kv_norm_g) @ w_ukv).reshape(B, S, N_HEADS, QK_NOPE + V_DIM)
    k_nope, v = kv[..., :QK_NOPE], kv[..., QK_NOPE:]
    k_rope = apply_rope(k_rope[:, :, None, :], positions)[:, :, 0, :]
    scale = 1.0 / math.sqrt(QK_NOPE + QK_ROPE)
    nb = S // Q_BLOCK
    qn_b = jnp.moveaxis(q_nope.reshape(B, nb, Q_BLOCK, N_HEADS, QK_NOPE), 1, 0)
    qr_b = jnp.moveaxis(q_rope.reshape(B, nb, Q_BLOCK, N_HEADS, QK_ROPE), 1, 0)
    starts = jnp.arange(nb, dtype=jnp.int32) * Q_BLOCK
    k_pos = jnp.arange(S, dtype=jnp.int32)

    def attend(args):
        qn, qr, start = args
        s = (jnp.einsum("bqhd,bkhd->bhqk", qn, k_nope)
             + jnp.einsum("bqhr,bkr->bhqk", qr, k_rope)).astype(jnp.float32) * scale
        q_pos = start + jnp.arange(Q_BLOCK, dtype=jnp.int32)
        mask = k_pos[None, :] <= q_pos[:, None]
        s = jnp.where(mask[None, None], s, -1e30)
        p = jax.nn.softmax(s, axis=-1).astype(v.dtype)
        return jnp.einsum("bhqk,bkhd->bqhd", p, v)

    o = lax.map(attend, (qn_b, qr_b, starts))
    return jnp.moveaxis(o, 0, 1).reshape(B, S, N_HEADS * V_DIM)

def peer(x, w_pq, sub_keys, u, v):
    B, S, D = x.shape
    xb_all = x.reshape(-1, TOKEN_BLOCK, D)

    def block(xb):
        q = (xb @ w_pq).reshape(TOKEN_BLOCK, PEER_HEADS, 2, PEER_DK // 2)
        s = jnp.einsum("thpd,hpkd->thpk", q, sub_keys).astype(jnp.float32)
        s_top, i_top = lax.top_k(s, PEER_TOPK)
        cand_s = s_top[:, :, 0, :, None] + s_top[:, :, 1, None, :]
        cand_i = i_top[:, :, 0, :, None] * N_KEYS + i_top[:, :, 1, None, :]
        cand_s = cand_s.reshape(TOKEN_BLOCK, PEER_HEADS, PEER_TOPK * PEER_TOPK)
        cand_i = cand_i.reshape(TOKEN_BLOCK, PEER_HEADS, PEER_TOPK * PEER_TOPK)
        best_s, best_pos = lax.top_k(cand_s, PEER_TOPK)
        idx = jnp.take_along_axis(cand_i, best_pos, axis=-1)
        g = jax.nn.softmax(best_s, axis=-1)
        ue = jnp.take(u, idx, axis=0)
        act = jax.nn.gelu(jnp.einsum("thkd,td->thk", ue, xb).astype(jnp.float32), approximate=False)
        ve = jnp.take(v, idx, axis=0)
        return jnp.einsum("thk,thkd->td", (g * act).astype(ve.dtype), ve)

    return lax.map(block, xb_all).reshape(B, S, D)

def setup_inputs(seed: int = 0) -> dict:
    key = jax.random.key(seed)
    ks = jax.random.split(key, 24)
    f32 = jnp.float32
    nrm = lambda k, shape, scale: jax.random.normal(k, shape, f32) * scale
    L = DEPTH
    x = jax.random.normal(ks[0], (BATCH, SEQ, D_MODEL), f32)
    offset = jax.random.randint(ks[1], (BATCH, 1), 0, 1024, dtype=jnp.int32)
    positions = (offset + jnp.arange(SEQ, dtype=jnp.int32)[None, :]).astype(jnp.int32)
    return {
        "x": x,
        "positions": positions,
        "mix_norm_g": 1.0 + nrm(ks[2], (L, D_MODEL), 0.02),
        "w_in": nrm(ks[3], (L, D_MODEL, IN_WIDTH), D_MODEL ** -0.5),
        "b_gate": nrm(ks[4], (L, 2 * D_MODEL), 0.1),
        "w_dw": nrm(ks[5], (L, CONV_WIDTH, 1, CONV_CH), CONV_WIDTH ** -0.5),
        "b_dw": nrm(ks[6], (L, CONV_CH), 0.02),
        "conv_ln_g": 1.0 + nrm(ks[7], (L, CONV_CH), 0.02),
        "conv_ln_b": nrm(ks[8], (L, CONV_CH), 0.02),
        "w_conv_out": nrm(ks[9], (L, CONV_CH, D_MODEL), CONV_CH ** -0.5),
        "q_norm_g": 1.0 + nrm(ks[10], (L, Q_LORA), 0.02),
        "w_uq": nrm(ks[11], (L, Q_LORA, N_HEADS * (QK_NOPE + QK_ROPE)), Q_LORA ** -0.5),
        "kv_norm_g": 1.0 + nrm(ks[12], (L, KV_LORA), 0.02),
        "w_ukv": nrm(ks[13], (L, KV_LORA, N_HEADS * (QK_NOPE + V_DIM)), KV_LORA ** -0.5),
        "w_attn_out": nrm(ks[14], (L, N_HEADS * V_DIM, D_MODEL), (N_HEADS * V_DIM) ** -0.5),
        "w_o": nrm(ks[15], (L, D_MODEL, D_MODEL), D_MODEL ** -0.5),
        "ffn_norm_g": 1.0 + nrm(ks[16], (L, D_MODEL), 0.02),
        "w_peer_q": nrm(ks[17], (L, D_MODEL, PEER_HEADS * PEER_DK), D_MODEL ** -0.5),
        "peer_sub_keys": nrm(ks[18], (L, PEER_HEADS, 2, N_KEYS, PEER_DK // 2), (PEER_DK // 2) ** -0.5),
        "peer_u": nrm(ks[19], (L, N_EXPERTS, D_MODEL), D_MODEL ** -0.5),
        "peer_v": nrm(ks[20], (L, N_EXPERTS, D_MODEL), 0.5),
        "final_norm_g": 1.0 + nrm(ks[21], (D_MODEL,), 0.02),
    }

def reference(x, positions, mix_norm_g, w_in, b_gate, w_dw, b_dw, conv_ln_g, conv_ln_b, w_conv_out,
              q_norm_g, w_uq, kv_norm_g, w_ukv, w_attn_out, w_o, ffn_norm_g, w_peer_q,
              peer_sub_keys, peer_u, peer_v, final_norm_g):
    h = x
    for l in range(DEPTH):
        a = rmsnorm(h, mix_norm_g[l])
        z = a @ w_in[l]
        conv_val, conv_gate, c_q, c_kv, gate_logits = jnp.split(z, IN_SPLITS, axis=-1)
        y_conv = conformer_conv(conv_val, conv_gate, w_dw[l], b_dw[l], conv_ln_g[l], conv_ln_b[l], w_conv_out[l])
        y_attn = mla(c_q, c_kv, positions, q_norm_g[l], w_uq[l], kv_norm_g[l], w_ukv[l]) @ w_attn_out[l]
        gates = jax.nn.sigmoid(gate_logits + b_gate[l])
        g_conv, g_attn = gates[..., :D_MODEL], gates[..., D_MODEL:]
        h = h + (g_conv * y_conv + g_attn * y_attn) @ w_o[l]
        h = h + peer(rmsnorm(h, ffn_norm_g[l]), w_peer_q[l], peer_sub_keys[l], peer_u[l], peer_v[l])
    return rmsnorm(h, final_norm_g)


_drawn_inputs = setup_inputs


def setup_inputs(seed=0):
    import zlib

    import numpy as np

    out = dict(_drawn_inputs(seed))
    spreads = {}
    factors = {'conv_ln_b': 16.657,
     'q_norm_g': 5.731,
     'kv_norm_g': 5.232,
     'final_norm_g': 7.554,
     'b_dw': 7.102,
     'conv_ln_g': 8.0,
     'ffn_norm_g': 4.244}
    for name, (base, spread) in spreads.items():
        noise = np.random.default_rng([zlib.crc32(name.encode()), seed]).standard_normal(out[name].shape)
        drawn = base * np.exp(spread * noise) if base else spread * noise
        out[name] = __import__('jax').numpy.asarray(drawn.astype(out[name].dtype))
    for name, factor in factors.items():
        out[name] = (out[name] * factor).astype(out[name].dtype)
    return out
```

```python
from contextlib import ExitStack

import concourse.bass as bass
import numpy as np
from concourse import mybir

F32 = mybir.dt.float32
I32 = mybir.dt.int32
U32 = mybir.dt.uint32
ALU = mybir.AluOpType
ACT = mybir.ActivationFunctionType
AX = mybir.AxisListType

P = 128
D = 1024
S = 1024
KT = D // P
C = 512
NCH = S // C
CB = C // P
EPS = 1e-6
TAPS = 31
PAD = TAPS - 1
PE_TAPS = (9, 4)
HEADS = 8
SUBS = 4
NOPE, ROPE, VDIM = 128, 64, 128
QL = 256
QT = QL // P
SCALE = float(1.0 / np.sqrt(NOPE + ROPE))
MASKED = -1e30
ROPE_BASE = 10000.0
PH = 8
NK = 128
TOPK = 16
PICKS = PH * TOPK
RING = 8
PRE = 5
LOWEST = -3e38

G_MIX, G_Q, G_KV = 0, KT, KT + QT
G_LNG = G_KV + 1
G_LNB = G_LNG + KT
G_BGATE = G_LNB + KT
G_COLS = G_BGATE + 2 * KT


class Chip:
    pass


def item(a):
    return a.rearrange("a p n -> (a p) n")


class Alone:

    def step(self, weight):
        pass

    def finish(self):
        pass


def scope(c, ctx, prefix):
    nc, sems = c.nc, []

    def clear():
        nc.clear_and_free_semaphores(sems)
        nc.all_engine_barrier()

    def sem(name):
        sems.append(nc.alloc_semaphore(name=prefix + name))
        return sems[-1]

    ctx.callback(clear)
    return (lambda name, shape, dtype=F32: ctx.enter_context(nc.sbuf_tensor(prefix + name, shape, dtype))), sem


def mixer_inputs(c, q):
    nc, bank, ident, ones = c.nc, c.bank, c.ident, c.ones
    aT, cqT, ckvT, krT, cosT, sinT = c.aT, c.cqT, c.ckvT, c.krT, c.cosT, c.sinT
    own = slice(q * C, (q + 1) * C)
    TWO_PI = 2 * np.pi
    C1 = 6.28125
    C2 = float(np.floor((TWO_PI - C1) * 2 ** 20) / 2 ** 20)
    C3 = float(np.float32(TWO_PI - C1 - C2))
    MAGIC = float(1.5 * 2 ** 23)
    with ExitStack() as ctx:
        sb, sem = scope(c, ctx, f"q{q}inputs_")
        wpre = sb("wpre", [P, PRE, D])
        sq = sb("sq", [P, 2, C])
        rs = sb("rs", [P, C])
        posi = sb("posi", [P, C], I32)
        ang = sb("ang", [P, C])
        turns = sb("turns", [P, C])
        red = sb("red", [P, 2, C])
        rope_c = sb("rope_c", [P, 2])
        x_in = [sem(f"x_in{i}") for i in range(KT)]
        w_in = [sem(f"wpre_in{i}") for i in range(PRE)]
        small_in = sem(f"small_in")
        cst = sem(f"cst")
        squared = sem(f"squared")
        summed = sem(f"summed")
        mean_ready = sem(f"mean_ready")
        root_ready = sem(f"root_ready")
        rs_ready = sem(f"rs_ready")
        a_ready = sem(f"a_ready")
        proj = sem(f"proj")
        copied = sem(f"copied")
        roped = sem(f"roped")
        normed = sem(f"normed")
        chain = sem(f"chain")
        angles = sem(f"angles")
        tables = sem(f"tables")
        block = ctx.enter_context(nc.Block())
        N_CQ, N_CKV = QT, 1

        @block.sync
        def _(sp):
            sp.dma_start(c.gcols[:, :], c.dram["gcols"]).then_inc(small_in, 16)
            sp.dma_start(c.wdw[:, :], c.dram["wdw"]).then_inc(small_in, 16)
            for k in range(KT):
                sp.dma_start(aT[:, k, :], c.dram["xT"][k, :, own]).then_inc(x_in[k], 16)
            for i in range(PRE):
                sp.dma_start(wpre[:, i, :], c.dram["w_pre"][i]).then_inc(w_in[i], 16)
            sp.dma_start(rope_c[:, :], c.dram["rope"]).then_inc(small_in, 16)
            sp.dma_start(posi[:, :], c.dram["pos"][:, own].broadcast_to([P, C])).then_inc(small_in, 16)

        @block.gpsimd
        def _(pool):
            if q:
                return
            pool.memset(ident[:, :], 0.0).then_inc(cst, 1)
            pool.memset(c.mask[:, :], 0.0).then_inc(cst, 1)
            pool.memset(ones[:, :], 1.0).then_inc(cst, 1)
            pool.wait_ge(cst, 3)
            pool.affine_select(out=ident[:, :], in_=ident[:, :], compare_op=ALU.not_equal, fill=1.0,
                               base=0, pattern=[[-1, P]], channel_multiplier=1).then_inc(cst, 1)
            pool.affine_select(out=c.mask[:, :], in_=c.mask[:, :], compare_op=ALU.is_ge, fill=MASKED,
                               base=0, pattern=[[-1, P]], channel_multiplier=1).then_inc(cst, 1)

        groups = [KT, N_CQ, N_CKV]
        width = [D, QL, P]

        @block.scalar
        def _(act):
            def squares(g, tile, ready):
                first = sum(groups[:g])
                for k in range(groups[g]):
                    n = first + k
                    ready(k)
                    if n >= 2:
                        act.wait_ge(summed, n - 1)
                    act.activation(sq[:, n % 2, :], tile(k), ACT.Square).then_inc(squared, 1)

            def root(g):
                act.wait_ge(mean_ready, g + 1)
                act.activation(rs[:, :], rs[:, :], ACT.Sqrt).then_inc(root_ready, 1)

            squares(0, lambda k: aT[:, k, :], lambda k: act.wait_ge(x_in[k], 16))
            root(0)
            act.wait_ge(angles, 2)
            act.activation(cosT[:, :], red[:, 0, :], ACT.Sin).then_inc(tables, 1)
            act.activation(sinT[:, :], red[:, 1, :], ACT.Sin, scale=rope_c[:, 1:2]).then_inc(tables, 1)
            for n in range(N_CQ + N_CKV):
                act.wait_ge(proj, n + 1)
                act.activation(cqT[:, n, :] if n < N_CQ else ckvT[:, own], bank[:, 1 + n, :],
                               ACT.Copy).then_inc(copied, 1)
            squares(1, lambda k: cqT[:, k, :], lambda k: act.wait_ge(copied, k + 1))
            root(1)
            squares(2, lambda k: ckvT[:, own], lambda k: act.wait_ge(copied, N_CQ + 1))
            act.wait_ge(normed, N_CQ)
            root(2)

        @block.tensor
        def _(pe):
            if q == 0:
                pe.wait_ge(cst, 5)

            def sums(g):
                first = sum(groups[:g])
                if g:
                    pe.wait_ge(mean_ready, g)
                for k in range(groups[g]):
                    pe.wait_ge(squared, first + k + 1)
                    pe.matmul(bank[:, 0, :], ones[:, :], sq[:, (first + k) % 2, :],
                              start=(k == 0), stop=(k == groups[g] - 1)).then_inc(summed, 1)

            sums(0)
            pe.wait_ge(a_ready, KT)
            for n in range(PRE):
                pe.wait_ge(w_in[n], 16)
                for k in range(KT):
                    mm = pe.matmul(bank[:, 1 + n, :], wpre[:, n, k * P:(k + 1) * P], aT[:, k, :],
                                   start=(k == 0), stop=(k == KT - 1))
                mm.then_inc(proj, 1)
            sums(1)
            sums(2)

        @block.vector
        def _(dve):
            count = [0]

            def link(ins):
                count[0] += 1
                ins.then_inc(chain, 1)
                dve.wait_ge(chain, count[0])

            def mean(g):
                dve.wait_ge(summed, sum(groups[:g + 1]))
                if g == 2:
                    dve.wait_ge(normed, N_CQ)
                dve.tensor_scalar(rs[:, :], bank[:, 0, :], 1.0 / width[g], EPS,
                                  ALU.mult, ALU.add).then_inc(mean_ready, 1)
                dve.wait_ge(root_ready, g + 1)
                dve.reciprocal(rs[:, :], rs[:, :]).then_inc(rs_ready, 1)
                dve.wait_ge(rs_ready, g + 1)

            dve.wait_ge(small_in, 64)
            mean(0)
            for k in range(KT):
                dve.scalar_tensor_tensor(out=aT[:, k, :], in0=aT[:, k, :], scalar=c.gcols[:, k:k + 1],
                                         in1=rs[:, :], op0=ALU.mult, op1=ALU.mult).then_inc(a_ready, 1)
            link(dve.tensor_copy(ang[:, :], posi[:, :]))
            link(dve.tensor_scalar(ang[:, :], ang[:, :], rope_c[:, 0:1], None, ALU.mult))
            for i, quarter in enumerate((0.25, 0.0)):
                link(dve.tensor_scalar(turns[:, :], ang[:, :], 1.0 / TWO_PI, quarter, ALU.mult, ALU.add))
                link(dve.tensor_scalar(turns[:, :], turns[:, :], MAGIC, None, ALU.add))
                link(dve.tensor_scalar(turns[:, :], turns[:, :], -MAGIC, None, ALU.add))
                src = ang[:, :]
                for part in (C1, C2, C3):
                    link(dve.scalar_tensor_tensor(out=red[:, i, :], in0=turns[:, :], scalar=-part, in1=src,
                                                  op0=ALU.mult, op1=ALU.add))
                    src = red[:, i, :]
                link(dve.tensor_scalar(src, src, quarter * TWO_PI, float(np.float32(3.1415925)), ALU.add, ALU.min))
                dve.tensor_scalar(src, src, float(np.float32(-3.1415925)), None, ALU.max).then_inc(angles, 1)
            dve.wait_ge(tables, 2)
            dve.wait_ge(proj, PRE - 1)
            link(dve.tensor_tensor(krT[:, own], bank[:, PRE - 1, :], cosT[:, :], ALU.mult))
            dve.wait_ge(proj, PRE)
            link(dve.tensor_tensor(turns[:, :], bank[:, PRE, :], sinT[:, :], ALU.mult))
            dve.tensor_tensor(krT[:, own], krT[:, own], turns[:, :], ALU.add).then_inc(roped, 1)
            dve.wait_ge(a_ready, KT)
            mean(1)
            for k in range(N_CQ):
                dve.scalar_tensor_tensor(out=cqT[:, k, :], in0=cqT[:, k, :], scalar=c.gcols[:, KT + k:KT + k + 1],
                                         in1=rs[:, :], op0=ALU.mult, op1=ALU.mult).then_inc(normed, 1)
            mean(2)
            dve.scalar_tensor_tensor(out=ckvT[:, own], in0=ckvT[:, own], scalar=c.gcols[:, KT + QT:KT + QT + 1],
                                     in1=rs[:, :], op0=ALU.mult, op1=ALU.mult).then_inc(normed, 1)
            dve.wait_ge(normed, N_CQ + 1)
            dve.wait_ge(roped, 1)


class Events:

    def __init__(self, names):
        self.names = list(names)
        self.n = len(self.names)
        self.place = {name: k + 1 for k, name in enumerate(self.names)}

    def value(self, t, *name):
        return (t + 1) * self.n + self.place[name]

    def before(self, t, back, *name):
        return (t + 1) * self.n + self.place[name] - back


def mixers(c, q, beside):
    nc, bank, ident = c.nc, c.bank, c.ident
    aT, cqT, ckvT, krT, cosT, sinT, oT, acc = c.aT, c.cqT, c.ckvT, c.krT, c.cosT, c.sinT, c.oT, c.acc
    NPE = PE_TAPS[q]
    V_TAPS = TAPS - NPE
    QUADS = q + 1
    SLOTS = NCH - q
    SUB, QB, KEYS = range(SUBS), range(CB), range(QUADS)
    quads = lambda j: range(QUADS)
    width = lambda j: (CB * q + j + 1) * P
    last_of = lambda p, j, back: (p, j - back) if j >= back else ((p - 1) % SUBS, CB + j - back)
    when = lambda t, p, j, back: t if j >= back or p else t - 1

    JOBS = [(p, name, h) for p in SUB for name in ["gate", "val", "q"] + ["qr", "qs"] * (p % 2 == 0) + ["k", "v", "conv"]
            for h in (KEYS if name in "kv" else range(1))]
    BY_DVE = ("val", "qr", "qs", "conv")
    proj_e = Events(JOBS)
    copied_e = Events(j for j in JOBS if j[1] not in BY_DVE)
    taken_e = Events(j for j in JOBS if j[1] in BY_DVE)
    blocks_e = Events((p, j) for p in SUB for j in QB)
    groups_e = Events((p, j, g) for p in SUB for j in QB for g in quads(j))
    subs_e = Events((p,) for p in SUB)
    taps_e = Events((p, k) for p in SUB for k in range(V_TAPS))
    roped_e = Events((p,) for p in SUB if p % 2 == 0)
    assert proj_e.n % 2 == 0 and groups_e.n % 2 == 0
    STEPS = {"gate": 7, "val": 7, "q": 3, "kv": 2 * QUADS, "first": 2 * QUADS, "block": 2 + 2 * QUADS, "rest": 0}

    with ExitStack() as ctx:
        sb, sem = scope(c, ctx, f"q{q}mixers_")
        w_vg = sb("w_vg", [P, 2, 2, D])
        w_head = sb("w_head", [P, 2, QT * P + 2 * P])
        w_rope = sb("w_rope", [P, 2, QT * P])
        hT = sb("hT", [P, 2, PAD + C])
        w_tap = sb("w_tap", [P, 2, TAPS + 1])
        tap_diag = sb("tap_diag", [P, NPE, P])
        sig = sb("sig", [P, C])
        qT = sb("qT", [P, 2, C])
        kT = sb("kT", [P, 2, QUADS * C])
        V = sb("V", [P, 2, QUADS * C])
        qrT = sb("qrT", [P, C])
        swapped = sb("swapped", [P, C])
        prob = sb("prob", [P, SLOTS, QUADS * C])
        probT = sb("probT", [P, 2, C])
        peak = sb("peak", [P, 2])
        low = sb("low", [P, 2])
        total = sb("total", [P, 2])
        inv = sb("inv", [P, 2])
        inv_diag = sb("inv_diag", [P, 2, P])

        w_vg_in = [[sem(f"w_vg_in{p}{i}") for i in range(2)] for p in range(2)]
        w_head_in = [sem(f"w_head_in{p}") for p in range(2)]
        w_rope_in = sem("w_rope_in")
        proj = sem("proj")
        copied = sem("copied")
        taken = sem("taken")
        roped = sem("roped")
        padded = sem("padded")
        tap_cols = sem("tap_cols")
        tap_mats = sem("tap_mats")
        scored = sem("scored")
        maxed = sem("maxed")
        peaked = sem("peaked")
        exped = sem("exped")
        inverted = sem("inverted")
        inv_ready = sem("inv_ready")
        turned = sem("turned")
        turned_out = sem("turned_out")
        used = sem("used")
        oT_out = sem("oT_out")
        tapped = sem("tapped")
        block = ctx.enter_context(nc.Block())
        tile = lambda t, p: bass.ds((SUBS * t + p) * C, C)
        score_banks = lambda j: bank[:, 2 + j % SLOTS:2 + j % SLOTS + QUADS, :].rearrange("p a n -> p (a n)")

        @block.sync
        def _(sp):
            with sp.Fori(0, HEADS // SUBS) as t:
                for p in SUB:
                    old = (p - 2) % SUBS
                    ago = t if p >= 2 else t - 1
                    for i, name in enumerate(("gate", "val")):
                        sp.wait_ge(proj, proj_e.value(ago, old, name, 0))
                        sp.dma_start(w_vg[:, p % 2, i, :], item(c.dram["w_vg"][bass.ds(2 * SUBS * t + 2 * p + i, 1)])
                                     ).then_inc(w_vg_in[p % 2][i], 16)
                    sp.wait_ge(proj, proj_e.value(ago, old, "v", q))
                    sp.dma_start(w_head[:, p % 2, :], item(c.dram["w_head"][bass.ds(SUBS * t + p, 1)])
                                 ).then_inc(w_head_in[p % 2], 16)
                    if p % 2 == 0:
                        sp.wait_ge(proj, proj_e.value(ago, old, "qs", 0))
                        sp.dma_start(w_rope[:, :, :].rearrange("p a n -> p (a n)"),
                                     item(c.dram["w_rope"][bass.ds(SUBS // 2 * t + p // 2, 1)])).then_inc(w_rope_in, 16)

        filled = lambda t, p: 16 * (SUBS // 2 * t + p // 2 + 1)

        @block.gpsimd
        def _(pool):
            pool.sem_inc(tap_cols, subs_e.n)
            pool.sem_inc(tap_mats, subs_e.n)
            with pool.Fori(0, HEADS // SUBS) as t:
                side = beside("pool", pool, t)
                for p in SUB:
                    pool.wait_ge(tapped, taps_e.value(t if p >= 2 else t - 1, (p - 2) % SUBS, V_TAPS - 1))
                    pool.sem_inc(c.passed, 1)
                    pool.tensor_copy(w_tap[:, p % 2, :], c.wdw[:, bass.ds((SUBS * t + p) * (TAPS + 1), TAPS + 1)]
                                     ).then_inc(tap_cols, 1)
                    pool.wait_ge(tap_cols, subs_e.value(t, p))
                    pool.wait_ge(proj, proj_e.value(t if p else t - 1, (p - 1) % SUBS, "conv", 0))
                    pool.sem_inc(c.passed, 1)
                    for k in range(NPE):
                        ins = pool.tensor_scalar(tap_diag[:, k, :], ident[:, :], w_tap[:, p % 2, k:k + 1], None, ALU.mult)
                    ins.then_inc(tap_mats, 1)
                    for name, w in STEPS.items():
                        for _ in range(CB if name == "block" else 1):
                            side.step(w)
                side.finish()

        @block.tensor
        def _(pe):
            for s_, e in ((proj, proj_e), (scored, blocks_e), (turned, groups_e), (used, groups_e)):
                pe.sem_inc(s_, e.n)
            with pe.Fori(0, HEADS // SUBS) as t:
                side = beside("tensor", pe, t)

                def job(p, name, h, products):
                    n = proj_e.place[p, name, h] - 1
                    last = JOBS[n - 2]
                    ev, s_ = (taken_e, taken) if last[1] in BY_DVE else (copied_e, copied)
                    pe.wait_ge(s_, ev.value(t if n >= 2 else t - 1, *last))
                    for lhs, rhs, lo, w, a, b in products:
                        mm = pe.matmul(bank[:, n % 2, lo:lo + w], lhs, rhs, start=a, stop=b)
                    mm.then_inc(proj, 1)

                def full(w, x, k_tiles):
                    return [(w(k), x(k), 0, C, k == 0, k == k_tiles - 1) for k in range(k_tiles)]

                def scores(p, j):
                    h64 = slice(64 * (p % 2), 64 * (p % 2) + 64)
                    if j == 0:
                        pe.wait_ge(copied, copied_e.value(t, p, "k", q))
                        if p % 2 == 0:
                            pe.wait_ge(roped, roped_e.value(t, p))
                    pe.wait_ge(exped, blocks_e.before(t, SLOTS, p, j))
                    qs = slice(j * P, (j + 1) * P)
                    for h in KEYS:
                        w = min(width(j) - h * C, C)
                        ks = slice(h * C, h * C + w)
                        out = bank[:, 2 + j % SLOTS + h, :]
                        diag = h == q
                        pe.matmul(out[:, 0:w], qT[:, p % 2, qs], kT[:, p % 2, ks], start=True, stop=False)
                        mm = pe.matmul(out[:, 0:w], qrT[h64, qs], krT[h64, ks], start=False, stop=not diag)
                        if diag:
                            mm = pe.matmul(out[:, w - P:w], ident[:, :], c.mask[:, :], start=False, stop=True)
                    mm.then_inc(scored, 1)

                def turn(p, j, g):
                    if g == 0:
                        pe.wait_ge(inv_ready, blocks_e.value(t, p, j))
                    pe.wait_ge(turned_out, groups_e.before(t, 1, p, j, g))
                    for b in range(min(CB * q + j + 1 - 4 * g, 4)):
                        kb = 4 * g + b
                        mm = pe.matmul(bank[:, 4, b * P:(b + 1) * P], prob[:, j % SLOTS, kb * P:(kb + 1) * P],
                                       inv_diag[:, j % 2, :], start=True, stop=True)
                    mm.then_inc(turned, 1)

                def attend(p, j, g):
                    if j == 0 and g == 0:
                        pe.wait_ge(copied, copied_e.value(t, p, "v", q))
                        pe.wait_ge(oT_out, subs_e.before(t, 1, p))
                    pe.wait_ge(turned_out, groups_e.value(t, p, j, g))
                    n = groups_e.place[p, j, g] - 1
                    own = CB * q + j
                    for kb in range(4 * g, min(own + 1, 4 * g + 4)):
                        mm = pe.matmul(bank[:, 5, j * P:(j + 1) * P], V[:, p % 2, kb * P:(kb + 1) * P],
                                       probT[:, n % 2, (kb % 4) * P:(kb % 4 + 1) * P], start=(kb == 0), stop=(kb == own))
                    mm.then_inc(used, 1)

                for p in SUB:
                    for i, name in enumerate(("gate", "val")):
                        pe.wait_ge(w_vg_in[p % 2][i], filled(t, p))
                        job(p, name, 0, full(lambda k: w_vg[:, p % 2, i, k * P:(k + 1) * P], lambda k: aT[:, k, :], KT))
                        side.step(STEPS[name])
                    pe.wait_ge(w_head_in[p % 2], filled(t, p))
                    job(p, "q", 0, full(lambda k: w_head[:, p % 2, k * P:(k + 1) * P], lambda k: cqT[:, k, :], QT))
                    if p % 2 == 0:
                        pe.wait_ge(w_rope_in, 16 * (SUBS // 2 * t + p // 2 + 1))
                        for i, name in enumerate(("qr", "qs")):
                            job(p, name, 0, full(lambda k: w_rope[:, i, k * P:(k + 1) * P], lambda k: cqT[:, k, :], QT))
                    side.step(STEPS["q"])
                    for h in KEYS:
                        job(p, "k", h, full(lambda k: w_head[:, p % 2, QT * P:(QT + 1) * P],
                                            lambda k: ckvT[:, h * C:(h + 1) * C], 1))
                    for h in KEYS:
                        job(p, "v", h, [(ckvT[:, (4 * h + b) * P:(4 * h + b + 1) * P], w_head[:, p % 2, (QT + 1) * P:],
                                         b * P, P, True, True) for b in range(4)])
                    side.step(STEPS["kv"])
                    for j in range(SLOTS):
                        scores(p, j)
                    side.step(STEPS["first"])
                    for j in QB:
                        turn(p, j, 0)
                        if j + SLOTS < CB and SLOTS > 1:
                            scores(p, j + SLOTS)
                        for g in quads(j)[1:]:
                            turn(p, j, g)
                        if j + SLOTS < CB and SLOTS == 1:
                            scores(p, j + SLOTS)
                        for g in quads(j):
                            attend(p, j, g)
                        if j == 0:
                            pe.wait_ge(padded, subs_e.value(t, p))
                            pe.wait_ge(taken, taken_e.value(t, p, "val", 0))
                            pe.wait_ge(tap_mats, subs_e.value(t, p))
                            job(p, "conv", 0, [(tap_diag[:, k, :], hT[:, p % 2, k:k + C], 0, C, k == 0, k == NPE - 1)
                                               for k in range(NPE)])
                        side.step(STEPS["block"])
                    side.step(STEPS["rest"])
                side.finish()

        @block.scalar
        def _(act):
            for s_, e in ((copied, copied_e), (exped, blocks_e), (turned_out, groups_e), (oT_out, subs_e)):
                act.sem_inc(s_, e.n)
            with act.Fori(0, HEADS // SUBS) as t:
                side = beside("scalar", act, t)

                def take(p, name, h=0):
                    n = proj_e.place[p, name, h] - 1
                    act.wait_ge(proj, proj_e.value(t, p, name, h))
                    if name == "gate":
                        act.wait_ge(taken, taken_e.value(t if p else t - 1, (p - 1) % SUBS, "val", 0))
                        dst, func = sig[:, :], ACT.Sigmoid
                    else:
                        dst, func = {"q": qT, "k": kT, "v": V}[name][:, p % 2, h * C:(h + 1) * C], ACT.Copy
                    act.activation(dst, bank[:, n % 2, :], func).then_inc(copied, 1)

                def exps(p, j):
                    act.wait_ge(peaked, blocks_e.value(t, p, j))
                    act.wait_ge(turned, groups_e.value(when(t, p, j, SLOTS), *last_of(p, j, SLOTS), q))
                    act.activation(prob[:, j % SLOTS, 0:width(j)], score_banks(j)[:, 0:width(j)], ACT.Exp,
                                   bias=low[:, j % 2:j % 2 + 1], scale=SCALE,
                                   accum_out=total[:, j % 2:j % 2 + 1]).then_inc(exped, 1)

                def turned_copy(p, j, g):
                    n = groups_e.place[p, j, g] - 1
                    w = min(width(j) - 4 * g * P, C)
                    act.wait_ge(turned, groups_e.value(t, p, j, g))
                    act.wait_ge(used, groups_e.before(t, 2, p, j, g))
                    act.activation(probT[:, n % 2, 0:w], bank[:, 4, 0:w], ACT.Copy).then_inc(turned_out, 1)

                for p in SUB:
                    take(p, "gate")
                    side.step(STEPS["gate"])
                    side.step(STEPS["val"])
                    take(p, "q")
                    side.step(STEPS["q"])
                    for name in "kv":
                        for h in KEYS:
                            take(p, name, h)
                    side.step(STEPS["kv"])
                    for j in range(SLOTS):
                        exps(p, j)
                    side.step(STEPS["first"])
                    for j in QB:
                        for g in quads(j):
                            turned_copy(p, j, g)
                        if j + SLOTS < CB:
                            exps(p, j + SLOTS)
                        if j == CB - 1:
                            act.wait_ge(used, groups_e.value(t, p, j, q))
                            act.activation(oT[:, tile(t, p)], bank[:, 5, :], ACT.Copy).then_inc(oT_out, 1)
                        side.step(STEPS["block"])
                    side.step(STEPS["rest"])
                side.finish()

        @block.vector
        def _(dve):
            for s_, e in ((taken, taken_e), (peaked, blocks_e), (inv_ready, blocks_e), (maxed, blocks_e),
                          (inverted, blocks_e), (tapped, taps_e), (roped, roped_e), (padded, subs_e)):
                dve.sem_inc(s_, e.n)
            with dve.Fori(0, HEADS // SUBS) as t:
                side = beside("vector", dve, t)

                def low_of(p, j):
                    one = slice(j % 2, j % 2 + 1)
                    dve.wait_ge(scored, blocks_e.value(t, p, j))
                    dve.wait_ge(peaked, blocks_e.before(t, 2, p, j))
                    dve.tensor_reduce(peak[:, one], score_banks(j)[:, 0:width(j)], AX.X, ALU.max).then_inc(maxed, 1)
                    dve.wait_ge(maxed, blocks_e.value(t, p, j))
                    dve.wait_ge(exped, blocks_e.before(t, 2, p, j))
                    dve.tensor_scalar(low[:, one], peak[:, one], -SCALE, None, ALU.mult).then_inc(peaked, 1)

                def inv_of(p, j):
                    one = slice(j % 2, j % 2 + 1)
                    dve.wait_ge(exped, blocks_e.value(t, p, j))
                    dve.reciprocal(inv[:, one], total[:, one]).then_inc(inverted, 1)
                    dve.wait_ge(inverted, blocks_e.value(t, p, j))
                    dve.wait_ge(turned, groups_e.value(when(t, p, j, 2), *last_of(p, j, 2), q))
                    dve.tensor_scalar(inv_diag[:, j % 2, :], ident[:, :], inv[:, one], None, ALU.mult).then_inc(inv_ready, 1)

                def conv_start(p):
                    n = proj_e.place[p, "conv", 0] - 1
                    dve.wait_ge(proj, proj_e.value(t, p, "conv", 0))
                    dve.wait_ge(tap_cols, subs_e.value(t, p))
                    dve.tensor_scalar(acc[:, tile(t, p)], bank[:, n % 2, :], w_tap[:, p % 2, TAPS:TAPS + 1], None,
                                      ALU.add).then_inc(taken, 1)

                def taps(p, first, n):
                    for k in range(first, min(first + n, V_TAPS)):
                        if k == 0:
                            dve.wait_ge(taken, taken_e.value(t, p, "conv", 0))
                        else:
                            dve.wait_ge(tapped, taps_e.value(t, p, k - 1))
                        dve.scalar_tensor_tensor(out=acc[:, tile(t, p)], in0=hT[:, p % 2, NPE + k:NPE + k + C],
                                                 scalar=w_tap[:, p % 2, NPE + k:NPE + k + 1], in1=acc[:, tile(t, p)],
                                                 op0=ALU.mult, op1=ALU.add).then_inc(tapped, 1)
                    return min(first + n, V_TAPS)

                for p in SUB:
                    dve.wait_ge(tapped, taps_e.value(t if p >= 2 else t - 1, (p - 2) % SUBS, V_TAPS - 1))
                    tail = c.tails[:, bass.ds((SUBS * t + p) * PAD, PAD)]
                    if q == 0:
                        dve.memset(hT[:, p % 2, 0:PAD], 0.0).then_inc(padded, 1)
                    else:
                        dve.tensor_copy(hT[:, p % 2, 0:PAD], tail).then_inc(padded, 1)
                    side.step(STEPS["gate"])
                    n = proj_e.place[p, "val", 0] - 1
                    dve.wait_ge(copied, copied_e.value(t, p, "gate", 0))
                    dve.wait_ge(proj, proj_e.value(t, p, "val", 0))
                    dve.tensor_tensor(hT[:, p % 2, PAD:], bank[:, n % 2, :], sig[:, :], ALU.mult).then_inc(taken, 1)
                    dve.wait_ge(taken, taken_e.value(t, p, "val", 0))
                    dve.wait_ge(padded, subs_e.value(t, p))
                    if q == 0:
                        dve.tensor_copy(tail, hT[:, p % 2, C:C + PAD])
                    side.step(STEPS["val"])
                    if p % 2 == 0:
                        for name, dst, table in (("qr", qrT, cosT), ("qs", swapped, sinT)):
                            n = proj_e.place[p, name, 0] - 1
                            dve.wait_ge(proj, proj_e.value(t, p, name, 0))
                            dve.tensor_tensor(dst[:, :], bank[:, n % 2, :], table[:, :], ALU.mult).then_inc(taken, 1)
                        dve.wait_ge(taken, taken_e.value(t, p, "qs", 0))
                        dve.tensor_tensor(qrT[:, :], qrT[:, :], swapped[:, :], ALU.add).then_inc(roped, 1)
                    side.step(STEPS["q"])
                    side.step(STEPS["kv"])
                    for j in range(SLOTS):
                        low_of(p, j)
                    side.step(STEPS["first"])
                    k = 0
                    for j in QB:
                        inv_of(p, j)
                        if j == 1:
                            conv_start(p)
                        if j >= 1:
                            k = taps(p, k, 2)
                        if j + SLOTS < CB:
                            low_of(p, j + SLOTS)
                        if j >= 1:
                            k = taps(p, k, 2)
                        side.step(STEPS["block"])
                    taps(p, k, V_TAPS)
                    side.step(STEPS["rest"])
                side.finish()


def mix(c, q, beside):
    nc, bank, ident, ones = c.nc, c.bank, c.ident, c.ones
    aT, oT, acc = c.aT, c.oT, c.acc
    x4 = acc[:, :].rearrange("p (b d) -> p b d", b=CB)
    h1 = oT[:, :].rearrange("p (b d) -> p b d", b=CB)
    WR, SG, BANKS = 3, 4, 5
    LEAD = 3
    JOBS = [("mean", 0)]
    for d in range(KT):
        JOBS += [("ga", d), ("ya", d)]
    JOBS += [("gc", d) for d in range(LEAD)]
    for d in range(KT):
        JOBS += [("yc", d)] + [("gc", d + LEAD)] * (d + LEAD < KT)
    JOBS += [("o", d) for d in range(KT)]
    TILES = JOBS[1:]
    GATES = [j for j in JOBS if j[0] in ("ga", "gc")]
    assert len(TILES) == 5 * KT
    N = {j: n for n, j in enumerate(JOBS)}
    BY_ACT = [j for j in JOBS if j[0] in ("ga", "gc")]
    BY_DVE = [j for j in JOBS if j[0] not in ("ga", "gc")]

    with ExitStack() as ctx:
        sb, sem = scope(c, ctx, f"q{q}mix_")
        mixT = sb("mixT", [P, KT, C])
        w = sb("w", [P, WR, D])
        sig = sb("sig", [P, SG, C])
        sq = sb("sq", [P, 2, C])
        mu = sb("mu", [P, C])
        part = sb("part", [P, C])
        g_ffn = sb("g_ffn", [P, D])
        ss = sb("ss", [P, CB])
        rstd = sb("rstd", [P, CB])
        g_in = sem("g_in")
        x_in = sem("x_in")
        w_in = [sem(f"w_in{r}") for r in range(WR)]
        proj = sem("proj")
        gated = sem("gated")
        taken = sem("taken")
        centred = sem("centred")
        squared = sem("squared")
        summed = sem("summed")
        var_ready = sem("var_ready")
        root_ready = sem("root_ready")
        inv_ready = sem("inv_ready")
        scaled = sem("scaled")
        silued = sem("silued")
        parted = sem("parted")
        mixed = sem("mixed")
        energy = sem("energy")
        normed = sem("normed")
        chain = sem("chain")
        turned = sem("turned")
        turned_out = sem("turned_out")
        stored = sem("stored")
        block = ctx.enter_context(nc.Block())

        def bank_free(pe, n):
            if n >= BANKS:
                j = JOBS[n - BANKS]
                if j in BY_ACT:
                    pe.wait_ge(gated, BY_ACT.index(j) + 1)
                else:
                    pe.wait_ge(taken, BY_DVE.index(j) + 1)

        def steps(front, side):
            front("mean", 0); side.step(7)
            for d in range(KT):
                front("a", d); side.step(15)
            front("lead", 0); side.step(7 * LEAD)
            for d in range(KT):
                front("c", d); side.step(14 if d + LEAD < KT else 7)
            for d in range(KT):
                front("o", d); side.step(7)
            front("norm", 0); side.step(2)
            for b in range(CB):
                front("turn", b); side.step(1)
            side.finish()

        @block.sync
        def _(sp):
            sp.dma_start(g_ffn[:, :], c.dram["g_ffn"].broadcast_to([P, D])).then_inc(g_in, 16)
            for i, j in enumerate(TILES):
                if i >= WR:
                    sp.wait_ge(proj, i - WR + 2)
                if j == ("o", 1):
                    sp.wait_ge(proj, N["yc", KT - 1] + 1)
                    sp.dma_start(x4, c.dram["x"][q * C:(q + 1) * C, :].rearrange("(b p) d -> p b d", p=P)
                                 ).then_inc(x_in, 16)
                sp.dma_start(w[:, i % WR, :], c.dram["w_mix"][i]).then_inc(w_in[i % WR], 16)
            for b in range(CB):
                rows = slice((q * CB + b) * P, (q * CB + b + 1) * P)
                sp.wait_ge(taken, len(BY_DVE))
                sp.dma_start(c.h1_dram[rows, :], h1[:, b, :]).then_inc(stored, 16)
                sp.wait_ge(normed, b + 1)
                sp.dma_start(c.xn_dram[rows, :], x4[:, b, :]).then_inc(stored, 16)
            sp.wait_ge(stored, 2 * CB * 16)

        @block.gpsimd
        def _(pool):
            steps(lambda *_: None, beside("pool", pool, None))

        @block.tensor
        def _(pe):
            def job(j, products):
                n = N[j]
                bank_free(pe, n)
                if n:
                    pe.wait_ge(w_in[(n - 1) % WR], 16 * ((n - 1) // WR + 1))
                for lhs, rhs, lo, wd, a, b in products:
                    mm = pe.matmul(bank[:, n % BANKS, lo:lo + wd], lhs, rhs, start=a, stop=b)
                mm.then_inc(proj, 1)

            def wt(j, k):
                return w[:, (N[j] - 1) % WR, k * P:(k + 1) * P]

            def full(j, x):
                job(j, [(wt(j, k), x(k), 0, C, k == 0, k == KT - 1) for k in range(KT)])

            tile = lambda a: lambda k: a[:, k * C:(k + 1) * C]

            def front(what, d):
                if what == "mean":
                    job(("mean", 0), [(ones[:, :], tile(acc)(k), 0, C, k == 0, k == KT - 1) for k in range(KT)])
                if what == "a":
                    full(("ga", d), lambda k: aT[:, k, :])
                    full(("ya", d), tile(oT))
                    pe.wait_ge(squared, d + 1)
                    pe.matmul(bank[:, 5, :], ones[:, :], sq[:, d % 2, :], start=(d == 0), stop=(d == KT - 1)).then_inc(summed, 1)
                if what == "lead":
                    for i in range(LEAD):
                        full(("gc", i), lambda k: aT[:, k, :])
                if what == "c":
                    if d == 0:
                        pe.wait_ge(silued, KT)
                    full(("yc", d), tile(acc))
                    if d + LEAD < KT:
                        full(("gc", d + LEAD), lambda k: aT[:, k, :])
                if what == "o":
                    if d == 0:
                        pe.wait_ge(mixed, KT)
                    job(("o", d), [(mixT[:, k, b * P:(b + 1) * P], wt(("o", d), k), b * P, P, k == 0, k == KT - 1)
                                   for b in range(CB) for k in range(KT)])
                if what == "turn":
                    pe.wait_ge(normed, d + 1)
                    for u in range(2):
                        n = 2 * d + u
                        if n < 2:
                            pe.wait_ge(taken, len(BY_DVE))
                        else:
                            pe.wait_ge(turned_out, n - 1)
                        for k in range(4):
                            mm = pe.transpose(bank[:, n % 2, k * P:(k + 1) * P],
                                              x4[:, d, (4 * u + k) * P:(4 * u + k + 1) * P], ident[:, :])
                        mm.then_inc(turned, 1)

            steps(front, beside("tensor", pe, None))

        @block.scalar
        def _(act):
            def gate(j, g0):
                i = GATES.index(j)
                if i >= SG:
                    old = GATES[i - SG]
                    act.wait_ge(taken, BY_DVE.index(("y" + old[0][1], old[1])) + 1)
                act.wait_ge(proj, N[j] + 1)
                act.activation(sig[:, i % SG, :], bank[:, N[j] % BANKS, :], ACT.Sigmoid,
                               bias=c.gcols[:, g0 + j[1]:g0 + j[1] + 1]).then_inc(gated, 1)

            def front(what, d):
                if what == "a":
                    gate(("ga", d), G_BGATE + KT)
                    act.wait_ge(centred, d + 1)
                    if d >= 2:
                        act.wait_ge(summed, d - 1)
                    act.activation(sq[:, d % 2, :], acc[:, d * C:(d + 1) * C], ACT.Square).then_inc(squared, 1)
                if what == "lead":
                    act.wait_ge(var_ready, 1)
                    act.activation(mu[:, :], mu[:, :], ACT.Sqrt).then_inc(root_ready, 1)
                    for k in range(KT):
                        t = acc[:, k * C:(k + 1) * C]
                        act.wait_ge(scaled, k + 1)
                        act.activation(t, t, ACT.Silu, bias=c.gcols[:, G_LNB + k:G_LNB + k + 1],
                                       scale=c.gcols[:, G_LNG + k:G_LNG + k + 1]).then_inc(silued, 1)
                    for i in range(LEAD):
                        gate(("gc", i), G_BGATE)
                if what == "c" and d + LEAD < KT:
                    gate(("gc", d + LEAD), G_BGATE)
                if what == "norm":
                    for b in range(CB):
                        act.wait_ge(taken, len(BY_DVE))
                        if b:
                            act.wait_ge(energy, b)
                        act.activation(sig[:, 0:2, :].rearrange("p a n -> p (a n)"), h1[:, b, :], ACT.Square,
                                       accum_out=ss[:, b:b + 1]).then_inc(energy, 1)
                    act.wait_ge(var_ready, 2)
                    act.activation(ss[:, :], ss[:, :], ACT.Sqrt).then_inc(root_ready, 1)
                if what == "turn":
                    for u in range(2):
                        n = 2 * d + u
                        act.wait_ge(turned, n + 1)
                        act.activation(aT[:, 4 * u:4 * u + 4, d * P:(d + 1) * P],
                                       bank[:, n % 2, :].rearrange("p (k n) -> p k n", k=4), ACT.Copy).then_inc(turned_out, 1)

            steps(front, beside("scalar", act, None))

        @block.vector
        def _(dve):
            count = [0]

            def link(ins):
                count[0] += 1
                ins.then_inc(chain, 1)
                dve.wait_ge(chain, count[0])

            def out_of(j):
                dve.wait_ge(proj, N[j] + 1)
                return bank[:, N[j] % BANKS, :]

            def gated_y(dst, j):
                g = ("g" + j[0][1], j[1])
                dve.wait_ge(gated, BY_ACT.index(g) + 1)
                return dve.tensor_tensor(dst, out_of(j), sig[:, GATES.index(g) % SG, :], ALU.mult).then_inc(taken, 1)

            def front(what, d):
                if what == "mean":
                    dve.tensor_scalar(mu[:, :], out_of(("mean", 0)), 1.0 / D, None, ALU.mult).then_inc(taken, 1)
                    dve.wait_ge(taken, 1)
                if what == "a":
                    t = acc[:, d * C:(d + 1) * C]
                    dve.tensor_tensor(t, t, mu[:, :], ALU.subtract).then_inc(centred, 1)
                    gated_y(mixT[:, d, :], ("ya", d))
                if what == "lead":
                    dve.wait_ge(summed, KT)
                    dve.wait_ge(centred, KT)
                    dve.tensor_scalar(mu[:, :], bank[:, 5, :], 1.0 / D, EPS, ALU.mult, ALU.add).then_inc(var_ready, 1)
                    dve.wait_ge(root_ready, 1)
                    link(dve.reciprocal(mu[:, :], mu[:, :]))
                    for k in range(KT):
                        t = acc[:, k * C:(k + 1) * C]
                        dve.tensor_tensor(t, t, mu[:, :], ALU.mult).then_inc(scaled, 1)
                if what == "c":
                    if d:
                        dve.wait_ge(mixed, d)
                    gated_y(part[:, :], ("yc", d))
                    dve.wait_ge(taken, BY_DVE.index(("yc", d)) + 1)
                    dve.tensor_tensor(mixT[:, d, :], mixT[:, d, :], part[:, :], ALU.add).then_inc(mixed, 1)
                if what == "o":
                    if d == 0:
                        dve.wait_ge(x_in, 16)
                    cols = slice(d * P, (d + 1) * P)
                    dve.tensor_tensor(h1[:, :, cols], out_of(("o", d)).rearrange("p (b n) -> p b n", b=CB),
                                      x4[:, :, cols], ALU.add).then_inc(taken, 1)
                if what == "norm":
                    dve.wait_ge(energy, CB)
                    dve.tensor_scalar(ss[:, :], ss[:, :], 1.0 / D, EPS, ALU.mult, ALU.add).then_inc(var_ready, 1)
                    dve.wait_ge(root_ready, 2)
                    link(dve.reciprocal(rstd[:, :], ss[:, :]))
                    dve.wait_ge(taken, len(BY_DVE))
                    dve.wait_ge(g_in, 16)
                    for b in range(CB):
                        dve.scalar_tensor_tensor(out=x4[:, b, :], in0=h1[:, b, :], scalar=rstd[:, b:b + 1],
                                                 in1=g_ffn[:, :], op0=ALU.mult, op1=ALU.mult).then_inc(normed, 1)

            steps(front, beside("vector", dve, None))


def peer_scores(c, q, beside):
    nc, bank, xnT = c.nc, c.bank, c.aT
    HS = 2 * PH
    WR = 4
    with ExitStack() as ctx:
        sb, sem = scope(c, ctx, f"q{q}scores_")
        w = sb("w", [P, WR, D])
        keysT = sb("keysT", [P, HS * NK])
        queryT = sb("queryT", [P, 2, C])
        out = sb("out", [P, 2, C])
        k_in = sem("k_in")
        w_in = [sem(f"w_in{r}") for r in range(WR)]
        proj = sem("proj")
        copied = sem("copied")
        scored = sem("scored")
        out_ready = sem("out_ready")
        stored = [sem(f"stored{r}") for r in range(2)]
        block = ctx.enter_context(nc.Block())

        def steps(front, side):
            for i in range(HS + 1):
                front(i)
                side.step(1)
            side.finish()

        def store(sp, i):
            sp.wait_ge(out_ready, i + 1)
            dst = c.sc_dram[q * C:(q + 1) * C, i * NK:(i + 1) * NK].rearrange("(b p) n -> p b n", p=P)
            sp.dma_start(dst, out[:, i % 2, :].rearrange("p (b n) -> p b n", b=CB)).then_inc(stored[i % 2], 16)

        @block.sync
        def _(sp):
            for i in range(HS):
                if i >= WR:
                    sp.wait_ge(proj, i - WR + 1)
                sp.dma_start(w[:, i % WR, :], c.dram["w_peer"][i]).then_inc(w_in[i % WR], 16)
                if i == 0:
                    sp.dma_start(keysT[:, :], c.dram["keysT"]).then_inc(k_in, 16)
                if i >= 2:
                    store(sp, i - 2)
            store(sp, HS - 2)
            store(sp, HS - 1)
            for r in range(2):
                sp.wait_ge(stored[r], 16 * (HS // 2))

        @block.gpsimd
        def _(pool):
            steps(lambda i: None, beside("pool", pool, None))

        @block.tensor
        def _(pe):
            def front(i):
                if i < HS:
                    pe.wait_ge(w_in[i % WR], 16 * (i // WR + 1))
                    if i >= 2:
                        pe.wait_ge(copied, i - 1)
                    for k in range(KT):
                        mm = pe.matmul(bank[:, i % 2, :], w[:, i % WR, k * P:(k + 1) * P], xnT[:, k, :],
                                       start=(k == 0), stop=(k == KT - 1))
                    mm.then_inc(proj, 1)
                if i:
                    i -= 1
                    if i == 0:
                        pe.wait_ge(k_in, 16)
                    pe.wait_ge(copied, i + 1)
                    if i >= 2:
                        pe.wait_ge(out_ready, i - 1)
                    for b in range(CB):
                        mm = pe.matmul(bank[:, 2 + i % 2, b * P:(b + 1) * P], queryT[:, i % 2, b * P:(b + 1) * P],
                                       keysT[:, i * NK:(i + 1) * NK], start=True, stop=True)
                    mm.then_inc(scored, 1)

            steps(front, beside("tensor", pe, None))

        @block.scalar
        def _(act):
            def front(i):
                if i < HS:
                    act.wait_ge(proj, i + 1)
                    if i >= 2:
                        act.wait_ge(scored, i - 1)
                    act.activation(queryT[:, i % 2, :], bank[:, i % 2, :], ACT.Copy).then_inc(copied, 1)
                if i:
                    i -= 1
                    act.wait_ge(scored, i + 1)
                    if i >= 2:
                        act.wait_ge(stored[i % 2], 16 * (i // 2))
                    act.activation(out[:, i % 2, :], bank[:, 2 + i % 2, :], ACT.Copy).then_inc(out_ready, 1)

            steps(front, beside("scalar", act, None))

        @block.vector
        def _(dve):
            steps(lambda i: None, beside("vector", dve, None))


class Peer:

    ROUTE_HEAD = 24
    ROUTE = PH * ROUTE_HEAD + 4
    DIAGS = 4

    def __init__(self, c, ctx):
        sb, sem = scope(c, ctx, "peer_")
        self.c = c
        self.ring = sb("ring", [P, RING, 2 * D])
        self.xn = sb("xn", [P, D])
        self.h1 = sb("h1", [P, D])
        self.y = sb("y", [P, D])
        self.g_final = sb("g_final", [P, D])
        self.sc = sb("sc", [P, 2 * PH * NK])
        self.diag = sb("diag", [P, self.DIAGS, P])
        self.dots = sb("dots", [P, PICKS])
        self.gelus = sb("gelus", [P, PICKS])
        self.gates = sb("gates", [P, PICKS])
        self.index = sb("index", [P, PICKS], I32)
        self.next_index = sb("next_index", [P, PICKS], I32)
        self.next_gates = sb("next_gates", [P, PICKS])
        self.best = sb("best", [P, PICKS])
        self.norm = sb("norm", [P, PH])
        self.top = sb("top", [P, 2, TOPK])
        self.top_at = sb("top_at", [P, 2, TOPK], U32)
        self.top_atf = sb("top_atf", [P, 2, TOPK])
        self.rest = sb("rest", [P, 2, NK])
        self.cand = sb("cand", [P, TOPK * TOPK])
        self.cand_rest = sb("cand_rest", [P, TOPK * TOPK])
        self.place = sb("place", [P, TOPK], U32)
        self.digits = sb("digits", [P, 2, TOPK], U32)
        self.digitsf = sb("digitsf", [P, 2, TOPK])
        self.hit = sb("hit", [P, 2 * TOPK * TOPK])
        self.side_at = sb("side_at", [P, 2 * TOPK])
        self.iota = sb("iota", [P, TOPK])
        self.ms = sb("ms", [P, 1])
        self.root = sb("root", [P, 1])
        self.got = [sem(f"got{r}") for r in range(RING)]
        self.xn_in, self.h1_in, self.sc_in, self.y_out = (sem(n) for n in ("xn_in", "h1_in", "sc_in", "y_out"))
        self.dotted = sem("dotted")
        self.gelued = sem("gelued")
        self.diag_ready = sem("diag_ready")
        self.added = sem("added")
        self.gates_set = sem("gates_set")
        self.index_set = sem("index_set")
        self.routed = sem("routed")
        self.exp_done = sem("exp_done")
        self.summed = sem("summed")
        self.ms_ready = sem("ms_ready")
        self.root_ready = sem("root_ready")
        self.inv_ready = sem("inv_ready")
        self.y_ready = sem("y_ready")
        self.carried = sem("carried")
        self.ready = sem("ready")
        self.ready_dma = sem("ready_dma")

    BEFORE = {"tensor": [("added", PICKS)], "scalar": [("gelued", PICKS), ("exp_done", 1), ("root_ready", 1)],
              "vector": [("dotted", PICKS), ("diag_ready", PICKS), ("gates_set", 1), ("routed", ROUTE), ("summed", 2),
                         ("ms_ready", 2), ("inv_ready", 1), ("y_ready", 1)],
              "pool": [("index_set", PH)]}

    def before(self, name, eng):
        for s_, n in self.BEFORE[name]:
            eng.sem_inc({"added": self.added, "gelued": self.gelued, "exp_done": self.exp_done,
                         "root_ready": self.root_ready, "dotted": self.dotted, "diag_ready": self.diag_ready,
                         "gates_set": self.gates_set, "routed": self.routed, "summed": self.summed,
                         "ms_ready": self.ms_ready, "inv_ready": self.inv_ready, "y_ready": self.y_ready,
                         "index_set": self.index_set}[s_], n)

    def route(self, dve, b):
        base, n = self.ROUTE * (b + 1), [0]

        def step(ins):
            n[0] += 1
            ins.then_inc(self.routed, 1)

        def after(k=None):
            dve.wait_ge(self.routed, base + (n[0] if k is None else k))

        def carry():
            after()
            dve.sem_inc(self.carried, 1)

        dve.wait_ge(self.sc_in, 16 * (b + 1))
        for h in range(PH):
            side = [self.sc[:, (2 * h + i) * NK:(2 * h + i + 1) * NK] for i in range(2)]
            for lo in (0, TOPK // 2):
                of = side if lo == 0 else [self.rest[:, i, :] for i in range(2)]
                some = slice(lo, lo + TOPK // 2)
                for i in range(2):
                    carry()
                    step(dve.max(self.top[:, i, some], of[i])); yield
                for i in range(2):
                    carry()
                    step(dve.max_index(self.top_at[:, i, some], self.top[:, i, some], of[i])); yield
                if lo == 0:
                    for i in range(2):
                        carry()
                        step(dve.match_replace(self.rest[:, i, :], self.top[:, i, some], of[i], LOWEST)); yield
            grid = lambda t: t.rearrange("p (i j) -> p i j", i=TOPK)
            after()
            step(dve.tensor_tensor(grid(self.cand[:, :]), self.top[:, 0, :].unsqueeze(2).broadcast_to([P, TOPK, TOPK]),
                                   self.top[:, 1, :].unsqueeze(1).broadcast_to([P, TOPK, TOPK]), ALU.add)); yield
            best = self.best[:, h * TOPK:(h + 1) * TOPK]
            for lo in (0, TOPK // 2):
                some = slice(lo, lo + TOPK // 2)
                of = self.cand if lo == 0 else self.cand_rest
                carry()
                step(dve.max(best[:, some], of[:, :])); yield
                carry()
                step(dve.max_index(self.place[:, some], best[:, some], of[:, :])); yield
                if lo == 0:
                    carry()
                    step(dve.match_replace(self.cand_rest[:, :], best[:, some], of[:, :], LOWEST)); yield
            after()
            step(dve.tensor_single_scalar(self.digits[:, 0, :], self.place[:, :], 4, ALU.logical_shift_right)); yield
            step(dve.tensor_single_scalar(self.digits[:, 1, :], self.place[:, :], TOPK - 1, ALU.bitwise_and)); yield
            after()
            step(dve.tensor_copy(self.digitsf[:, :, :], self.digits[:, :, :])); yield
            step(dve.tensor_copy(self.top_atf[:, :, :], self.top_at[:, :, :])); yield
            hit3 = self.hit[:, :].rearrange("p (k a) -> p k a", a=TOPK)
            hit4 = self.hit[:, :].rearrange("p (s k a) -> p s k a", s=2, a=TOPK)
            after()
            step(dve.tensor_tensor(hit3, self.digitsf[:, :, :].rearrange("p s k -> p (s k)").unsqueeze(2)
                                   .broadcast_to([P, 2 * TOPK, TOPK]),
                                   self.iota[:, :].unsqueeze(1).broadcast_to([P, 2 * TOPK, TOPK]), ALU.is_equal)); yield
            after()
            step(dve.tensor_tensor(hit4, hit4, self.top_atf[:, :, :].unsqueeze(2)
                                   .broadcast_to([P, 2, TOPK, TOPK]), ALU.mult)); yield
            after()
            step(dve.tensor_reduce(self.side_at[:, :], hit3, AX.X, ALU.add)); yield
            after()
            dve.wait_ge(self.index_set, PH * b + h + 1)
            step(dve.scalar_tensor_tensor(out=self.next_index[:, h * TOPK:(h + 1) * TOPK], in0=self.side_at[:, 0:TOPK],
                                          scalar=float(NK), in1=self.side_at[:, TOPK:], op0=ALU.mult, op1=ALU.add)); yield
            assert n[0] == self.ROUTE_HEAD * (h + 1), n
        heads = lambda t: t[:, :].rearrange("p (h k) -> p h k", h=PH)
        after()
        dve.wait_ge(self.gates_set, b + 1)
        step(dve.tensor_tensor(heads(self.next_gates), heads(self.best),
                               heads(self.best)[:, :, 0:1].broadcast_to([P, PH, TOPK]), ALU.subtract)); yield
        dve.wait_ge(self.exp_done, b + 2)
        step(dve.tensor_reduce(self.norm[:, :], heads(self.next_gates), AX.X, ALU.add)); yield
        after()
        step(dve.reciprocal(self.norm[:, :], self.norm[:, :])); yield
        after()
        step(dve.tensor_tensor(heads(self.next_gates), heads(self.next_gates),
                               self.norm[:, :].unsqueeze(2).broadcast_to([P, PH, TOPK]), ALU.mult)); yield
        assert n[0] == self.ROUTE

    def route_exp(self, act, b):
        act.wait_ge(self.routed, self.ROUTE * (b + 1) + self.ROUTE - 3)
        act.activation(self.next_gates[:, :], self.next_gates[:, :], ACT.Exp).then_inc(self.exp_done, 1)

    def load_scores(self, eng, b):
        eng.wait_ge(self.routed, self.ROUTE * (b + 1))
        eng.dma_start(self.sc[:, :], self.rows("sc_dram", b)).then_inc(self.sc_in, 16)

    def rows(self, name, b):
        return {"sc_dram": self.c.sc_dram, "xn_dram": self.c.xn_dram, "h1_dram": self.c.h1_dram,
                "y": self.c.dram["y"]}[name][bass.ds(b * P, P), :]


class PeerBlock:

    AHEAD = {"pool": RING // 2, "tensor": -2, "scalar": 0, "vector": 0}
    ROUTE_FROM = 4

    def __init__(self, peer, name, eng, b, route, weight):
        self.p, self.name, self.eng, self.b, self.route, self.weight = peer, name, eng, b, route, weight
        self.n = self.passed = self.done = 0
        self.part = {"pool": self.fetch, "tensor": self.add, "scalar": self.gelu, "vector": self.dot}[name]
        self.routing = peer.route(eng, b + 1) if route and name == "vector" else None

    def step(self, weight):
        self.passed += weight
        self.upto(PICKS * self.passed // self.weight + self.AHEAD[self.name])

    def upto(self, n):
        while self.n < min(n, PICKS):
            self.part(self.n)
            self.n += 1

    def finish(self):
        assert self.passed <= self.weight
        self.upto(PICKS)
        if self.name == "vector":
            self.close()
        if self.name == "scalar":
            self.close_root()

    def fetch(self, n):
        p, pool, b, r = self.p, self.eng, self.b, n % RING
        if n % TOPK == 0:
            h = n // TOPK
            cols = slice(n, n + TOPK)
            pool.wait_ge(p.routed, p.ROUTE * (b + 2))
            pool.wait_ge(p.added, PICKS * b + n + 1 + TOPK)
            pool.sem_inc(self.p.c.passed, 1)
            pool.tensor_copy(p.index[:, cols], p.next_index[:, cols]).then_inc(p.index_set, 1)
            pool.wait_ge(p.index_set, PH * (b + 1) + h + 1)
        pool.wait_ge(p.added, PICKS * (b + 1) + n + 1 - RING)
        pool.sem_inc(self.p.c.passed, 1)
        pool.indirect_dma_start(out=p.ring[:, r, :], out_offset=None, in_=p.c.dram["uv"],
                                in_offset=bass.IndirectOffsetOnAxis(ap=p.index[:, n:n + 1], axis=0)).then_inc(p.got[r], 16)

    def dot(self, n):
        p, dve, b, r = self.p, self.eng, self.b, n % RING
        if n == 0:
            dve.wait_ge(p.routed, p.ROUTE * (b + 2))
            dve.wait_ge(p.diag_ready, PICKS * (b + 1))
            dve.tensor_copy(p.gates[:, :], p.next_gates[:, :]).then_inc(p.gates_set, 1)
            dve.wait_ge(p.xn_in, 16 * (b + 1))
        row = p.ring[:, r, 0:D]
        dve.wait_ge(p.got[r], 16 * (PICKS // RING) * b + 16 * (n // RING + 1))
        dve.tensor_tensor_reduce(row, row, p.xn[:, :], 1.0, 0.0, ALU.mult, ALU.add,
                                 p.dots[:, n:n + 1]).then_inc(p.dotted, 1)
        if n:
            self.make_diag(n - 1)
        if self.routing and n >= self.ROUTE_FROM:
            todo = p.ROUTE if n == PICKS - 1 else min(p.ROUTE - 3, -(-p.ROUTE * (n + 1 - self.ROUTE_FROM) // (PICKS - 8)))
            while self.done < todo:
                next(self.routing)
                self.done += 1

    def make_diag(self, n):
        p, dve, b = self.p, self.eng, self.b
        if n == 0:
            dve.wait_ge(p.gates_set, b + 2)
        dve.wait_ge(p.added, PICKS * (b + 1) + n + 1 - p.DIAGS)
        dve.wait_ge(p.gelued, PICKS * (b + 1) + n + 1)
        dve.tensor_scalar(p.diag[:, n % p.DIAGS, :], p.c.ident[:, :], p.gelus[:, n:n + 1], p.gates[:, n:n + 1],
                          ALU.mult, ALU.mult).then_inc(p.diag_ready, 1)

    def close(self):
        p, dve, b = self.p, self.eng, self.b
        self.make_diag(PICKS - 1)
        dve.wait_ge(p.h1_in, 16 * (b + 1))
        dve.wait_ge(p.added, PICKS * (b + 2))
        for h in range(2):
            cols = slice(h * C, (h + 1) * C)
            dve.tensor_tensor(p.h1[:, cols], p.h1[:, cols], p.c.bank[:, 6 + h, :], ALU.add).then_inc(p.summed, 1)
        dve.wait_ge(p.summed, 2 * (b + 2))
        dve.wait_ge(p.y_out, 16 * b + 16)
        dve.tensor_tensor_reduce(p.y[:, :], p.h1[:, :], p.h1[:, :], 1.0, 0.0, ALU.mult, ALU.add,
                                 p.ms[:, :]).then_inc(p.ms_ready, 1)
        dve.wait_ge(p.ms_ready, 2 * (b + 1) + 1)
        dve.tensor_scalar(p.ms[:, :], p.ms[:, :], 1.0 / D, EPS, ALU.mult, ALU.add).then_inc(p.ms_ready, 1)
        dve.wait_ge(p.root_ready, b + 2)
        dve.reciprocal(p.root[:, :], p.root[:, :]).then_inc(p.inv_ready, 1)
        dve.wait_ge(p.inv_ready, b + 2)
        dve.scalar_tensor_tensor(out=p.y[:, :], in0=p.h1[:, :], scalar=p.root[:, 0:1], in1=p.g_final[:, :],
                                 op0=ALU.mult, op1=ALU.mult).then_inc(p.y_ready, 1)

    def gelu(self, n):
        p, act, b = self.p, self.eng, self.b
        if n == 0:
            act.wait_ge(p.dotted, PICKS * (b + 1))
            act.dma_start(p.xn[:, :], p.rows("xn_dram", b)).then_inc(p.xn_in, 16)
            if self.route:
                p.load_scores(act, b + 1)
        if n == 8:
            act.wait_ge(p.y_ready, b + 1)
            act.dma_start(p.h1[:, :], p.rows("h1_dram", b)).then_inc(p.h1_in, 16)
        act.wait_ge(p.dotted, PICKS * (b + 1) + n + 1)
        act.activation(p.gelus[:, n:n + 1], p.dots[:, n:n + 1], ACT.Gelu).then_inc(p.gelued, 1)
        if self.route and n == PICKS - 2:
            p.route_exp(act, b + 1)

    def close_root(self):
        p, act, b = self.p, self.eng, self.b
        act.wait_ge(p.ms_ready, 2 * (b + 2))
        act.activation(p.root[:, :], p.ms[:, :], ACT.Sqrt).then_inc(p.root_ready, 1)
        act.wait_ge(p.y_ready, b + 2)
        act.dma_start(p.rows("y", b), p.y[:, :]).then_inc(p.y_out, 16)

    def add(self, n):
        p, pe, b, r = self.p, self.eng, self.b, n % RING
        if n == 0:
            pe.wait_ge(p.summed, 2 * (b + 1))
        pe.wait_ge(p.diag_ready, PICKS * (b + 1) + n + 1)
        for h in range(2):
            mm = pe.matmul(p.c.bank[:, 6 + h, :], p.diag[:, n % p.DIAGS, :], p.ring[:, r, D + h * C:D + (h + 1) * C],
                           start=(n == 0), stop=(n == PICKS - 1))
        mm.then_inc(p.added, 1)


def first_route(c, peer, b):
    nc = c.nc
    with ExitStack() as ctx:
        sb, sem = scope(c, ctx, f"route{b}_")
        block = ctx.enter_context(nc.Block())

        @block.gpsimd
        def _(pool):
            if b == 0:
                peer.before("pool", pool)
                pool.iota(peer.iota[:, :], pattern=[[1, TOPK]], base=0, channel_multiplier=0,
                          allow_small_or_imprecise_dtypes=True).then_inc(peer.ready, 1)

        @block.tensor
        def _(pe):
            if b == 0:
                peer.before("tensor", pe)

        @block.scalar
        def _(act):
            if b == 0:
                peer.before("scalar", act)
                act.sem_inc(peer.y_out, 16)
                act.dma_start(peer.g_final[:, :], c.dram["g_final"].broadcast_to([P, D])).then_inc(peer.ready_dma, 16)
            peer.load_scores(act, b)
            peer.route_exp(act, b)
            if b == 0:
                act.wait_ge(peer.ready_dma, 16)

        @block.vector
        def _(dve):
            if b == 0:
                peer.before("vector", dve)
                dve.wait_ge(peer.ready, 1)
            for _ in peer.route(dve, b):
                pass


def peer_blocks(c, peer, b0, b1, route):
    nc = c.nc
    with ExitStack() as ctx:
        block = ctx.enter_context(nc.Block())

        def run(name, eng):
            def one(b):
                PeerBlock(peer, name, eng, b, route, 1).finish()
            if b1 - b0 > 1:
                with eng.Fori(b0, b1) as b:
                    one(b)
            else:
                one(b0)

        @block.gpsimd
        def _(pool):
            run("pool", pool)

        @block.tensor
        def _(pe):
            run("tensor", pe)

        @block.scalar
        def _(act):
            run("scalar", act)
            act.wait_ge(peer.y_out, 16 * (b1 + 1))

        @block.vector
        def _(dve):
            run("vector", dve)


def build(nc, dram, dump=None):
    c = Chip()
    c.nc, c.dram = nc, dram
    with ExitStack() as ctx:
        sb = lambda n, s, d=F32: ctx.enter_context(nc.sbuf_tensor(n, s, d))
        c.bank = ctx.enter_context(nc.psum_tensor("bank", [P, 8, C], F32))
        c.passed = ctx.enter_context(nc.semaphore("passed"))
        scratch = lambda n, s: nc.dram_tensor(n, s, F32, kind="Internal").ap()
        c.h1_dram = scratch("h1_dram", [S, D])
        c.xn_dram = scratch("xn_dram", [S, D])
        c.sc_dram = scratch("sc_dram", [S, 2 * PH * NK])
        c.ident = sb("ident", [P, P])
        c.ones = sb("ones", [P, P])
        c.gcols = sb("gcols", [P, G_COLS])
        c.mask = sb("mask", [P, P])
        c.wdw = sb("wdw", [P, KT * (TAPS + 1)])
        c.tails = sb("tails", [P, KT * PAD])
        c.ckvT = sb("ckvT", [P, S])
        c.krT = sb("krT", [P, S])
        alone = lambda *_: Alone()
        for q in range(NCH):
            with ExitStack() as front:
                sb = lambda n, s, d=F32: front.enter_context(nc.sbuf_tensor(f"q{q}_{n}", s, d))
                c.aT = sb("aT", [P, KT, C])
                c.oT = sb("oT", [P, HEADS * C])
                c.acc = sb("acc", [P, KT * C])
                with ExitStack() as mx:
                    sb = lambda n, s, d=F32: mx.enter_context(nc.sbuf_tensor(f"q{q}_{n}", s, d))
                    c.cqT = sb("cqT", [P, QT, C])
                    c.cosT = sb("cosT", [P, C])
                    c.sinT = sb("sinT", [P, C])
                    mixer_inputs(c, q)
                    if dump: dump(c, (q, 0))
                    mixers(c, q, alone)
                if dump: dump(c, (q, 1))
                mix(c, q, alone)
                if dump: dump(c, (q, 2))
                peer_scores(c, q, alone)
                if dump: dump(c, (q, 3))
        with ExitStack() as pe_ctx:
            peer = Peer(c, pe_ctx)
            first_route(c, peer, 0)
            if dump: dump(c, (2, 0), peer)
            peer_blocks(c, peer, 0, S // P - 1, True)
            peer_blocks(c, peer, S // P - 1, S // P, False)


def lay_out(i):
    tile = lambda w: w.reshape(w.shape[0] // P, P, -1).transpose(1, 0, 2)
    cols = lambda v: v.reshape(-1, P).T
    w_in, r = i["w_in"][0], np.arange(ROPE)
    swap = (r + ROPE // 2) % ROPE
    o_gate, o_q, o_kv = D, 2 * D, 2 * D + QL
    o_kr = o_kv + P
    o_mix = o_kr + ROPE
    kr = np.concatenate([r, r])
    pick = lambda cs: tile(w_in[:, cs]).reshape(P, -1)
    at = lambda o: np.arange(o, o + P)
    w_uq = tile(i["w_uq"][0]).reshape(P, QT, HEADS, NOPE + ROPE)
    w_ukv = i["w_ukv"][0].reshape(P, HEADS, NOPE + VDIM)
    by_tile = lambda w: np.stack([tile(w[:, o:o + P]).reshape(P, -1) for o in range(0, w.shape[1], P)])
    ga, gc = by_tile(w_in[:, o_mix + D:]), by_tile(w_in[:, o_mix:o_mix + D])
    ya, yc, yo = by_tile(i["w_attn_out"][0]), by_tile(i["w_conv_out"][0]), by_tile(i["w_o"][0])
    lead = 3
    w_mix = [t for d in range(KT) for t in (ga[d], ya[d])] + [gc[d] for d in range(lead)]
    for d in range(KT):
        w_mix += [yc[d]] + ([gc[d + lead]] if d + lead < KT else [])
    w_mix = np.stack(w_mix + list(yo))
    half = ROPE // 2
    freq = np.float32(ROPE_BASE) ** (-np.arange(half, dtype=np.float32) / np.float32(half))
    sign = np.repeat(np.array([-1, 1, -1, 1], np.float32), half)
    return {
        "x": i["x"][0],
        "xT": i["x"][0].T.reshape(KT, P, S),
        "pos": i["positions"],
        "rope": np.stack([np.tile(freq, 4), sign], 1).astype(np.float32),
        "gcols": np.concatenate([cols(i[n][0]) for n in ("mix_norm_g", "q_norm_g", "kv_norm_g", "conv_ln_g",
                                                          "conv_ln_b", "b_gate")], 1),
        "wdw": np.concatenate([i["w_dw"][0, :, 0], i["b_dw"]], 0).reshape(TAPS + 1, KT, P)
                 .transpose(2, 1, 0).reshape(P, -1),
        "w_pre": np.stack([pick(at(o_q)), pick(at(o_q + P)), pick(at(o_kv)), pick(o_kr + kr),
                           pick(o_kr + swap[kr])]),
        "w_vg": np.stack([pick(at(o + h * P)) for h in range(KT) for o in (o_gate, 0)]),
        "w_head": np.stack([np.concatenate([w_uq[:, :, h, :NOPE].reshape(P, -1), w_ukv[:, h, :NOPE],
                                            w_ukv[:, h, NOPE:]], 1) for h in range(HEADS)]),
        "w_rope": np.stack([np.concatenate([w_uq[:, :, h:h + 2, NOPE + rs].reshape(P, -1) for rs in (r, swap)], 1)
                            for h in range(0, HEADS, 2)]),
        "w_mix": w_mix,
        "g_ffn": i["ffn_norm_g"],
        "w_peer": by_tile(i["w_peer_q"][0]),
        "keysT": i["peer_sub_keys"][0].transpose(3, 0, 1, 2).reshape(P, -1),
        "uv": np.concatenate([i["peer_u"][0], i["peer_v"][0]], 1),
        "g_final": i["final_norm_g"][None],
    }


def kernel(**inputs):
    import concourse.bacc as bacc
    from concourse.bass_utils import run_bass_kernel_spmd

    nc = bacc.Bacc("TRN2", target_bir_lowering=False, num_devices=1)
    arrays, dram = {}, {}
    for name, a in lay_out({k: np.asarray(v) for k, v in inputs.items()}).items():
        arrays["in_" + name] = np.ascontiguousarray(a)
        dram[name] = nc.dram_tensor("in_" + name, a.shape, mybir.dt.from_np(a.dtype), kind="ExternalInput").ap()
    dram["y"] = nc.dram_tensor("out_y", (S, D), F32, kind="ExternalOutput").ap()
    build(nc, dram)
    return run_bass_kernel_spmd(nc, [arrays], core_ids=[0]).results[0]["out_y"].reshape(1, S, D)
```

```python
from contextlib import ExitStack

import concourse.bass as bass
import numpy as np
from concourse import mybir

F32 = mybir.dt.float32
I32 = mybir.dt.int32
U32 = mybir.dt.uint32
ALU = mybir.AluOpType
ACT = mybir.ActivationFunctionType
AX = mybir.AxisListType

P = 128
D = 1024
S = 1024
KT = D // P
C = 512
NCH = S // C
CB = C // P
EPS = 1e-6
TAPS = 31
PAD = TAPS - 1
PE_TAPS = (9, 4)
HEADS = 8
SUBS = 4
NOPE, ROPE, VDIM = 128, 64, 128
QL = 256
QT = QL // P
SCALE = float(1.0 / np.sqrt(NOPE + ROPE))
MASKED = -1e30
ROPE_BASE = 10000.0
PH = 8
NK = 128
TOPK = 16
PICKS = PH * TOPK
RING = 8
PRE = 5
LOWEST = -3e38

G_MIX, G_Q, G_KV = 0, KT, KT + QT
G_LNG = G_KV + 1
G_LNB = G_LNG + KT
G_BGATE = G_LNB + KT
G_COLS = G_BGATE + 2 * KT


class Chip:
    pass


def item(a):
    return a.rearrange("a p n -> (a p) n")


class Alone:

    def step(self, weight):
        pass

    def finish(self):
        pass


def total_weight(steps):
    passed = []
    counter = Alone()
    counter.step = passed.append
    steps(lambda *_: None, counter)
    return sum(passed)


def scope(c, ctx, prefix):
    nc, sems = c.nc, []

    def clear():
        nc.clear_and_free_semaphores(sems)
        nc.all_engine_barrier()

    def sem(name):
        sems.append(nc.alloc_semaphore(name=prefix + name))
        return sems[-1]

    ctx.callback(clear)
    return (lambda name, shape, dtype=F32: ctx.enter_context(nc.sbuf_tensor(prefix + name, shape, dtype))), sem


def mixer_inputs(c, q, peer):
    nc, bank, ident, ones = c.nc, c.bank, c.ident, c.ones
    aT, cqT, ckvT, krT, cosT, sinT = c.aT, c.cqT, c.ckvT, c.krT, c.cosT, c.sinT
    own = slice(q * C, (q + 1) * C)
    TWO_PI = 2 * np.pi
    C1 = 6.28125
    C2 = float(np.floor((TWO_PI - C1) * 2 ** 20) / 2 ** 20)
    C3 = float(np.float32(TWO_PI - C1 - C2))
    MAGIC = float(1.5 * 2 ** 23)
    with ExitStack() as ctx:
        sb, sem = scope(c, ctx, f"q{q}inputs_")
        wpre = sb("wpre", [P, PRE, D])
        sq = sb("sq", [P, 2, C])
        rs = sb("rs", [P, C])
        posi = sb("posi", [P, C], I32)
        ang = sb("ang", [P, C])
        turns = sb("turns", [P, C])
        red = sb("red", [P, 2, C])
        rope_c = sb("rope_c", [P, 2])
        x_in = [sem(f"x_in{i}") for i in range(KT)]
        w_in = [sem(f"wpre_in{i}") for i in range(PRE)]
        small_in = sem(f"small_in")
        cst = sem(f"cst")
        squared = sem(f"squared")
        summed = sem(f"summed")
        mean_ready = sem(f"mean_ready")
        root_ready = sem(f"root_ready")
        rs_ready = sem(f"rs_ready")
        a_ready = sem(f"a_ready")
        proj = sem(f"proj")
        copied = sem(f"copied")
        roped = sem(f"roped")
        normed = sem(f"normed")
        chain = sem(f"chain")
        angles = sem(f"angles")
        tables = sem(f"tables")
        block = ctx.enter_context(nc.Block())
        N_CQ, N_CKV = QT, 1

        @block.sync
        def _(sp):
            if q == 0:
                sp.dma_start(c.gcols[:, :], c.dram["gcols"]).then_inc(small_in, 16)
                sp.dma_start(c.wdw[:, :], c.dram["wdw"]).then_inc(small_in, 16)
            for k in range(KT):
                sp.dma_start(aT[:, k, :], c.dram["xT"][k, :, own]).then_inc(x_in[k], 16)
            for i in range(PRE):
                sp.dma_start(wpre[:, i, :], c.dram["w_pre"][i]).then_inc(w_in[i], 16)
            sp.dma_start(rope_c[:, :], c.dram["rope"]).then_inc(small_in, 16)
            sp.dma_start(posi[:, :], c.dram["pos"][:, own].broadcast_to([P, C])).then_inc(small_in, 16)
            if q:
                sp.dma_start(peer.g_final[:, :], c.dram["g_final"].broadcast_to([P, D])).then_inc(small_in, 16)

        @block.gpsimd
        def _(pool):
            if q:
                return
            pool.memset(ident[:, :], 0.0).then_inc(cst, 1)
            pool.memset(c.mask[:, :], 0.0).then_inc(cst, 1)
            pool.memset(ones[:, :], 1.0).then_inc(cst, 1)
            pool.wait_ge(cst, 3)
            pool.affine_select(out=ident[:, :], in_=ident[:, :], compare_op=ALU.not_equal, fill=1.0,
                               base=0, pattern=[[-1, P]], channel_multiplier=1).then_inc(cst, 1)
            pool.affine_select(out=c.mask[:, :], in_=c.mask[:, :], compare_op=ALU.is_ge, fill=MASKED,
                               base=0, pattern=[[-1, P]], channel_multiplier=1).then_inc(cst, 1)

        groups = [KT, N_CQ, N_CKV]
        width = [D, QL, P]

        @block.scalar
        def _(act):
            def squares(g, tile, ready):
                first = sum(groups[:g])
                for k in range(groups[g]):
                    n = first + k
                    ready(k)
                    if n >= 2:
                        act.wait_ge(summed, n - 1)
                    act.activation(sq[:, n % 2, :], tile(k), ACT.Square).then_inc(squared, 1)

            def root(g):
                act.wait_ge(mean_ready, g + 1)
                act.activation(rs[:, :], rs[:, :], ACT.Sqrt).then_inc(root_ready, 1)

            squares(0, lambda k: aT[:, k, :], lambda k: act.wait_ge(x_in[k], 16))
            root(0)
            act.wait_ge(angles, 2)
            act.activation(cosT[:, :], red[:, 0, :], ACT.Sin).then_inc(tables, 1)
            act.activation(sinT[:, :], red[:, 1, :], ACT.Sin, scale=rope_c[:, 1:2]).then_inc(tables, 1)
            for n in range(N_CQ + N_CKV):
                act.wait_ge(proj, n + 1)
                act.activation(cqT[:, n, :] if n < N_CQ else ckvT[:, own], bank[:, 1 + n, :],
                               ACT.Copy).then_inc(copied, 1)
            squares(1, lambda k: cqT[:, k, :], lambda k: act.wait_ge(copied, k + 1))
            root(1)
            squares(2, lambda k: ckvT[:, own], lambda k: act.wait_ge(copied, N_CQ + 1))
            act.wait_ge(normed, N_CQ)
            root(2)

        @block.tensor
        def _(pe):
            if q == 0:
                pe.wait_ge(cst, 5)

            def sums(g):
                first = sum(groups[:g])
                if g:
                    pe.wait_ge(mean_ready, g)
                for k in range(groups[g]):
                    pe.wait_ge(squared, first + k + 1)
                    pe.matmul(bank[:, 0, :], ones[:, :], sq[:, (first + k) % 2, :],
                              start=(k == 0), stop=(k == groups[g] - 1)).then_inc(summed, 1)

            sums(0)
            pe.wait_ge(a_ready, KT)
            for n in range(PRE):
                pe.wait_ge(w_in[n], 16)
                for k in range(KT):
                    mm = pe.matmul(bank[:, 1 + n, :], wpre[:, n, k * P:(k + 1) * P], aT[:, k, :],
                                   start=(k == 0), stop=(k == KT - 1))
                mm.then_inc(proj, 1)
            sums(1)
            sums(2)

        @block.vector
        def _(dve):
            count = [0]

            def link(ins):
                count[0] += 1
                ins.then_inc(chain, 1)
                dve.wait_ge(chain, count[0])

            def mean(g):
                dve.wait_ge(summed, sum(groups[:g + 1]))
                if g == 2:
                    dve.wait_ge(normed, N_CQ)
                dve.tensor_scalar(rs[:, :], bank[:, 0, :], 1.0 / width[g], EPS,
                                  ALU.mult, ALU.add).then_inc(mean_ready, 1)
                dve.wait_ge(root_ready, g + 1)
                dve.reciprocal(rs[:, :], rs[:, :]).then_inc(rs_ready, 1)
                dve.wait_ge(rs_ready, g + 1)

            dve.wait_ge(small_in, 48 if q else 64)
            mean(0)
            for k in range(KT):
                dve.scalar_tensor_tensor(out=aT[:, k, :], in0=aT[:, k, :], scalar=c.gcols[:, k:k + 1],
                                         in1=rs[:, :], op0=ALU.mult, op1=ALU.mult).then_inc(a_ready, 1)
            link(dve.tensor_copy(ang[:, :], posi[:, :]))
            link(dve.tensor_scalar(ang[:, :], ang[:, :], rope_c[:, 0:1], None, ALU.mult))
            for i, quarter in enumerate((0.25, 0.0)):
                link(dve.tensor_scalar(turns[:, :], ang[:, :], 1.0 / TWO_PI, quarter, ALU.mult, ALU.add))
                link(dve.tensor_scalar(turns[:, :], turns[:, :], MAGIC, None, ALU.add))
                link(dve.tensor_scalar(turns[:, :], turns[:, :], -MAGIC, None, ALU.add))
                src = ang[:, :]
                for part in (C1, C2, C3):
                    link(dve.scalar_tensor_tensor(out=red[:, i, :], in0=turns[:, :], scalar=-part, in1=src,
                                                  op0=ALU.mult, op1=ALU.add))
                    src = red[:, i, :]
                link(dve.tensor_scalar(src, src, quarter * TWO_PI, float(np.float32(3.1415925)), ALU.add, ALU.min))
                dve.tensor_scalar(src, src, float(np.float32(-3.1415925)), None, ALU.max).then_inc(angles, 1)
            dve.wait_ge(tables, 2)
            dve.wait_ge(proj, PRE - 1)
            link(dve.tensor_tensor(krT[:, own], bank[:, PRE - 1, :], cosT[:, :], ALU.mult))
            dve.wait_ge(proj, PRE)
            link(dve.tensor_tensor(turns[:, :], bank[:, PRE, :], sinT[:, :], ALU.mult))
            dve.tensor_tensor(krT[:, own], krT[:, own], turns[:, :], ALU.add).then_inc(roped, 1)
            dve.wait_ge(a_ready, KT)
            mean(1)
            for k in range(N_CQ):
                dve.scalar_tensor_tensor(out=cqT[:, k, :], in0=cqT[:, k, :], scalar=c.gcols[:, KT + k:KT + k + 1],
                                         in1=rs[:, :], op0=ALU.mult, op1=ALU.mult).then_inc(normed, 1)
            mean(2)
            dve.scalar_tensor_tensor(out=ckvT[:, own], in0=ckvT[:, own], scalar=c.gcols[:, KT + QT:KT + QT + 1],
                                     in1=rs[:, :], op0=ALU.mult, op1=ALU.mult).then_inc(normed, 1)
            dve.wait_ge(normed, N_CQ + 1)
            dve.wait_ge(roped, 1)


class Events:

    def __init__(self, names):
        self.names = list(names)
        self.n = len(self.names)
        self.place = {name: k + 1 for k, name in enumerate(self.names)}

    def value(self, t, *name):
        return (t + 1) * self.n + self.place[name]

    def before(self, t, back, *name):
        return (t + 1) * self.n + self.place[name] - back


def mixers(c, q, beside):
    nc, bank, ident = c.nc, c.bank, c.ident
    aT, cqT, ckvT, krT, cosT, sinT, oT, acc = c.aT, c.cqT, c.ckvT, c.krT, c.cosT, c.sinT, c.oT, c.acc
    NPE = PE_TAPS[q]
    V_TAPS = TAPS - NPE
    EARLY_TAPS, STEP_TAPS = ((2, 0), (3, 2))[q]
    QUADS = q + 1
    SLOTS = NCH - q
    SUB, QB, KEYS = range(SUBS), range(CB), range(QUADS)
    quads = lambda j: range(QUADS)
    width = lambda j: (CB * q + j + 1) * P
    last_of = lambda p, j, back: (p, j - back) if j >= back else ((p - 1) % SUBS, CB + j - back)
    when = lambda t, p, j, back: t if j >= back or p else t - 1

    JOBS = [(p, name, h) for p in SUB for name in ["gate", "val", "q"] + ["qr", "qs"] * (p % 2 == 0) + ["conv", "k", "v"]
            for h in (KEYS if name in "kv" else range(1))]
    BY_DVE = ("val", "qr", "qs", "conv")
    proj_e = Events(JOBS)
    copied_e = Events(j for j in JOBS if j[1] not in BY_DVE)
    taken_e = Events(j for j in JOBS if j[1] in BY_DVE)
    blocks_e = Events((p, j) for p in SUB for j in QB)
    groups_e = Events((p, j, g) for p in SUB for j in QB for g in quads(j))
    subs_e = Events((p,) for p in SUB)
    taps_e = Events((p, k) for p in SUB for k in range(V_TAPS))
    roped_e = Events((p,) for p in SUB if p % 2 == 0)
    assert proj_e.n % 2 == 0 and groups_e.n % 2 == 0
    STEPS = {"gate": 7, "val": 7, "q": 3, "conv": NPE, "kv": 2 * QUADS, "first": 2 * QUADS, 
             "turn": 2 + QUADS, "attend": QUADS, "tail": 1}
    PER_BLOCK = ("turn", "attend", "tail")
    WEIGHT = SUBS * sum(w * (CB if name in PER_BLOCK else 1) for name, w in STEPS.items())

    with ExitStack() as ctx:
        sb, sem = scope(c, ctx, f"q{q}mixers_")
        w_vg = sb("w_vg", [P, 2, D])
        w_head = sb("w_head", [P, QT * P + 2 * P])
        w_rope = sb("w_rope", [P, 2, QT * P])
        hT = sb("hT", [P, PAD + C])
        w_tap = sb("w_tap", [P, 2, TAPS + 1])
        tap_diag = sb("tap_diag", [P, NPE, P])
        sig = sb("sig", [P, C])
        qT = sb("qT", [P, C])
        kT = sb("kT", [P, QUADS * C])
        V = sb("V", [P, QUADS * C])
        qrT = sb("qrT", [P, C])
        swapped = sig
        prob = sb("prob", [P, SLOTS, QUADS * C])
        probT = sb("probT", [P, 2, C])
        peak = sb("peak", [P, 2])
        low = sb("low", [P, 2])
        total = sb("total", [P, 2])
        inv = sb("inv", [P, 2])
        inv_diag = sb("inv_diag", [P, 2, P])

        w_vg_in = [sem(f"w_vg_in{i}") for i in range(2)]
        w_head_in = sem("w_head_in")
        w_rope_in = sem("w_rope_in")
        proj = sem("proj")
        copied = sem("copied")
        taken = sem("taken")
        roped = sem("roped")
        padded = sem("padded")
        tap_cols = sem("tap_cols")
        tap_mats = sem("tap_mats")
        scored = sem("scored")
        maxed = sem("maxed")
        peaked = sem("peaked")
        exped = sem("exped")
        inverted = sem("inverted")
        inv_ready = sem("inv_ready")
        turned = sem("turned")
        turned_out = sem("turned_out")
        used = sem("used")
        oT_out = sem("oT_out")
        tapped = sem("tapped")
        block = ctx.enter_context(nc.Block())
        tile = lambda t, p: bass.ds((SUBS * t + p) * C, C)
        score_banks = lambda j: bank[:, 2 + j % SLOTS:2 + j % SLOTS + QUADS, :].rearrange("p a n -> p (a n)")

        @block.sync
        def _(sp):
            with sp.Fori(0, HEADS // SUBS) as t:
                for p in SUB:
                    old = (p - 1) % SUBS
                    ago = t if p else t - 1
                    for i, name in enumerate(("gate", "val")):
                        sp.wait_ge(proj, proj_e.value(ago, old, name, 0))
                        sp.dma_start(w_vg[:, i, :], item(c.dram["w_vg"][bass.ds(2 * SUBS * t + 2 * p + i, 1)])
                                     ).then_inc(w_vg_in[i], 16)
                    sp.wait_ge(proj, proj_e.value(ago, old, "v", q))
                    sp.dma_start(w_head[:, :], item(c.dram["w_head"][bass.ds(SUBS * t + p, 1)])
                                 ).then_inc(w_head_in, 16)
                    if p % 2 == 0:
                        sp.wait_ge(proj, proj_e.value(t if p else t - 1, (p - 2) % SUBS, "qs", 0))
                        sp.dma_start(w_rope[:, :, :].rearrange("p a n -> p (a n)"),
                                     item(c.dram["w_rope"][bass.ds(SUBS // 2 * t + p // 2, 1)])).then_inc(w_rope_in, 16)

        filled = lambda t, p: 16 * (SUBS * t + p + 1)

        @block.gpsimd
        def _(pool):
            pool.sem_inc(tap_cols, subs_e.n)
            pool.sem_inc(tap_mats, subs_e.n)
            with pool.Fori(0, HEADS // SUBS) as t:
                side = beside("pool", pool, t, WEIGHT)
                for p in SUB:
                    pool.wait_ge(tapped, taps_e.value(t if p >= 2 else t - 1, (p - 2) % SUBS, V_TAPS - 1))
                    pool.sem_inc(c.passed, 1)
                    pool.tensor_copy(w_tap[:, p % 2, :], c.wdw[:, bass.ds((SUBS * t + p) * (TAPS + 1), TAPS + 1)]
                                     ).then_inc(tap_cols, 1)
                    pool.wait_ge(tap_cols, subs_e.value(t, p))
                    pool.wait_ge(proj, proj_e.value(t if p else t - 1, (p - 1) % SUBS, "conv", 0))
                    pool.sem_inc(c.passed, 1)
                    for k in range(NPE):
                        ins = pool.tensor_scalar(tap_diag[:, k, :], ident[:, :], w_tap[:, p % 2, k:k + 1], None, ALU.mult)
                    ins.then_inc(tap_mats, 1)
                    for name, w in STEPS.items():
                        if name not in PER_BLOCK:
                            side.step(w)
                    for _ in QB:
                        for name in PER_BLOCK:
                            side.step(STEPS[name])
                side.finish()

        @block.tensor
        def _(pe):
            for s_, e in ((proj, proj_e), (scored, blocks_e), (turned, groups_e), (used, groups_e)):
                pe.sem_inc(s_, e.n)
            with pe.Fori(0, HEADS // SUBS) as t:
                side = beside("tensor", pe, t, WEIGHT)

                def job(p, name, h, products):
                    n = proj_e.place[p, name, h] - 1
                    last = JOBS[n - 2]
                    ev, s_ = (taken_e, taken) if last[1] in BY_DVE else (copied_e, copied)
                    pe.wait_ge(s_, ev.value(t if n >= 2 else t - 1, *last))
                    for lhs, rhs, lo, w, a, b in products:
                        mm = pe.matmul(bank[:, n % 2, lo:lo + w], lhs, rhs, start=a, stop=b)
                    mm.then_inc(proj, 1)

                def full(w, x, k_tiles):
                    return [(w(k), x(k), 0, C, k == 0, k == k_tiles - 1) for k in range(k_tiles)]

                def scores(p, j):
                    h64 = slice(64 * (p % 2), 64 * (p % 2) + 64)
                    if j == 0:
                        pe.wait_ge(copied, copied_e.value(t, p, "k", q))
                        if p % 2 == 0:
                            pe.wait_ge(roped, roped_e.value(t, p))
                    pe.wait_ge(exped, blocks_e.before(t, SLOTS, p, j))
                    qs = slice(j * P, (j + 1) * P)
                    for h in KEYS:
                        w = min(width(j) - h * C, C)
                        ks = slice(h * C, h * C + w)
                        out = bank[:, 2 + j % SLOTS + h, :]
                        diag = h == q
                        pe.matmul(out[:, 0:w], qT[:, qs], kT[:, ks], start=True, stop=False)
                        mm = pe.matmul(out[:, 0:w], qrT[h64, qs], krT[h64, ks], start=False, stop=not diag)
                        if diag:
                            mm = pe.matmul(out[:, w - P:w], ident[:, :], c.mask[:, :], start=False, stop=True)
                    mm.then_inc(scored, 1)

                def turn(p, j, g):
                    if g == 0:
                        pe.wait_ge(inv_ready, blocks_e.value(t, p, j))
                    pe.wait_ge(turned_out, groups_e.before(t, 1, p, j, g))
                    for b in range(min(CB * q + j + 1 - 4 * g, 4)):
                        kb = 4 * g + b
                        mm = pe.matmul(bank[:, 4, b * P:(b + 1) * P], prob[:, j % SLOTS, kb * P:(kb + 1) * P],
                                       inv_diag[:, j % 2, :], start=True, stop=True)
                    mm.then_inc(turned, 1)

                def attend(p, j, g):
                    if j == 0 and g == 0:
                        pe.wait_ge(copied, copied_e.value(t, p, "v", q))
                        pe.wait_ge(oT_out, subs_e.before(t, 1, p))
                    pe.wait_ge(turned_out, groups_e.value(t, p, j, g))
                    n = groups_e.place[p, j, g] - 1
                    own = CB * q + j
                    for kb in range(4 * g, min(own + 1, 4 * g + 4)):
                        mm = pe.matmul(bank[:, 5, j * P:(j + 1) * P], V[:, kb * P:(kb + 1) * P],
                                       probT[:, n % 2, (kb % 4) * P:(kb % 4 + 1) * P], start=(kb == 0), stop=(kb == own))
                    mm.then_inc(used, 1)

                for p in SUB:
                    for i, name in enumerate(("gate", "val")):
                        pe.wait_ge(w_vg_in[i], filled(t, p))
                        job(p, name, 0, full(lambda k: w_vg[:, i, k * P:(k + 1) * P], lambda k: aT[:, k, :], KT))
                        side.step(STEPS[name])
                    pe.wait_ge(w_head_in, filled(t, p))
                    job(p, "q", 0, full(lambda k: w_head[:, k * P:(k + 1) * P], lambda k: cqT[:, k, :], QT))
                    if p % 2 == 0:
                        pe.wait_ge(w_rope_in, 16 * (SUBS // 2 * t + p // 2 + 1))
                        for i, name in enumerate(("qr", "qs")):
                            job(p, name, 0, full(lambda k: w_rope[:, i, k * P:(k + 1) * P], lambda k: cqT[:, k, :], QT))
                    side.step(STEPS["q"])
                    pe.wait_ge(padded, subs_e.value(t, p))
                    pe.wait_ge(taken, taken_e.value(t, p, "val", 0))
                    pe.wait_ge(tap_mats, subs_e.value(t, p))
                    job(p, "conv", 0, [(tap_diag[:, k, :], hT[:, k:k + C], 0, C, k == 0, k == NPE - 1)
                                       for k in range(NPE)])
                    side.step(STEPS["conv"])
                    for h in KEYS:
                        job(p, "k", h, full(lambda k: w_head[:, QT * P:(QT + 1) * P],
                                            lambda k: ckvT[:, h * C:(h + 1) * C], 1))
                    for h in KEYS:
                        job(p, "v", h, [(ckvT[:, (4 * h + b) * P:(4 * h + b + 1) * P], w_head[:, (QT + 1) * P:],
                                         b * P, P, True, True) for b in range(4)])
                    side.step(STEPS["kv"])
                    for j in range(SLOTS):
                        scores(p, j)
                    side.step(STEPS["first"])
                    for j in QB:
                        turn(p, j, 0)
                        if j + SLOTS < CB and SLOTS > 1:
                            scores(p, j + SLOTS)
                        for g in quads(j)[1:]:
                            turn(p, j, g)
                        if j + SLOTS < CB and SLOTS == 1:
                            scores(p, j + SLOTS)
                        side.step(STEPS["turn"])
                        for g in quads(j):
                            attend(p, j, g)
                        side.step(STEPS["attend"])
                        side.step(STEPS["tail"])
                side.finish()

        @block.scalar
        def _(act):
            for s_, e in ((copied, copied_e), (exped, blocks_e), (turned_out, groups_e), (oT_out, subs_e)):
                act.sem_inc(s_, e.n)
            with act.Fori(0, HEADS // SUBS) as t:
                side = beside("scalar", act, t, WEIGHT)

                def take(p, name, h=0):
                    n = proj_e.place[p, name, h] - 1
                    act.wait_ge(proj, proj_e.value(t, p, name, h))
                    if name == "gate":
                        if p % 2:
                            act.wait_ge(roped, roped_e.value(t, p - 1))
                        else:
                            act.wait_ge(taken, taken_e.value(t if p else t - 1, (p - 1) % SUBS, "val", 0))
                        dst, func = sig[:, :], ACT.Sigmoid
                    else:
                        dst, func = {"q": qT, "k": kT, "v": V}[name][:, h * C:(h + 1) * C], ACT.Copy
                    act.activation(dst, bank[:, n % 2, :], func).then_inc(copied, 1)

                def exps(p, j):
                    act.wait_ge(peaked, blocks_e.value(t, p, j))
                    act.wait_ge(turned, groups_e.value(when(t, p, j, SLOTS), *last_of(p, j, SLOTS), q))
                    act.activation(prob[:, j % SLOTS, 0:width(j)], score_banks(j)[:, 0:width(j)], ACT.Exp,
                                   bias=low[:, j % 2:j % 2 + 1], scale=SCALE,
                                   accum_out=total[:, j % 2:j % 2 + 1]).then_inc(exped, 1)

                def turned_copy(p, j, g):
                    n = groups_e.place[p, j, g] - 1
                    w = min(width(j) - 4 * g * P, C)
                    act.wait_ge(turned, groups_e.value(t, p, j, g))
                    act.wait_ge(used, groups_e.before(t, 2, p, j, g))
                    act.activation(probT[:, n % 2, 0:w], bank[:, 4, 0:w], ACT.Copy).then_inc(turned_out, 1)

                for p in SUB:
                    take(p, "gate")
                    side.step(STEPS["gate"])
                    side.step(STEPS["val"])
                    take(p, "q")
                    side.step(STEPS["q"])
                    side.step(STEPS["conv"])
                    for name in "kv":
                        for h in KEYS:
                            take(p, name, h)
                    side.step(STEPS["kv"])
                    for j in range(SLOTS):
                        exps(p, j)
                    side.step(STEPS["first"])
                    for j in QB:
                        for g in quads(j):
                            turned_copy(p, j, g)
                        side.step(STEPS["turn"])
                        if j + SLOTS < CB:
                            exps(p, j + SLOTS)
                        side.step(STEPS["attend"])
                        if j == CB - 1:
                            act.wait_ge(used, groups_e.value(t, p, j, q))
                            act.activation(oT[:, tile(t, p)], bank[:, 5, :], ACT.Copy).then_inc(oT_out, 1)
                        side.step(STEPS["tail"])
                side.finish()

        @block.vector
        def _(dve):
            for s_, e in ((taken, taken_e), (peaked, blocks_e), (inv_ready, blocks_e), (maxed, blocks_e),
                          (inverted, blocks_e), (tapped, taps_e), (roped, roped_e), (padded, subs_e)):
                dve.sem_inc(s_, e.n)
            with dve.Fori(0, HEADS // SUBS) as t:
                side = beside("vector", dve, t, WEIGHT)

                def low_of(p, j):
                    one = slice(j % 2, j % 2 + 1)
                    dve.wait_ge(scored, blocks_e.value(t, p, j))
                    dve.wait_ge(peaked, blocks_e.before(t, 2, p, j))
                    dve.tensor_reduce(peak[:, one], score_banks(j)[:, 0:width(j)], AX.X, ALU.max).then_inc(maxed, 1)
                    dve.wait_ge(maxed, blocks_e.value(t, p, j))
                    dve.wait_ge(exped, blocks_e.before(t, 2, p, j))
                    dve.tensor_scalar(low[:, one], peak[:, one], -SCALE, None, ALU.mult).then_inc(peaked, 1)

                def inv_of(p, j):
                    one = slice(j % 2, j % 2 + 1)
                    dve.wait_ge(exped, blocks_e.value(t, p, j))
                    dve.reciprocal(inv[:, one], total[:, one]).then_inc(inverted, 1)
                    dve.wait_ge(inverted, blocks_e.value(t, p, j))
                    dve.wait_ge(turned, groups_e.value(when(t, p, j, 2), *last_of(p, j, 2), q))
                    dve.tensor_scalar(inv_diag[:, j % 2, :], ident[:, :], inv[:, one], None, ALU.mult).then_inc(inv_ready, 1)

                def conv_start(p):
                    n = proj_e.place[p, "conv", 0] - 1
                    dve.wait_ge(proj, proj_e.value(t, p, "conv", 0))
                    dve.wait_ge(tap_cols, subs_e.value(t, p))
                    dve.tensor_scalar(acc[:, tile(t, p)], bank[:, n % 2, :], w_tap[:, p % 2, TAPS:TAPS + 1], None,
                                      ALU.add).then_inc(taken, 1)

                def taps(p, first, n):
                    for k in range(first, min(first + n, V_TAPS)):
                        if k == 0:
                            dve.wait_ge(taken, taken_e.value(t, p, "conv", 0))
                        else:
                            dve.wait_ge(tapped, taps_e.value(t, p, k - 1))
                        dve.scalar_tensor_tensor(out=acc[:, tile(t, p)], in0=hT[:, NPE + k:NPE + k + C],
                                                 scalar=w_tap[:, p % 2, NPE + k:NPE + k + 1], in1=acc[:, tile(t, p)],
                                                 op0=ALU.mult, op1=ALU.add).then_inc(tapped, 1)
                    return min(first + n, V_TAPS)

                for p in SUB:
                    dve.wait_ge(tapped, taps_e.value(t if p else t - 1, (p - 1) % SUBS, V_TAPS - 1))
                    tail = c.tails[:, bass.ds((SUBS * t + p) * PAD, PAD)]
                    if q == 0:
                        dve.memset(hT[:, 0:PAD], 0.0).then_inc(padded, 1)
                    else:
                        dve.tensor_copy(hT[:, 0:PAD], tail).then_inc(padded, 1)
                    side.step(STEPS["gate"])
                    n = proj_e.place[p, "val", 0] - 1
                    dve.wait_ge(copied, copied_e.value(t, p, "gate", 0))
                    dve.wait_ge(proj, proj_e.value(t, p, "val", 0))
                    dve.tensor_tensor(hT[:, PAD:], bank[:, n % 2, :], sig[:, :], ALU.mult).then_inc(taken, 1)
                    dve.wait_ge(taken, taken_e.value(t, p, "val", 0))
                    dve.wait_ge(padded, subs_e.value(t, p))
                    if q == 0:
                        dve.tensor_copy(tail, hT[:, C:C + PAD])
                    side.step(STEPS["val"])
                    if p % 2 == 0:
                        for name, dst, table in (("qr", qrT, cosT), ("qs", swapped, sinT)):
                            n = proj_e.place[p, name, 0] - 1
                            dve.wait_ge(proj, proj_e.value(t, p, name, 0))
                            dve.tensor_tensor(dst[:, :], bank[:, n % 2, :], table[:, :], ALU.mult).then_inc(taken, 1)
                        dve.wait_ge(taken, taken_e.value(t, p, "qs", 0))
                        dve.tensor_tensor(qrT[:, :], qrT[:, :], swapped[:, :], ALU.add).then_inc(roped, 1)
                    side.step(STEPS["q"])
                    conv_start(p)
                    k = taps(p, 0, EARLY_TAPS)
                    side.step(STEPS["conv"])
                    side.step(STEPS["kv"])
                    for j in range(SLOTS):
                        low_of(p, j)
                    side.step(STEPS["first"])
                    for j in QB:
                        inv_of(p, j)
                        k = taps(p, k, STEP_TAPS)
                        side.step(STEPS["turn"])
                        if j + SLOTS < CB:
                            low_of(p, j + SLOTS)
                        k = taps(p, k, STEP_TAPS)
                        side.step(STEPS["attend"])
                        k = taps(p, k, STEP_TAPS)
                        side.step(STEPS["tail"])
                    taps(p, k, V_TAPS)
                side.finish()


def mix(c, q, beside):
    nc, bank, ident, ones = c.nc, c.bank, c.ident, c.ones
    aT, oT, acc = c.aT, c.oT, c.acc
    x4 = acc[:, :].rearrange("p (b d) -> p b d", b=CB)
    h1 = oT[:, :].rearrange("p (b d) -> p b d", b=CB)
    WR, SG, BANKS = 3, 4, 5
    LEAD = 3
    JOBS = [("mean", 0)]
    for d in range(KT):
        JOBS += [("ga", d), ("ya", d)]
    JOBS += [("gc", d) for d in range(LEAD)]
    for d in range(KT):
        JOBS += [("yc", d)] + [("gc", d + LEAD)] * (d + LEAD < KT)
    JOBS += [("o", d) for d in range(KT)]
    TILES = JOBS[1:]
    GATES = [j for j in JOBS if j[0] in ("ga", "gc")]
    assert len(TILES) == 5 * KT
    N = {j: n for n, j in enumerate(JOBS)}
    BY_ACT = [j for j in JOBS if j[0] in ("ga", "gc")]
    BY_DVE = [j for j in JOBS if j[0] not in ("ga", "gc")]

    with ExitStack() as ctx:
        sb, sem = scope(c, ctx, f"q{q}mix_")
        mixT = sb("mixT", [P, KT, C])
        w = sb("w", [P, WR, D])
        sig = sb("sig", [P, SG, C])
        sq = sb("sq", [P, 2, C])
        mu = sb("mu", [P, C])
        part = sq
        g_ffn = sb("g_ffn", [P, D])
        ss = sb("ss", [P, CB])
        rstd = sb("rstd", [P, CB])
        g_in = sem("g_in")
        x_in = sem("x_in")
        w_in = [sem(f"w_in{r}") for r in range(WR)]
        proj = sem("proj")
        gated = sem("gated")
        taken = sem("taken")
        centred = sem("centred")
        squared = sem("squared")
        summed = sem("summed")
        var_ready = sem("var_ready")
        root_ready = sem("root_ready")
        inv_ready = sem("inv_ready")
        scaled = sem("scaled")
        silued = sem("silued")
        parted = sem("parted")
        mixed = sem("mixed")
        energy = sem("energy")
        normed = sem("normed")
        chain = sem("chain")
        turned = sem("turned")
        turned_out = sem("turned_out")
        stored = sem("stored")
        block = ctx.enter_context(nc.Block())

        def bank_free(pe, n):
            if n >= BANKS:
                j = JOBS[n - BANKS]
                if j in BY_ACT:
                    pe.wait_ge(gated, BY_ACT.index(j) + 1)
                else:
                    pe.wait_ge(taken, BY_DVE.index(j) + 1)

        def steps(front, side):
            front("mean", 0); side.step(7)
            for d in range(KT):
                front("a", d); side.step(15)
            front("lead", 0); side.step(7 * LEAD)
            for d in range(KT):
                front("c", d); side.step(14 if d + LEAD < KT else 7)
            for d in range(KT):
                front("o", d); side.step(7)
            front("norm", 0); side.step(2)
            for b in range(CB):
                front("turn", b); side.step(1)
            side.finish()

        WEIGHT = total_weight(steps)

        @block.sync
        def _(sp):
            sp.dma_start(g_ffn[:, :], c.dram["g_ffn"].broadcast_to([P, D])).then_inc(g_in, 16)
            for i, j in enumerate(TILES):
                if i >= WR:
                    sp.wait_ge(proj, i - WR + 2)
                if j == ("o", 1):
                    sp.wait_ge(proj, N["yc", KT - 1] + 1)
                    sp.dma_start(x4, c.dram["x"][q * C:(q + 1) * C, :].rearrange("(b p) d -> p b d", p=P)
                                 ).then_inc(x_in, 16)
                sp.dma_start(w[:, i % WR, :], c.dram["w_mix"][i]).then_inc(w_in[i % WR], 16)
            for b in range(CB):
                rows = slice((q * CB + b) * P, (q * CB + b + 1) * P)
                sp.wait_ge(taken, len(BY_DVE))
                sp.dma_start(c.h1_dram[rows, :], h1[:, b, :]).then_inc(stored, 16)
                sp.wait_ge(normed, b + 1)
                sp.dma_start(c.xn_dram[rows, :], x4[:, b, :]).then_inc(stored, 16)
            sp.wait_ge(stored, 2 * CB * 16)

        @block.gpsimd
        def _(pool):
            steps(lambda *_: None, beside("pool", pool, None, WEIGHT))

        @block.tensor
        def _(pe):
            def job(j, products):
                n = N[j]
                bank_free(pe, n)
                if n:
                    pe.wait_ge(w_in[(n - 1) % WR], 16 * ((n - 1) // WR + 1))
                for lhs, rhs, lo, wd, a, b in products:
                    mm = pe.matmul(bank[:, n % BANKS, lo:lo + wd], lhs, rhs, start=a, stop=b)
                mm.then_inc(proj, 1)

            def wt(j, k):
                return w[:, (N[j] - 1) % WR, k * P:(k + 1) * P]

            def full(j, x):
                job(j, [(wt(j, k), x(k), 0, C, k == 0, k == KT - 1) for k in range(KT)])

            tile = lambda a: lambda k: a[:, k * C:(k + 1) * C]

            def front(what, d):
                if what == "mean":
                    job(("mean", 0), [(ones[:, :], tile(acc)(k), 0, C, k == 0, k == KT - 1) for k in range(KT)])
                if what == "a":
                    full(("ga", d), lambda k: aT[:, k, :])
                    full(("ya", d), tile(oT))
                    pe.wait_ge(squared, d + 1)
                    pe.matmul(bank[:, 5, :], ones[:, :], sq[:, d % 2, :], start=(d == 0), stop=(d == KT - 1)).then_inc(summed, 1)
                if what == "lead":
                    for i in range(LEAD):
                        full(("gc", i), lambda k: aT[:, k, :])
                if what == "c":
                    if d == 0:
                        pe.wait_ge(silued, KT)
                    full(("yc", d), tile(acc))
                    if d + LEAD < KT:
                        full(("gc", d + LEAD), lambda k: aT[:, k, :])
                if what == "o":
                    if d == 0:
                        pe.wait_ge(mixed, KT)
                    job(("o", d), [(mixT[:, k, b * P:(b + 1) * P], wt(("o", d), k), b * P, P, k == 0, k == KT - 1)
                                   for b in range(CB) for k in range(KT)])
                if what == "turn":
                    pe.wait_ge(normed, d + 1)
                    for u in range(2):
                        n = 2 * d + u
                        if n < 2:
                            pe.wait_ge(taken, len(BY_DVE))
                        else:
                            pe.wait_ge(turned_out, n - 1)
                        for k in range(4):
                            mm = pe.transpose(bank[:, n % 2, k * P:(k + 1) * P],
                                              x4[:, d, (4 * u + k) * P:(4 * u + k + 1) * P], ident[:, :])
                        mm.then_inc(turned, 1)

            steps(front, beside("tensor", pe, None, WEIGHT))

        @block.scalar
        def _(act):
            def gate(j, g0):
                i = GATES.index(j)
                if i >= SG:
                    old = GATES[i - SG]
                    act.wait_ge(taken, BY_DVE.index(("y" + old[0][1], old[1])) + 1)
                act.wait_ge(proj, N[j] + 1)
                act.activation(sig[:, i % SG, :], bank[:, N[j] % BANKS, :], ACT.Sigmoid,
                               bias=c.gcols[:, g0 + j[1]:g0 + j[1] + 1]).then_inc(gated, 1)

            def front(what, d):
                if what == "a":
                    gate(("ga", d), G_BGATE + KT)
                    act.wait_ge(centred, d + 1)
                    if d >= 2:
                        act.wait_ge(summed, d - 1)
                    act.activation(sq[:, d % 2, :], acc[:, d * C:(d + 1) * C], ACT.Square).then_inc(squared, 1)
                if what == "lead":
                    act.wait_ge(var_ready, 1)
                    act.activation(mu[:, :], mu[:, :], ACT.Sqrt).then_inc(root_ready, 1)
                    for k in range(KT):
                        t = acc[:, k * C:(k + 1) * C]
                        act.wait_ge(scaled, k + 1)
                        act.activation(t, t, ACT.Silu, bias=c.gcols[:, G_LNB + k:G_LNB + k + 1],
                                       scale=c.gcols[:, G_LNG + k:G_LNG + k + 1]).then_inc(silued, 1)
                    for i in range(LEAD):
                        gate(("gc", i), G_BGATE)
                if what == "c" and d + LEAD < KT:
                    gate(("gc", d + LEAD), G_BGATE)
                if what == "norm":
                    for b in range(CB):
                        act.wait_ge(taken, len(BY_DVE))
                        if b:
                            act.wait_ge(energy, b)
                        act.activation(sig[:, 0:2, :].rearrange("p a n -> p (a n)"), h1[:, b, :], ACT.Square,
                                       accum_out=ss[:, b:b + 1]).then_inc(energy, 1)
                    act.wait_ge(var_ready, 2)
                    act.activation(ss[:, :], ss[:, :], ACT.Sqrt).then_inc(root_ready, 1)
                if what == "turn":
                    for u in range(2):
                        n = 2 * d + u
                        act.wait_ge(turned, n + 1)
                        act.activation(aT[:, 4 * u:4 * u + 4, d * P:(d + 1) * P],
                                       bank[:, n % 2, :].rearrange("p (k n) -> p k n", k=4), ACT.Copy).then_inc(turned_out, 1)

            steps(front, beside("scalar", act, None, WEIGHT))

        @block.vector
        def _(dve):
            count = [0]

            def link(ins):
                count[0] += 1
                ins.then_inc(chain, 1)
                dve.wait_ge(chain, count[0])

            def out_of(j):
                dve.wait_ge(proj, N[j] + 1)
                return bank[:, N[j] % BANKS, :]

            def gated_y(dst, j):
                g = ("g" + j[0][1], j[1])
                dve.wait_ge(gated, BY_ACT.index(g) + 1)
                return dve.tensor_tensor(dst, out_of(j), sig[:, GATES.index(g) % SG, :], ALU.mult).then_inc(taken, 1)

            def front(what, d):
                if what == "mean":
                    dve.tensor_scalar(mu[:, :], out_of(("mean", 0)), 1.0 / D, None, ALU.mult).then_inc(taken, 1)
                    dve.wait_ge(taken, 1)
                if what == "a":
                    t = acc[:, d * C:(d + 1) * C]
                    dve.tensor_tensor(t, t, mu[:, :], ALU.subtract).then_inc(centred, 1)
                    gated_y(mixT[:, d, :], ("ya", d))
                if what == "lead":
                    dve.wait_ge(summed, KT)
                    dve.wait_ge(centred, KT)
                    dve.tensor_scalar(mu[:, :], bank[:, 5, :], 1.0 / D, EPS, ALU.mult, ALU.add).then_inc(var_ready, 1)
                    dve.wait_ge(root_ready, 1)
                    link(dve.reciprocal(mu[:, :], mu[:, :]))
                    for k in range(KT):
                        t = acc[:, k * C:(k + 1) * C]
                        dve.tensor_tensor(t, t, mu[:, :], ALU.mult).then_inc(scaled, 1)
                if what == "c":
                    if d >= 2:
                        dve.wait_ge(mixed, d - 1)
                    gated_y(part[:, d % 2, :], ("yc", d))
                    dve.wait_ge(taken, BY_DVE.index(("yc", d)) + 1)
                    dve.tensor_tensor(mixT[:, d, :], mixT[:, d, :], part[:, d % 2, :], ALU.add).then_inc(mixed, 1)
                if what == "o":
                    if d == 0:
                        dve.wait_ge(x_in, 16)
                    cols = slice(d * P, (d + 1) * P)
                    dve.tensor_tensor(h1[:, :, cols], out_of(("o", d)).rearrange("p (b n) -> p b n", b=CB),
                                      x4[:, :, cols], ALU.add).then_inc(taken, 1)
                if what == "norm":
                    dve.wait_ge(energy, CB)
                    dve.tensor_scalar(ss[:, :], ss[:, :], 1.0 / D, EPS, ALU.mult, ALU.add).then_inc(var_ready, 1)
                    dve.wait_ge(root_ready, 2)
                    link(dve.reciprocal(rstd[:, :], ss[:, :]))
                    dve.wait_ge(taken, len(BY_DVE))
                    dve.wait_ge(g_in, 16)
                    for b in range(CB):
                        dve.scalar_tensor_tensor(out=x4[:, b, :], in0=h1[:, b, :], scalar=rstd[:, b:b + 1],
                                                 in1=g_ffn[:, :], op0=ALU.mult, op1=ALU.mult).then_inc(normed, 1)

            steps(front, beside("vector", dve, None, WEIGHT))


def peer_scores(c, q, beside, peer):
    FIRST = q * CB
    nc, bank, xnT = c.nc, c.bank, c.aT
    HS = 2 * PH
    WR = 4
    with ExitStack() as ctx:
        sb, sem = scope(c, ctx, f"q{q}scores_")
        w = sb("w", [P, WR, D])
        keysT = sb("keysT", [P, HS * NK])
        queryT = sb("queryT", [P, 2, C])
        out = sb("out", [P, 2, C])
        k_in = sem("k_in")
        w_in = [sem(f"w_in{r}") for r in range(WR)]
        proj = sem("proj")
        copied = sem("copied")
        scored = sem("scored")
        out_ready = sem("out_ready")
        fed = sem("fed")
        stored = [sem(f"stored{r}") for r in range(2)]
        block = ctx.enter_context(nc.Block())

        def steps(front, side):
            for i in range(HS + 1):
                front(i)
                side.step(8)
            front("end")
            side.finish()

        WEIGHT = total_weight(steps) * 9 // 8

        def store(sp, i):
            sp.wait_ge(out_ready, i + 1)
            dst = c.sc_dram[q * C + P:(q + 1) * C, i * NK:(i + 1) * NK].rearrange("(b p) n -> p b n", p=P)
            sp.dma_start(dst, out[:, i % 2, P:].rearrange("p (b n) -> p b n", b=CB - 1)).then_inc(stored[i % 2], 16)

        @block.sync
        def _(sp):
            for i in range(HS):
                if i >= WR:
                    sp.wait_ge(proj, i - WR + 1)
                sp.dma_start(w[:, i % WR, :], c.dram["w_peer"][i]).then_inc(w_in[i % WR], 16)
                if i == 0:
                    sp.dma_start(keysT[:, :], c.dram["keysT"]).then_inc(k_in, 16)
                if i >= 2:
                    store(sp, i - 2)
            store(sp, HS - 2)
            store(sp, HS - 1)
            for r in range(2):
                sp.wait_ge(stored[r], 16 * (HS // 2))

        @block.gpsimd
        def _(pool):
            if q == 0:
                peer.before("pool", pool)
                pool.iota(peer.iota[:, :], pattern=[[1, TOPK]], base=0, channel_multiplier=0,
                          allow_small_or_imprecise_dtypes=True).then_inc(peer.ready, 1)
            steps(lambda i: None, beside("pool", pool, None, WEIGHT))

        @block.tensor
        def _(pe):
            if q == 0:
                peer.before("tensor", pe)

            def front(i):
                if i == "end":
                    return
                if i < HS:
                    pe.wait_ge(w_in[i % WR], 16 * (i // WR + 1))
                    if i >= 2:
                        pe.wait_ge(copied, i - 1)
                    for k in range(KT):
                        mm = pe.matmul(bank[:, i % 2, :], w[:, i % WR, k * P:(k + 1) * P], xnT[:, k, :],
                                       start=(k == 0), stop=(k == KT - 1))
                    mm.then_inc(proj, 1)
                if i:
                    i -= 1
                    if i == 0:
                        pe.wait_ge(k_in, 16)
                    pe.wait_ge(copied, i + 1)
                    if i >= 2:
                        pe.wait_ge(out_ready, i - 1)
                    for b in range(CB):
                        mm = pe.matmul(bank[:, 2 + i % 2, b * P:(b + 1) * P], queryT[:, i % 2, b * P:(b + 1) * P],
                                       keysT[:, i * NK:(i + 1) * NK], start=True, stop=True)
                    mm.then_inc(scored, 1)

            steps(front, beside("tensor", pe, None, WEIGHT))

        @block.scalar
        def _(act):
            def front(i):
                if i == "end":
                    act.sem_inc(peer.sc_in, 16)
                    peer.route_exp(act, FIRST)
                    return
                if i < HS:
                    act.wait_ge(proj, i + 1)
                    if i >= 2:
                        act.wait_ge(scored, i - 1)
                    act.activation(queryT[:, i % 2, :], bank[:, i % 2, :], ACT.Copy).then_inc(copied, 1)
                if i:
                    i -= 1
                    act.wait_ge(scored, i + 1)
                    act.activation(peer.sc[:, i * NK:(i + 1) * NK], bank[:, 2 + i % 2, 0:P], ACT.Copy).then_inc(fed, 1)
                    if i >= 2:
                        act.wait_ge(stored[i % 2], 16 * (i // 2))
                    act.activation(out[:, i % 2, P:], bank[:, 2 + i % 2, P:], ACT.Copy).then_inc(out_ready, 1)

            if q == 0:
                peer.before("scalar", act)
                act.sem_inc(peer.y_out, 16)
            act.wait_ge(peer.routed, peer.ROUTE * (FIRST + 1))
            steps(front, beside("scalar", act, None, WEIGHT))

        @block.vector
        def _(dve):
            if q == 0:
                peer.before("vector", dve)
                dve.wait_ge(peer.ready, 1)
            routing, done = peer.route(dve, FIRST, fed), [0]

            def route_to(n):
                while done[0] < n:
                    next(routing)
                    done[0] += 1

            def front(i):
                if i == "end":
                    route_to(peer.ROUTE)
                elif i >= 2:
                    route_to(peer.ROUTE_HEAD * PH if i == HS else peer.ROUTE_HEAD // 2 * (i - 1))

            steps(front, beside("vector", dve, None, WEIGHT))


class Peer:

    ROUTE_HEAD = 24
    ROUTE = PH * ROUTE_HEAD + 4
    DIAGS = 6
    SHARE = 4
    V_PICKS = PICKS // SHARE
    PE_PICKS = PICKS - V_PICKS

    def __init__(self, c, ctx):
        sb, sem = scope(c, ctx, "peer_")
        self.c = c
        self.sc = sb("sc", [P, 2 * PH * NK])
        self.next_index = sb("next_index", [P, PICKS], I32)
        self.next_gates = sb("next_gates", [P, PICKS])
        self.best = sb("best", [P, PICKS])
        self.norm = sb("norm", [P, PH])
        self.top = sb("top", [P, 2, TOPK])
        self.top_at = sb("top_at", [P, 2, TOPK], U32)
        self.top_atf = sb("top_atf", [P, 2, TOPK])
        self.rest = sb("rest", [P, 2, NK])
        self.cand = sb("cand", [P, TOPK * TOPK])
        self.cand_rest = sb("cand_rest", [P, TOPK * TOPK])
        self.place = sb("place", [P, TOPK], U32)
        self.digits = sb("digits", [P, 2, TOPK], U32)
        self.digitsf = sb("digitsf", [P, 2, TOPK])
        self.hit = sb("hit", [P, 2 * TOPK * TOPK])
        self.side_at = sb("side_at", [P, 2 * TOPK])
        self.iota = sb("iota", [P, TOPK])
        self.got = [sem(f"got{r}") for r in range(RING)]
        self.xn_in, self.h1_in, self.sc_in, self.y_out = (sem(n) for n in ("xn_in", "h1_in", "sc_in", "y_out"))
        self.dotted = sem("dotted")
        self.gelued = sem("gelued")
        self.diag_ready = sem("diag_ready")
        self.added = sem("added")
        self.gates_set = sem("gates_set")
        self.index_set = sem("index_set")
        self.routed = sem("routed")
        self.exp_done = sem("exp_done")
        self.summed = sem("summed")
        self.ms_ready = sem("ms_ready")
        self.root_ready = sem("root_ready")
        self.inv_ready = sem("inv_ready")
        self.y_ready = sem("y_ready")
        self.carried = sem("carried")
        self.ready = sem("ready")
        self.coef_ready = sem("coef_ready")
        self.added_v = sem("added_v")
        self.vsum_ready = sem("vsum_ready")

    def rows_buffers(self, c, ctx):
        sb = lambda name, shape, dtype=F32: ctx.enter_context(c.nc.sbuf_tensor("peer_" + name, shape, dtype))
        self.ring = sb("ring", [P, RING, 2 * D])
        self.xn = sb("xn", [P, D])
        self.h1 = sb("h1", [P, D])
        self.vsum = sb("vsum", [P, D])
        self.g_final = sb("g_final", [P, D])
        self.diag = sb("diag", [P, self.DIAGS, P])
        self.coef = sb("coef", [P, 2])
        self.dots = sb("dots", [P, PICKS])
        self.gelus = sb("gelus", [P, PICKS])
        self.gates = sb("gates", [P, PICKS])
        self.index = sb("index", [P, PICKS], I32)
        self.ms = sb("ms", [P, 1])
        self.root = sb("root", [P, 1])

    BEFORE = {"tensor": [("added", PE_PICKS)], "scalar": [("gelued", PICKS), ("exp_done", 1), ("root_ready", 1)],
              "vector": [("dotted", PICKS), ("diag_ready", PE_PICKS), ("coef_ready", V_PICKS),
                         ("added_v", V_PICKS), ("vsum_ready", 1), ("gates_set", 1), ("routed", ROUTE), ("summed", 2),
                         ("ms_ready", 2), ("inv_ready", 1), ("y_ready", 1)],
              "pool": [("index_set", PH)]}

    def before(self, name, eng):
        for s_, n in self.BEFORE[name]:
            eng.sem_inc({"added": self.added, "gelued": self.gelued, "exp_done": self.exp_done,
                         "root_ready": self.root_ready, "dotted": self.dotted, "diag_ready": self.diag_ready,
                         "gates_set": self.gates_set, "routed": self.routed, "summed": self.summed,
                         "ms_ready": self.ms_ready, "inv_ready": self.inv_ready, "y_ready": self.y_ready,
                         "index_set": self.index_set, "coef_ready": self.coef_ready, "added_v": self.added_v,
                         "vsum_ready": self.vsum_ready}[s_], n)

    def by_vector(self, n):
        return n % self.SHARE == self.SHARE - 1

    def wait_used(self, eng, b, n):
        if self.by_vector(n):
            eng.wait_ge(self.added_v, self.V_PICKS * (b + 1) + n // self.SHARE + 1)
        else:
            eng.wait_ge(self.added, self.PE_PICKS * (b + 1) + self.pe_place(n) + 1)

    def pe_place(self, n):
        return n - n // self.SHARE

    def route(self, dve, b, fed=None):
        base, n = self.ROUTE * (b + 1), [0]

        def step(ins):
            n[0] += 1
            ins.then_inc(self.routed, 1)

        def after(k=None):
            dve.wait_ge(self.routed, base + (n[0] if k is None else k))

        def carry():
            after()
            dve.sem_inc(self.carried, 1)

        if fed is None:
            dve.wait_ge(self.sc_in, 16 * (b + 1))
        for h in range(PH):
            if fed is not None:
                dve.wait_ge(fed, 2 * h + 2)
            side = [self.sc[:, (2 * h + i) * NK:(2 * h + i + 1) * NK] for i in range(2)]
            for lo in (0, TOPK // 2):
                of = side if lo == 0 else [self.rest[:, i, :] for i in range(2)]
                some = slice(lo, lo + TOPK // 2)
                for i in range(2):
                    carry()
                    step(dve.max(self.top[:, i, some], of[i])); yield
                for i in range(2):
                    carry()
                    step(dve.max_index(self.top_at[:, i, some], self.top[:, i, some], of[i])); yield
                if lo == 0:
                    for i in range(2):
                        carry()
                        step(dve.match_replace(self.rest[:, i, :], self.top[:, i, some], of[i], LOWEST)); yield
            grid = lambda t: t.rearrange("p (i j) -> p i j", i=TOPK)
            after()
            step(dve.tensor_tensor(grid(self.cand[:, :]), self.top[:, 0, :].unsqueeze(2).broadcast_to([P, TOPK, TOPK]),
                                   self.top[:, 1, :].unsqueeze(1).broadcast_to([P, TOPK, TOPK]), ALU.add)); yield
            best = self.best[:, h * TOPK:(h + 1) * TOPK]
            for lo in (0, TOPK // 2):
                some = slice(lo, lo + TOPK // 2)
                of = self.cand if lo == 0 else self.cand_rest
                carry()
                step(dve.max(best[:, some], of[:, :])); yield
                carry()
                step(dve.max_index(self.place[:, some], best[:, some], of[:, :])); yield
                if lo == 0:
                    carry()
                    step(dve.match_replace(self.cand_rest[:, :], best[:, some], of[:, :], LOWEST)); yield
            after()
            step(dve.tensor_single_scalar(self.digits[:, 0, :], self.place[:, :], 4, ALU.logical_shift_right)); yield
            step(dve.tensor_single_scalar(self.digits[:, 1, :], self.place[:, :], TOPK - 1, ALU.bitwise_and)); yield
            after()
            step(dve.tensor_copy(self.digitsf[:, :, :], self.digits[:, :, :])); yield
            step(dve.tensor_copy(self.top_atf[:, :, :], self.top_at[:, :, :])); yield
            hit3 = self.hit[:, :].rearrange("p (k a) -> p k a", a=TOPK)
            hit4 = self.hit[:, :].rearrange("p (s k a) -> p s k a", s=2, a=TOPK)
            after()
            step(dve.tensor_tensor(hit3, self.digitsf[:, :, :].rearrange("p s k -> p (s k)").unsqueeze(2)
                                   .broadcast_to([P, 2 * TOPK, TOPK]),
                                   self.iota[:, :].unsqueeze(1).broadcast_to([P, 2 * TOPK, TOPK]), ALU.is_equal)); yield
            after()
            step(dve.tensor_tensor(hit4, hit4, self.top_atf[:, :, :].unsqueeze(2)
                                   .broadcast_to([P, 2, TOPK, TOPK]), ALU.mult)); yield
            after()
            step(dve.tensor_reduce(self.side_at[:, :], hit3, AX.X, ALU.add)); yield
            after()
            dve.wait_ge(self.index_set, PH * b + h + 1)
            step(dve.scalar_tensor_tensor(out=self.next_index[:, h * TOPK:(h + 1) * TOPK], in0=self.side_at[:, 0:TOPK],
                                          scalar=float(NK), in1=self.side_at[:, TOPK:], op0=ALU.mult, op1=ALU.add)); yield
            assert n[0] == self.ROUTE_HEAD * (h + 1), n
        heads = lambda t: t[:, :].rearrange("p (h k) -> p h k", h=PH)
        after()
        dve.wait_ge(self.gates_set, b + 1)
        step(dve.tensor_tensor(heads(self.next_gates), heads(self.best),
                               heads(self.best)[:, :, 0:1].broadcast_to([P, PH, TOPK]), ALU.subtract)); yield
        dve.wait_ge(self.exp_done, b + 2)
        step(dve.tensor_reduce(self.norm[:, :], heads(self.next_gates), AX.X, ALU.add)); yield
        after()
        step(dve.reciprocal(self.norm[:, :], self.norm[:, :])); yield
        after()
        step(dve.tensor_tensor(heads(self.next_gates), heads(self.next_gates),
                               self.norm[:, :].unsqueeze(2).broadcast_to([P, PH, TOPK]), ALU.mult)); yield
        assert n[0] == self.ROUTE

    def route_exp(self, act, b):
        act.wait_ge(self.routed, self.ROUTE * (b + 1) + self.ROUTE - 3)
        act.activation(self.next_gates[:, :], self.next_gates[:, :], ACT.Exp).then_inc(self.exp_done, 1)

    def load_scores(self, eng, b):
        eng.wait_ge(self.routed, self.ROUTE * (b + 1))
        eng.dma_start(self.sc[:, :], self.rows("sc_dram", b)).then_inc(self.sc_in, 16)

    def rows(self, name, b):
        return {"sc_dram": self.c.sc_dram, "xn_dram": self.c.xn_dram, "h1_dram": self.c.h1_dram,
                "y": self.c.dram["y"]}[name][bass.ds(b * P, P), :]


class PeerBlock:

    AHEAD = {"pool": RING // 2, "tensor": -3, "scalar": 0, "vector": 0}
    ROUTE_FROM = 4
    ROUTE_EXP = PICKS - 2 * RING

    def __init__(self, peer, name, eng, b, route, weight, start=0):
        self.p, self.name, self.eng, self.b, self.route = peer, name, eng, b, route
        self.weight, self.start = weight, start
        self.n = self.passed = self.done = 0
        self.part = {"pool": self.fetch, "tensor": self.add, "scalar": self.gelu, "vector": self.dot}[name]
        self.routing = peer.route(eng, b + 1) if route and name == "vector" else None

    def step(self, weight):
        self.passed += weight
        self.upto(PICKS * (self.passed - self.start) // (self.weight - self.start) + self.AHEAD[self.name])

    def upto(self, n):
        while self.n < min(n, PICKS):
            self.part(self.n)
            self.n += 1

    def finish(self):
        assert self.passed <= self.weight
        self.upto(PICKS)
        if self.name == "vector":
            self.close()
        if self.name == "scalar":
            self.close_root()

    def fetch(self, n):
        p, pool, b, r = self.p, self.eng, self.b, n % RING
        if n % TOPK == 0:
            h = n // TOPK
            cols = slice(n, n + TOPK)
            pool.wait_ge(p.routed, p.ROUTE * (b + 2))
            pool.sem_inc(self.p.c.passed, 1)
            pool.tensor_copy(p.index[:, cols], p.next_index[:, cols]).then_inc(p.index_set, 1)
            pool.wait_ge(p.index_set, PH * (b + 1) + h + 1)
        p.wait_used(pool, b, n - RING)
        pool.sem_inc(self.p.c.passed, 1)
        pool.indirect_dma_start(out=p.ring[:, r, :], out_offset=None, in_=p.c.dram["uv"],
                                in_offset=bass.IndirectOffsetOnAxis(ap=p.index[:, n:n + 1], axis=0)).then_inc(p.got[r], 16)

    def dot(self, n):
        p, dve, b, r = self.p, self.eng, self.b, n % RING
        if n == 0:
            dve.wait_ge(p.routed, p.ROUTE * (b + 2))
            dve.wait_ge(p.diag_ready, p.PE_PICKS * (b + 1))
            dve.wait_ge(p.coef_ready, p.V_PICKS * (b + 1))
            dve.tensor_copy(p.gates[:, :], p.next_gates[:, :]).then_inc(p.gates_set, 1)
            dve.wait_ge(p.xn_in, 16 * (b + 1))
        row = p.ring[:, r, 0:D]
        dve.wait_ge(p.got[r], 16 * (PICKS // RING) * b + 16 * (n // RING + 1))
        dve.tensor_tensor_reduce(row, row, p.xn[:, :], 1.0, 0.0, ALU.mult, ALU.add,
                                 p.dots[:, n:n + 1]).then_inc(p.dotted, 1)
        if n:
            self.weigh(n - 1)
        if self.routing and n >= self.ROUTE_FROM:
            todo = p.ROUTE if n >= self.ROUTE_EXP + 2 else min(
                p.ROUTE - 3, -(-p.ROUTE * (n + 1 - self.ROUTE_FROM) // (self.ROUTE_EXP - self.ROUTE_FROM)))
            while self.done < todo:
                next(self.routing)
                self.done += 1

    def weigh(self, n):
        p, dve, b = self.p, self.eng, self.b
        if n == 0:
            dve.wait_ge(p.gates_set, b + 2)
        dve.wait_ge(p.gelued, PICKS * (b + 1) + n + 1)
        if not p.by_vector(n):
            m = p.pe_place(n)
            dve.wait_ge(p.added, p.PE_PICKS * (b + 1) + m + 1 - p.DIAGS)
            dve.tensor_scalar(p.diag[:, m % p.DIAGS, :], p.c.ident[:, :], p.gelus[:, n:n + 1], p.gates[:, n:n + 1],
                              ALU.mult, ALU.mult).then_inc(p.diag_ready, 1)
            return
        k = n // p.SHARE
        row, coef = p.ring[:, n % RING, D:], p.coef[:, k % 2:k % 2 + 1]
        dve.wait_ge(p.added_v, p.V_PICKS * (b + 1) + k - 1)
        dve.tensor_tensor(coef, p.gelus[:, n:n + 1], p.gates[:, n:n + 1], ALU.mult).then_inc(p.coef_ready, 1)
        dve.wait_ge(p.coef_ready, p.V_PICKS * (b + 1) + k + 1)
        if k == 0:
            dve.wait_ge(p.vsum_ready, b + 1)
            ins = dve.tensor_scalar(p.vsum[:, :], row, coef, None, ALU.mult)
        else:
            dve.wait_ge(p.added_v, p.V_PICKS * (b + 1) + k)
            ins = dve.scalar_tensor_tensor(out=p.vsum[:, :], in0=row, scalar=coef, in1=p.vsum[:, :],
                                           op0=ALU.mult, op1=ALU.add)
        ins.then_inc(p.added_v, 1)

    def close(self):
        p, dve, b = self.p, self.eng, self.b
        self.weigh(PICKS - 1)
        dve.wait_ge(p.h1_in, 16 * (b + 1))
        dve.wait_ge(p.added_v, p.V_PICKS * (b + 2))
        dve.tensor_tensor(p.h1[:, :], p.h1[:, :], p.vsum[:, :], ALU.add).then_inc(p.vsum_ready, 1)
        dve.wait_ge(p.vsum_ready, b + 2)
        dve.wait_ge(p.added, p.PE_PICKS * (b + 2))
        for h in range(2):
            cols = slice(h * C, (h + 1) * C)
            dve.tensor_tensor(p.h1[:, cols], p.h1[:, cols], p.c.bank[:, 6 + h, :], ALU.add).then_inc(p.summed, 1)
        dve.wait_ge(p.summed, 2 * (b + 2))
        squares = p.c.bank[:, 6:8, :].rearrange("p a n -> p (a n)")
        dve.tensor_tensor_reduce(squares, p.h1[:, :], p.h1[:, :], 1.0, 0.0, ALU.mult, ALU.add,
                                 p.ms[:, :]).then_inc(p.ms_ready, 1)
        dve.wait_ge(p.ms_ready, 2 * (b + 1) + 1)
        dve.tensor_scalar(p.ms[:, :], p.ms[:, :], 1.0 / D, EPS, ALU.mult, ALU.add).then_inc(p.ms_ready, 1)
        dve.wait_ge(p.root_ready, b + 2)
        dve.reciprocal(p.root[:, :], p.root[:, :]).then_inc(p.inv_ready, 1)
        dve.wait_ge(p.inv_ready, b + 2)
        dve.scalar_tensor_tensor(out=p.h1[:, :], in0=p.h1[:, :], scalar=p.root[:, 0:1], in1=p.g_final[:, :],
                                 op0=ALU.mult, op1=ALU.mult).then_inc(p.y_ready, 1)

    def gelu(self, n):
        p, act, b = self.p, self.eng, self.b
        if n == 0:
            act.wait_ge(p.dotted, PICKS * (b + 1))
            act.dma_start(p.xn[:, :], p.rows("xn_dram", b)).then_inc(p.xn_in, 16)
            if self.route:
                p.load_scores(act, b + 1)
        if n == 8:
            act.wait_ge(p.y_out, 16 * (b + 1))
            act.dma_start(p.h1[:, :], p.rows("h1_dram", b)).then_inc(p.h1_in, 16)
        if self.route and n == self.ROUTE_EXP:
            p.route_exp(act, b + 1)
        act.wait_ge(p.dotted, PICKS * (b + 1) + n + 1)
        act.activation(p.gelus[:, n:n + 1], p.dots[:, n:n + 1], ACT.Gelu).then_inc(p.gelued, 1)

    def close_root(self):
        p, act, b = self.p, self.eng, self.b
        act.wait_ge(p.ms_ready, 2 * (b + 2))
        act.activation(p.root[:, :], p.ms[:, :], ACT.Sqrt).then_inc(p.root_ready, 1)
        act.wait_ge(p.y_ready, b + 2)
        act.dma_start(p.rows("y", b), p.h1[:, :]).then_inc(p.y_out, 16)

    def add(self, n):
        p, pe, b, r = self.p, self.eng, self.b, n % RING
        if p.by_vector(n):
            return
        m = p.pe_place(n)
        if n == 0:
            pe.wait_ge(p.ms_ready, 2 * b + 1 + 1)
        pe.wait_ge(p.diag_ready, p.PE_PICKS * (b + 1) + m + 1)
        for h in range(2):
            mm = pe.matmul(p.c.bank[:, 6 + h, :], p.diag[:, m % p.DIAGS, :], p.ring[:, r, D + h * C:D + (h + 1) * C],
                           start=(n == 0), stop=(m == p.PE_PICKS - 1))
        mm.then_inc(p.added, 1)


def peer_blocks(c, peer, b0):
    nc, last = c.nc, S // P - 1
    with ExitStack() as ctx:
        block = ctx.enter_context(nc.Block())

        def run(name, eng):
            with eng.Fori(b0, last) as b:
                PeerBlock(peer, name, eng, b, True, 1).finish()
            PeerBlock(peer, name, eng, last, False, 1).finish()

        @block.gpsimd
        def _(pool):
            run("pool", pool)

        @block.tensor
        def _(pe):
            run("tensor", pe)

        @block.scalar
        def _(act):
            run("scalar", act)
            act.wait_ge(peer.y_out, 16 * (last + 2))

        @block.vector
        def _(dve):
            run("vector", dve)


def build(nc, dram, dump=None):
    c = Chip()
    c.nc, c.dram = nc, dram
    with ExitStack() as ctx:
        sb = lambda n, s, d=F32: ctx.enter_context(nc.sbuf_tensor(n, s, d))
        c.bank = ctx.enter_context(nc.psum_tensor("bank", [P, 8, C], F32))
        c.passed = ctx.enter_context(nc.semaphore("passed"))
        scratch = lambda n, s: nc.dram_tensor(n, s, F32, kind="Internal").ap()
        c.h1_dram = scratch("h1_dram", [S, D])
        c.xn_dram = scratch("xn_dram", [S, D])
        c.sc_dram = scratch("sc_dram", [S, 2 * PH * NK])
        c.ident = sb("ident", [P, P])
        c.ones = sb("ones", [P, P])
        c.gcols = sb("gcols", [P, G_COLS])
        c.mask = sb("mask", [P, P])
        c.wdw = sb("wdw", [P, KT * (TAPS + 1)])
        c.tails = sb("tails", [P, KT * PAD])
        c.ckvT = sb("ckvT", [P, S])
        c.krT = sb("krT", [P, S])
        with ExitStack() as rest:
            peer = Peer(c, rest)
            front(c, 0, peer, dump)
            peer.rows_buffers(c, rest)
            front(c, 1, peer, dump)
            peer_blocks(c, peer, CB)


def front(c, q, peer, dump):
    nc = c.nc

    def beside(b, route):
        if q == 0:
            return lambda *_: Alone()
        return lambda name, eng, t, weight: PeerBlock(peer, name, eng, b if t is None else t + b, route, weight,
                                                      weight // 16 if t is None else 0)

    with ExitStack() as ctx:
        sb = lambda n, s, d=F32: ctx.enter_context(nc.sbuf_tensor(f"q{q}_{n}", s, d))
        c.aT = sb("aT", [P, KT, C])
        c.oT = sb("oT", [P, HEADS * C])
        c.acc = sb("acc", [P, KT * C])
        with ExitStack() as ctx2:
            sb = lambda n, s, d=F32: ctx2.enter_context(nc.sbuf_tensor(f"q{q}_{n}", s, d))
            c.cqT = sb("cqT", [P, QT, C])
            c.cosT = sb("cosT", [P, C])
            c.sinT = sb("sinT", [P, C])
            mixer_inputs(c, q, peer)
            mixers(c, q, beside(0, True))
        if dump: dump(c, (q, 1))
        mix(c, q, beside(2, True))
        peer_scores(c, q, beside(3, False), peer)


def lay_out(i):
    tile = lambda w: w.reshape(w.shape[0] // P, P, -1).transpose(1, 0, 2)
    cols = lambda v: v.reshape(-1, P).T
    w_in, r = i["w_in"][0], np.arange(ROPE)
    swap = (r + ROPE // 2) % ROPE
    o_gate, o_q, o_kv = D, 2 * D, 2 * D + QL
    o_kr = o_kv + P
    o_mix = o_kr + ROPE
    kr = np.concatenate([r, r])
    pick = lambda cs: tile(w_in[:, cs]).reshape(P, -1)
    at = lambda o: np.arange(o, o + P)
    w_uq = tile(i["w_uq"][0]).reshape(P, QT, HEADS, NOPE + ROPE)
    w_ukv = i["w_ukv"][0].reshape(P, HEADS, NOPE + VDIM)
    by_tile = lambda w: np.stack([tile(w[:, o:o + P]).reshape(P, -1) for o in range(0, w.shape[1], P)])
    ga, gc = by_tile(w_in[:, o_mix + D:]), by_tile(w_in[:, o_mix:o_mix + D])
    ya, yc, yo = by_tile(i["w_attn_out"][0]), by_tile(i["w_conv_out"][0]), by_tile(i["w_o"][0])
    lead = 3
    w_mix = [t for d in range(KT) for t in (ga[d], ya[d])] + [gc[d] for d in range(lead)]
    for d in range(KT):
        w_mix += [yc[d]] + ([gc[d + lead]] if d + lead < KT else [])
    w_mix = np.stack(w_mix + list(yo))
    half = ROPE // 2
    freq = np.float32(ROPE_BASE) ** (-np.arange(half, dtype=np.float32) / np.float32(half))
    sign = np.repeat(np.array([-1, 1, -1, 1], np.float32), half)
    return {
        "x": i["x"][0],
        "xT": i["x"][0].T.reshape(KT, P, S),
        "pos": i["positions"],
        "rope": np.stack([np.tile(freq, 4), sign], 1).astype(np.float32),
        "gcols": np.concatenate([cols(i[n][0]) for n in ("mix_norm_g", "q_norm_g", "kv_norm_g", "conv_ln_g",
                                                          "conv_ln_b", "b_gate")], 1),
        "wdw": np.concatenate([i["w_dw"][0, :, 0], i["b_dw"]], 0).reshape(TAPS + 1, KT, P)
                 .transpose(2, 1, 0).reshape(P, -1),
        "w_pre": np.stack([pick(at(o_q)), pick(at(o_q + P)), pick(at(o_kv)), pick(o_kr + kr),
                           pick(o_kr + swap[kr])]),
        "w_vg": np.stack([pick(at(o + h * P)) for h in range(KT) for o in (o_gate, 0)]),
        "w_head": np.stack([np.concatenate([w_uq[:, :, h, :NOPE].reshape(P, -1), w_ukv[:, h, :NOPE],
                                            w_ukv[:, h, NOPE:]], 1) for h in range(HEADS)]),
        "w_rope": np.stack([np.concatenate([w_uq[:, :, h:h + 2, NOPE + rs].reshape(P, -1) for rs in (r, swap)], 1)
                            for h in range(0, HEADS, 2)]),
        "w_mix": w_mix,
        "g_ffn": i["ffn_norm_g"],
        "w_peer": by_tile(i["w_peer_q"][0]),
        "keysT": i["peer_sub_keys"][0].transpose(3, 0, 1, 2).reshape(P, -1),
        "uv": np.concatenate([i["peer_u"][0], i["peer_v"][0]], 1),
        "g_final": i["final_norm_g"][None],
    }


def kernel(**inputs):
    import concourse.bacc as bacc
    from concourse.bass_utils import run_bass_kernel_spmd

    nc = bacc.Bacc("TRN2", target_bir_lowering=False, num_devices=1)
    arrays, dram = {}, {}
    for name, a in lay_out({k: np.asarray(v) for k, v in inputs.items()}).items():
        arrays["in_" + name] = np.ascontiguousarray(a)
        dram[name] = nc.dram_tensor("in_" + name, a.shape, mybir.dt.from_np(a.dtype), kind="ExternalInput").ap()
    dram["y"] = nc.dram_tensor("out_y", (S, D), F32, kind="ExternalOutput").ap()
    build(nc, dram)
    return run_bass_kernel_spmd(nc, [arrays], core_ids=[0]).results[0]["out_y"].reshape(1, S, D)
```

```python
from contextlib import ExitStack

import concourse.bass as bass
import numpy as np
from concourse import mybir

F32 = mybir.dt.float32
I32 = mybir.dt.int32
U32 = mybir.dt.uint32
F32R = mybir.dt.float32r
ALU = mybir.AluOpType
ACT = mybir.ActivationFunctionType
AX = mybir.AxisListType

P = 128
D = 1024
S = 1024
KT = D // P
C = 512
NCH = S // C
CB = C // P
EPS = 1e-6
TAPS = 31
PAD = TAPS - 1
PE_TAPS = (6, 4)
HEADS = 8
SUBS = 4
NOPE, ROPE, VDIM = 128, 64, 128
QL = 256
QT = QL // P
SCALE = float(1.0 / np.sqrt(NOPE + ROPE))
MASKED = -1e30
ROPE_BASE = 10000.0
PH = 8
NK = 128
TOPK = 16
PICKS = PH * TOPK
RING = 8
PRE = 5
LOWEST = -3e38
HR = 3

G_MIX, G_Q, G_KV = 0, KT, KT + QT
G_LNG = G_KV + 1
G_LNB = G_LNG + KT
G_BGATE = G_LNB + KT
G_COLS = G_BGATE + 2 * KT


class Chip:
    pass


def item(a):
    return a.rearrange("a p n -> (a p) n")


def parts(x, both, *at):
    return x if both is None else tuple(both[(slice(None), i) + at] for i in range(2))


def lo_of(eng, x, split):
    hi, lo = split
    return eng.tensor_tensor(lo, x, hi.bitcast(F32), ALU.subtract)


def product(pe, out, left, right, first, last):
    if not isinstance(left, tuple):
        return pe.matmul(out, left, right, start=first, stop=last)
    passes = [(left[0], right[0]), (left[0], right[1]), (left[1], right[0])]
    for n, (a, b) in enumerate(passes):
        mm = pe.matmul(out, a, b, start=first and n == 0, stop=last and n == len(passes) - 1)
    return mm


class Alone:

    def step(self, weight):
        pass

    def finish(self):
        pass


def total_weight(steps):
    passed = []
    counter = Alone()
    counter.step = passed.append
    steps(lambda *_: None, counter)
    return sum(passed)


def scope(c, ctx, prefix):
    nc, sems = c.nc, []

    def clear():
        nc.clear_and_free_semaphores(sems)
        nc.all_engine_barrier()

    def sem(name):
        sems.append(nc.alloc_semaphore(name=prefix + name))
        return sems[-1]

    ctx.callback(clear)
    return (lambda name, shape, dtype=F32: ctx.enter_context(nc.sbuf_tensor(prefix + name, shape, dtype))), sem


def mixer_inputs(c, q, peer):
    nc, bank, ident, ones = c.nc, c.bank, c.ident, c.ones
    aT, cqT, ckvT, krT, cosT, sinT = c.aT, c.cqT, c.ckvT, c.krT, c.cosT, c.sinT
    own = slice(q * C, (q + 1) * C)
    TWO_PI = 2 * np.pi
    C1 = 6.28125
    C2 = float(np.floor((TWO_PI - C1) * 2 ** 20) / 2 ** 20)
    C3 = float(np.float32(TWO_PI - C1 - C2))
    MAGIC = float(1.5 * 2 ** 23)
    with ExitStack() as ctx:
        sb, sem = scope(c, ctx, f"q{q}inputs_")
        wpre = sb("wpre", [P, PRE, D])
        sq = sb("sq", [P, 2, C])
        rs = sb("rs", [P, 2, C])
        posi = sb("posi", [P, C], I32)
        ang = sb("ang", [P, C])
        turns = sb("turns", [P, C])
        red = sb("red", [P, 2, C])
        rope_c = sb("rope_c", [P, 2])
        x_in = [sem(f"x_in{i}") for i in range(KT)]
        w_in = [sem(f"wpre_in{i}") for i in range(PRE)]
        small_in = sem(f"small_in")
        cst = sem(f"cst")
        squared = sem(f"squared")
        summed = sem(f"summed")
        mean_ready = sem(f"mean_ready")
        root_ready = sem(f"root_ready")
        rs_ready = sem(f"rs_ready")
        a_ready = sem(f"a_ready")
        proj = sem(f"proj")
        copied = sem(f"copied")
        roped = sem(f"roped")
        normed = sem(f"normed")
        chain = sem(f"chain")
        angles = sem(f"angles")
        tables = sem(f"tables")
        block = ctx.enter_context(nc.Block())
        N_CQ, N_CKV = QT, 1

        @block.sync
        def _(sp):
            for k in range(KT):
                sp.dma_start(aT[:, k, :], c.dram["xT"][k, :, own]).then_inc(x_in[k], 16)
            for i in range(PRE):
                sp.dma_start(wpre[:, i, :], c.dram["w_pre"][i]).then_inc(w_in[i], 16)

        @block.gpsimd
        def _(pool):
            if q:
                return
            pool.memset(ident[:, :], 0.0).then_inc(cst, 1)
            pool.memset(c.mask[:, :], 0.0).then_inc(cst, 1)
            pool.memset(ones[:, :], 1.0).then_inc(cst, 1)
            pool.wait_ge(cst, 3)
            pool.affine_select(out=ident[:, :], in_=ident[:, :], compare_op=ALU.not_equal, fill=1.0,
                               base=0, pattern=[[-1, P]], channel_multiplier=1).then_inc(cst, 1)
            pool.affine_select(out=c.mask[:, :], in_=c.mask[:, :], compare_op=ALU.is_ge, fill=MASKED,
                               base=0, pattern=[[-1, P]], channel_multiplier=1).then_inc(cst, 1)

        groups = [KT, N_CQ, N_CKV]
        width = [D, QL, P]
        SUM_BANK = [0, 6, 7]

        @block.scalar
        def _(act):
            act.dma_start(rope_c[:, :], c.dram["rope"]).then_inc(small_in, 16)
            act.dma_start(posi[:, :], c.dram["pos"][:, own].broadcast_to([P, C])).then_inc(small_in, 16)
            if q == 0:
                act.dma_start(c.gcols[:, :], c.dram["gcols"]).then_inc(small_in, 16)
                act.dma_start(c.wdw[:, :], c.dram["wdw"]).then_inc(small_in, 16)
            else:
                act.dma_start(peer.g_final[:, :], c.dram["g_final"].broadcast_to([P, D])).then_inc(small_in, 16)

            def squares(g, tile, ready):
                first = sum(groups[:g])
                for k in range(groups[g]):
                    n = first + k
                    ready(k)
                    if n >= 2:
                        act.wait_ge(summed, n - 1)
                    act.activation(sq[:, n % 2, :], tile(k), ACT.Square).then_inc(squared, 1)

            def root(g):
                act.wait_ge(mean_ready, g + 1)
                act.activation(rs[:, g % 2, :], rs[:, g % 2, :], ACT.Sqrt).then_inc(root_ready, 1)

            squares(0, lambda k: aT[:, k, :], lambda k: act.wait_ge(x_in[k], 16))
            root(0)
            act.wait_ge(angles, 2)
            act.activation(cosT[:, :], red[:, 0, :], ACT.Sin).then_inc(tables, 1)
            act.activation(sinT[:, :], red[:, 1, :], ACT.Sin, scale=rope_c[:, 1:2]).then_inc(tables, 1)
            for n in range(N_CQ + N_CKV):
                act.wait_ge(proj, n + 1)
                act.activation(cqT[:, n, :] if n < N_CQ else ckvT[:, own], bank[:, 1 + n, :],
                               ACT.Copy).then_inc(copied, 1)
            squares(1, lambda k: cqT[:, k, :], lambda k: act.wait_ge(copied, k + 1))
            squares(2, lambda k: ckvT[:, own], lambda k: act.wait_ge(copied, N_CQ + 1))
            root(1)
            root(2)

        @block.tensor
        def _(pe):
            if q == 0:
                pe.wait_ge(cst, 5)

            def sums(g):
                first = sum(groups[:g])
                for k in range(groups[g]):
                    pe.wait_ge(squared, first + k + 1)
                    pe.matmul(bank[:, SUM_BANK[g], :], ones[:, :], sq[:, (first + k) % 2, :],
                              start=(k == 0), stop=(k == groups[g] - 1)).then_inc(summed, 1)

            sums(0)
            pe.wait_ge(a_ready, KT)
            for n in range(PRE):
                pe.wait_ge(w_in[n], 16)
                for k in range(KT):
                    mm = pe.matmul(bank[:, 1 + n, :], wpre[:, n, k * P:(k + 1) * P], aT[:, k, :],
                                   start=(k == 0), stop=(k == KT - 1))
                mm.then_inc(proj, 1)
            sums(1)
            sums(2)

        @block.vector
        def _(dve):
            count = [0]

            def link(ins):
                count[0] += 1
                ins.then_inc(chain, 1)
                dve.wait_ge(chain, count[0])

            def mean(g):
                dve.wait_ge(summed, sum(groups[:g + 1]))
                if g == 2:
                    dve.wait_ge(a_ready, KT)
                dve.tensor_scalar(rs[:, g % 2, :], bank[:, SUM_BANK[g], :], 1.0 / width[g], EPS,
                                  ALU.mult, ALU.add).then_inc(mean_ready, 1)

            def inverse(g):
                dve.wait_ge(root_ready, g + 1)
                dve.reciprocal(rs[:, g % 2, :], rs[:, g % 2, :]).then_inc(rs_ready, 1)
                dve.wait_ge(rs_ready, g + 1)

            dve.wait_ge(small_in, 48 if q else 64)
            link(dve.tensor_copy(ang[:, :], posi[:, :]))
            link(dve.tensor_scalar(ang[:, :], ang[:, :], rope_c[:, 0:1], None, ALU.mult))
            for i, quarter in enumerate((0.25, 0.0)):
                link(dve.tensor_scalar(turns[:, :], ang[:, :], 1.0 / TWO_PI, quarter, ALU.mult, ALU.add))
                link(dve.tensor_scalar(turns[:, :], turns[:, :], MAGIC, None, ALU.add))
                link(dve.tensor_scalar(turns[:, :], turns[:, :], -MAGIC, None, ALU.add))
                src = ang[:, :]
                for part in (C1, C2, C3):
                    link(dve.scalar_tensor_tensor(out=red[:, i, :], in0=turns[:, :], scalar=-part, in1=src,
                                                  op0=ALU.mult, op1=ALU.add))
                    src = red[:, i, :]
                link(dve.tensor_scalar(src, src, quarter * TWO_PI, float(np.float32(3.1415925)), ALU.add, ALU.min))
                dve.tensor_scalar(src, src, float(np.float32(-3.1415925)), None, ALU.max).then_inc(angles, 1)
            mean(0)
            inverse(0)
            for k in range(KT):
                dve.scalar_tensor_tensor(out=aT[:, k, :], in0=aT[:, k, :], scalar=c.gcols[:, k:k + 1],
                                         in1=rs[:, 0, :], op0=ALU.mult, op1=ALU.mult).then_inc(a_ready, 1)
            dve.wait_ge(tables, 2)
            dve.wait_ge(proj, PRE - 1)
            link(dve.tensor_tensor(krT[:, own], bank[:, PRE - 1, :], cosT[:, :], ALU.mult))
            dve.wait_ge(proj, PRE)
            link(dve.tensor_tensor(turns[:, :], bank[:, PRE, :], sinT[:, :], ALU.mult))
            dve.tensor_tensor(krT[:, own], krT[:, own], turns[:, :], ALU.add).then_inc(roped, 1)
            mean(1)
            mean(2)
            inverse(1)
            for k in range(N_CQ):
                dve.scalar_tensor_tensor(out=cqT[:, k, :], in0=cqT[:, k, :], scalar=c.gcols[:, KT + k:KT + k + 1],
                                         in1=rs[:, 1, :], op0=ALU.mult, op1=ALU.mult).then_inc(normed, 1)
            inverse(2)
            dve.scalar_tensor_tensor(out=ckvT[:, own], in0=ckvT[:, own], scalar=c.gcols[:, KT + QT:KT + QT + 1],
                                     in1=rs[:, 0, :], op0=ALU.mult, op1=ALU.mult).then_inc(normed, 1)
            dve.wait_ge(normed, N_CQ + 1)
            dve.wait_ge(roped, 1)


class Events:

    def __init__(self, names):
        self.names = list(names)
        self.n = len(self.names)
        self.place = {name: k + 1 for k, name in enumerate(self.names)}

    def value(self, t, *name):
        return (t + 1) * self.n + self.place[name]

    def before(self, t, back, *name):
        return (t + 1) * self.n + self.place[name] - back


def mixers(c, q, beside):
    nc, bank, ident = c.nc, c.bank, c.ident
    aT, cqT, ckvT, krT, cosT, sinT, oT, acc = c.aT, c.cqT, c.ckvT, c.krT, c.cosT, c.sinT, c.oT, c.acc
    NPE = PE_TAPS[q]
    V_TAPS = TAPS - NPE
    EARLY_TAPS, STEP_TAPS = ((0, 0), (2, 1))[q]
    QUADS = q + 1
    SLOTS = NCH - q
    SUB, QB, KEYS = range(SUBS), range(CB), range(QUADS)
    quads = lambda j: range(QUADS)
    width = lambda j: (CB * q + j + 1) * P
    last_of = lambda p, j, back: (p, j - back) if j >= back else ((p - 1) % SUBS, CB + j - back)
    when = lambda t, p, j, back: t if j >= back or p else t - 1

    JOBS = [(p, name, h) for p in SUB for name in ["gate", "val", "q"] + ["qr", "qs"] * (p % 2 == 0) + ["conv", "k", "v"]
            for h in (KEYS if name in "kv" else range(1))]
    BY_DVE = ("val", "qr", "qs", "conv")
    proj_e = Events(JOBS)
    copied_e = Events(j for j in JOBS if j[1] not in BY_DVE)
    taken_e = Events(j for j in JOBS if j[1] in BY_DVE)
    blocks_e = Events((p, j) for p in SUB for j in QB)
    groups_e = Events((p, j, g) for p in SUB for j in QB for g in quads(j))
    subs_e = Events((p,) for p in SUB)
    taps_e = Events((p, k) for p in SUB for k in range(V_TAPS))
    roped_e = Events((p,) for p in SUB if p % 2 == 0)
    assert proj_e.n % 2 == 0 and groups_e.n % 2 == 0
    STEPS = {"gate": 4, "gate2": 4, "val": 4, "val2": 4, "q": 3, "conv": NPE, "kv": 2 * QUADS, "first": 2 * QUADS, 
             "turn": 2 + QUADS, "attend": QUADS, "tail": 1}
    PER_BLOCK = ("turn", "attend", "tail")
    WEIGHT = SUBS * sum(w * (CB if name in PER_BLOCK else 1) for name, w in STEPS.items())

    with ExitStack() as ctx:
        sb, sem = scope(c, ctx, f"q{q}mixers_")
        w_vg = sb("w_vg", [P, 2, D])
        w_head = sb("w_head", [P, QT * P + 2 * P])
        w_rope = sb("w_rope", [P, 2, QT * P])
        hT = sb("hT", [P, PAD + C])
        w_tap = sb("w_tap", [P, 2, TAPS + 1])
        tap_diag = sb("tap_diag", [P, NPE, P])
        sig = sb("sig", [P, C])
        qT = sb("qT", [P, C])
        kT = sb("kT", [P, QUADS * C])
        V = sb("V", [P, QUADS * C])
        qrT = sb("qrT", [P, C])
        swapped = sig
        prob = sb("prob", [P, SLOTS, QUADS * C])
        probT = sb("probT", [P, 2, C])
        peak = sb("peak", [P, 2])
        low = sb("low", [P, 2])
        total = sb("total", [P, 2])
        inv = sb("inv", [P, 2])
        inv_diag = sb("inv_diag", [P, 2, P])

        w_vg_in = [sem(f"w_vg_in{i}") for i in range(2)]
        w_head_in = sem("w_head_in")
        w_rope_in = sem("w_rope_in")
        proj = sem("proj")
        copied = sem("copied")
        taken = sem("taken")
        roped = sem("roped")
        padded = sem("padded")
        tap_cols = sem("tap_cols")
        tap_mats = sem("tap_mats")
        scored = sem("scored")
        maxed = sem("maxed")
        peaked = sem("peaked")
        exped = sem("exped")
        inverted = sem("inverted")
        inv_ready = sem("inv_ready")
        turned = sem("turned")
        turned_out = sem("turned_out")
        used = sem("used")
        oT_out = sem("oT_out")
        tapped = sem("tapped")
        block = ctx.enter_context(nc.Block())
        tile = lambda t, p: bass.ds((SUBS * t + p) * C, C)
        score_banks = lambda j: bank[:, 2 + j % SLOTS:2 + j % SLOTS + QUADS, :].rearrange("p a n -> p (a n)")

        @block.sync
        def _(sp):
            with sp.Fori(0, HEADS // SUBS) as t:
                for p in SUB:
                    old = (p - 1) % SUBS
                    ago = t if p else t - 1
                    for i, name in enumerate(("gate", "val")):
                        sp.wait_ge(proj, proj_e.value(ago, old, name, 0))
                        sp.dma_start(w_vg[:, i, :], item(c.dram["w_vg"][bass.ds(2 * SUBS * t + 2 * p + i, 1)])
                                     ).then_inc(w_vg_in[i], 16)
                    sp.wait_ge(proj, proj_e.value(ago, old, "v", q))
                    sp.dma_start(w_head[:, :], item(c.dram["w_head"][bass.ds(SUBS * t + p, 1)])
                                 ).then_inc(w_head_in, 16)
                    if p % 2 == 0:
                        sp.wait_ge(proj, proj_e.value(t if p else t - 1, (p - 2) % SUBS, "qs", 0))
                        sp.dma_start(w_rope[:, :, :].rearrange("p a n -> p (a n)"),
                                     item(c.dram["w_rope"][bass.ds(SUBS // 2 * t + p // 2, 1)])).then_inc(w_rope_in, 16)

        filled = lambda t, p: 16 * (SUBS * t + p + 1)

        @block.gpsimd
        def _(pool):
            pool.sem_inc(tap_cols, subs_e.n)
            pool.sem_inc(tap_mats, subs_e.n)
            with pool.Fori(0, HEADS // SUBS) as t:
                side = beside("pool", pool, t, WEIGHT)
                for p in SUB:
                    pool.wait_ge(tapped, taps_e.value(t if p >= 2 else t - 1, (p - 2) % SUBS, V_TAPS - 1))
                    pool.sem_inc(c.passed, 1)
                    pool.tensor_copy(w_tap[:, p % 2, :], c.wdw[:, bass.ds((SUBS * t + p) * (TAPS + 1), TAPS + 1)]
                                     ).then_inc(tap_cols, 1)
                    pool.wait_ge(tap_cols, subs_e.value(t, p))
                    pool.wait_ge(proj, proj_e.value(t if p else t - 1, (p - 1) % SUBS, "conv", 0))
                    pool.sem_inc(c.passed, 1)
                    for k in range(NPE):
                        ins = pool.tensor_scalar(tap_diag[:, k, :], ident[:, :], w_tap[:, p % 2, k:k + 1], None, ALU.mult)
                    ins.then_inc(tap_mats, 1)
                    for name, w in STEPS.items():
                        if name not in PER_BLOCK:
                            side.step(w)
                    for _ in QB:
                        for name in PER_BLOCK:
                            side.step(STEPS[name])
                side.finish()

        @block.tensor
        def _(pe):
            for s_, e in ((proj, proj_e), (scored, blocks_e), (turned, groups_e), (used, groups_e)):
                pe.sem_inc(s_, e.n)
            with pe.Fori(0, HEADS // SUBS) as t:
                side = beside("tensor", pe, t, WEIGHT)

                def job(p, name, h, products, halfway=None):
                    n = proj_e.place[p, name, h] - 1
                    last = JOBS[n - 2]
                    ev, s_ = (taken_e, taken) if last[1] in BY_DVE else (copied_e, copied)
                    pe.wait_ge(s_, ev.value(t if n >= 2 else t - 1, *last))
                    for i, (lhs, rhs, lo, w, a, b) in enumerate(products):
                        if halfway and 2 * i == len(products):
                            halfway()
                        mm = pe.matmul(bank[:, n % 2, lo:lo + w], lhs, rhs, start=a, stop=b)
                    mm.then_inc(proj, 1)

                def full(w, x, k_tiles):
                    return [(w(k), x(k), 0, C, k == 0, k == k_tiles - 1) for k in range(k_tiles)]

                def scores(p, j):
                    h64 = slice(64 * (p % 2), 64 * (p % 2) + 64)
                    if j == 0:
                        pe.wait_ge(copied, copied_e.value(t, p, "k", q))
                        if p % 2 == 0:
                            pe.wait_ge(roped, roped_e.value(t, p))
                    pe.wait_ge(exped, blocks_e.before(t, SLOTS, p, j))
                    qs = slice(j * P, (j + 1) * P)
                    for h in KEYS:
                        w = min(width(j) - h * C, C)
                        ks = slice(h * C, h * C + w)
                        out = bank[:, 2 + j % SLOTS + h, :]
                        diag = h == q
                        pe.matmul(out[:, 0:w], qT[:, qs], kT[:, ks], start=True, stop=False)
                        mm = pe.matmul(out[:, 0:w], qrT[h64, qs], krT[h64, ks], start=False, stop=not diag)
                        if diag:
                            mm = pe.matmul(out[:, w - P:w], ident[:, :], c.mask[:, :], start=False, stop=True)
                    mm.then_inc(scored, 1)

                def turn(p, j, g):
                    if g == 0:
                        pe.wait_ge(inv_ready, blocks_e.value(t, p, j))
                    pe.wait_ge(turned_out, groups_e.before(t, 1, p, j, g))
                    for b in range(min(CB * q + j + 1 - 4 * g, 4)):
                        kb = 4 * g + b
                        mm = pe.matmul(bank[:, 4, b * P:(b + 1) * P], prob[:, j % SLOTS, kb * P:(kb + 1) * P],
                                       inv_diag[:, j % 2, :], start=True, stop=True)
                    mm.then_inc(turned, 1)

                def attend(p, j, g):
                    if j == 0 and g == 0:
                        pe.wait_ge(copied, copied_e.value(t, p, "v", q))
                        pe.wait_ge(oT_out, subs_e.before(t, 1, p))
                    pe.wait_ge(turned_out, groups_e.value(t, p, j, g))
                    n = groups_e.place[p, j, g] - 1
                    own = CB * q + j
                    for kb in range(4 * g, min(own + 1, 4 * g + 4)):
                        mm = pe.matmul(bank[:, 5, j * P:(j + 1) * P], V[:, kb * P:(kb + 1) * P],
                                       probT[:, n % 2, (kb % 4) * P:(kb % 4 + 1) * P], start=(kb == 0), stop=(kb == own))
                    mm.then_inc(used, 1)

                for p in SUB:
                    for i, name in enumerate(("gate", "val")):
                        pe.wait_ge(w_vg_in[i], filled(t, p))
                        job(p, name, 0, full(lambda k: w_vg[:, i, k * P:(k + 1) * P], lambda k: aT[:, k, :], KT),
                            lambda: side.step(STEPS[name]))
                        side.step(STEPS[name + "2"])
                    pe.wait_ge(w_head_in, filled(t, p))
                    job(p, "q", 0, full(lambda k: w_head[:, k * P:(k + 1) * P], lambda k: cqT[:, k, :], QT))
                    if p % 2 == 0:
                        pe.wait_ge(w_rope_in, 16 * (SUBS // 2 * t + p // 2 + 1))
                        for i, name in enumerate(("qr", "qs")):
                            job(p, name, 0, full(lambda k: w_rope[:, i, k * P:(k + 1) * P], lambda k: cqT[:, k, :], QT))
                    side.step(STEPS["q"])
                    pe.wait_ge(padded, subs_e.value(t, p))
                    pe.wait_ge(taken, taken_e.value(t, p, "val", 0))
                    pe.wait_ge(tap_mats, subs_e.value(t, p))
                    job(p, "conv", 0, [(tap_diag[:, k, :], hT[:, k:k + C], 0, C, k == 0, k == NPE - 1)
                                       for k in range(NPE)])
                    side.step(STEPS["conv"])
                    for h in KEYS:
                        job(p, "k", h, full(lambda k: w_head[:, QT * P:(QT + 1) * P],
                                            lambda k: ckvT[:, h * C:(h + 1) * C], 1))
                    for h in KEYS:
                        job(p, "v", h, [(ckvT[:, (4 * h + b) * P:(4 * h + b + 1) * P], w_head[:, (QT + 1) * P:],
                                         b * P, P, True, True) for b in range(4)])
                    side.step(STEPS["kv"])
                    for j in range(SLOTS):
                        scores(p, j)
                    side.step(STEPS["first"])
                    for j in QB:
                        turn(p, j, 0)
                        if j + SLOTS < CB and SLOTS > 1:
                            scores(p, j + SLOTS)
                        for g in quads(j)[1:]:
                            turn(p, j, g)
                        if j + SLOTS < CB and SLOTS == 1:
                            scores(p, j + SLOTS)
                        side.step(STEPS["turn"])
                        for g in quads(j):
                            attend(p, j, g)
                        side.step(STEPS["attend"])
                        side.step(STEPS["tail"])
                side.finish()

        @block.scalar
        def _(act):
            for s_, e in ((copied, copied_e), (exped, blocks_e), (turned_out, groups_e), (oT_out, subs_e)):
                act.sem_inc(s_, e.n)
            with act.Fori(0, HEADS // SUBS) as t:
                side = beside("scalar", act, t, WEIGHT)

                def take(p, name, h=0):
                    n = proj_e.place[p, name, h] - 1
                    act.wait_ge(proj, proj_e.value(t, p, name, h))
                    if name == "gate":
                        if p % 2:
                            act.wait_ge(roped, roped_e.value(t, p - 1))
                        else:
                            act.wait_ge(taken, taken_e.value(t if p else t - 1, (p - 1) % SUBS, "val", 0))
                        dst, func = sig[:, :], ACT.Sigmoid
                    else:
                        dst, func = {"q": qT, "k": kT, "v": V}[name][:, h * C:(h + 1) * C], ACT.Copy
                    act.activation(dst, bank[:, n % 2, :], func).then_inc(copied, 1)

                def exps(p, j):
                    act.wait_ge(peaked, blocks_e.value(t, p, j))
                    act.wait_ge(turned, groups_e.value(when(t, p, j, SLOTS), *last_of(p, j, SLOTS), q))
                    act.activation(prob[:, j % SLOTS, 0:width(j)], score_banks(j)[:, 0:width(j)], ACT.Exp,
                                   bias=low[:, j % 2:j % 2 + 1], scale=SCALE,
                                   accum_out=total[:, j % 2:j % 2 + 1]).then_inc(exped, 1)

                def turned_copy(p, j, g):
                    n = groups_e.place[p, j, g] - 1
                    w = min(width(j) - 4 * g * P, C)
                    act.wait_ge(turned, groups_e.value(t, p, j, g))
                    act.wait_ge(used, groups_e.before(t, 2, p, j, g))
                    act.activation(probT[:, n % 2, 0:w], bank[:, 4, 0:w], ACT.Copy).then_inc(turned_out, 1)

                for p in SUB:
                    side.step(STEPS["gate"])
                    take(p, "gate")
                    for name in ("gate2", "val", "val2"):
                        side.step(STEPS[name])
                    take(p, "q")
                    side.step(STEPS["q"])
                    side.step(STEPS["conv"])
                    for name in "kv":
                        for h in KEYS:
                            take(p, name, h)
                    side.step(STEPS["kv"])
                    for j in range(SLOTS):
                        exps(p, j)
                    side.step(STEPS["first"])
                    for j in QB:
                        for g in quads(j):
                            turned_copy(p, j, g)
                        side.step(STEPS["turn"])
                        if j + SLOTS < CB:
                            exps(p, j + SLOTS)
                        side.step(STEPS["attend"])
                        if j == CB - 1:
                            act.wait_ge(used, groups_e.value(t, p, j, q))
                            act.activation(oT[:, tile(t, p)], bank[:, 5, :], ACT.Copy).then_inc(oT_out, 1)
                        side.step(STEPS["tail"])
                side.finish()

        @block.vector
        def _(dve):
            for s_, e in ((taken, taken_e), (peaked, blocks_e), (inv_ready, blocks_e), (maxed, blocks_e),
                          (inverted, blocks_e), (tapped, taps_e), (roped, roped_e), (padded, subs_e)):
                dve.sem_inc(s_, e.n)
            with dve.Fori(0, HEADS // SUBS) as t:
                side = beside("vector", dve, t, WEIGHT)

                def low_of(p, j):
                    one = slice(j % 2, j % 2 + 1)
                    dve.wait_ge(scored, blocks_e.value(t, p, j))
                    dve.wait_ge(peaked, blocks_e.before(t, 2, p, j))
                    dve.tensor_reduce(peak[:, one], score_banks(j)[:, 0:width(j)], AX.X, ALU.max).then_inc(maxed, 1)
                    dve.wait_ge(maxed, blocks_e.value(t, p, j))
                    dve.wait_ge(exped, blocks_e.before(t, 2, p, j))
                    dve.tensor_scalar(low[:, one], peak[:, one], -SCALE, None, ALU.mult).then_inc(peaked, 1)

                def inv_of(p, j):
                    one = slice(j % 2, j % 2 + 1)
                    dve.wait_ge(exped, blocks_e.value(t, p, j))
                    dve.reciprocal(inv[:, one], total[:, one]).then_inc(inverted, 1)
                    dve.wait_ge(inverted, blocks_e.value(t, p, j))
                    dve.wait_ge(turned, groups_e.value(when(t, p, j, 2), *last_of(p, j, 2), q))
                    dve.tensor_scalar(inv_diag[:, j % 2, :], ident[:, :], inv[:, one], None, ALU.mult).then_inc(inv_ready, 1)

                def conv_start(p):
                    n = proj_e.place[p, "conv", 0] - 1
                    dve.wait_ge(proj, proj_e.value(t, p, "conv", 0))
                    dve.wait_ge(tap_cols, subs_e.value(t, p))
                    dve.tensor_scalar(acc[:, tile(t, p)], bank[:, n % 2, :], w_tap[:, p % 2, TAPS:TAPS + 1], None,
                                      ALU.add).then_inc(taken, 1)

                def taps(p, first, n):
                    for k in range(first, min(first + n, V_TAPS)):
                        if k == 0:
                            dve.wait_ge(taken, taken_e.value(t, p, "conv", 0))
                        else:
                            dve.wait_ge(tapped, taps_e.value(t, p, k - 1))
                        dve.scalar_tensor_tensor(out=acc[:, tile(t, p)], in0=hT[:, NPE + k:NPE + k + C],
                                                 scalar=w_tap[:, p % 2, NPE + k:NPE + k + 1], in1=acc[:, tile(t, p)],
                                                 op0=ALU.mult, op1=ALU.add).then_inc(tapped, 1)
                    return min(first + n, V_TAPS)

                for p in SUB:
                    dve.wait_ge(tapped, taps_e.value(t if p else t - 1, (p - 1) % SUBS, V_TAPS - 1))
                    tail = c.tails[:, bass.ds((SUBS * t + p) * PAD, PAD)]
                    if q == 0:
                        dve.memset(hT[:, 0:PAD], 0.0).then_inc(padded, 1)
                    else:
                        dve.tensor_copy(hT[:, 0:PAD], tail).then_inc(padded, 1)
                    for name in ("gate", "gate2", "val"):
                        side.step(STEPS[name])
                    n = proj_e.place[p, "val", 0] - 1
                    dve.wait_ge(copied, copied_e.value(t, p, "gate", 0))
                    dve.wait_ge(proj, proj_e.value(t, p, "val", 0))
                    dve.tensor_tensor(hT[:, PAD:], bank[:, n % 2, :], sig[:, :], ALU.mult).then_inc(taken, 1)
                    dve.wait_ge(taken, taken_e.value(t, p, "val", 0))
                    dve.wait_ge(padded, subs_e.value(t, p))
                    if q == 0:
                        dve.tensor_copy(tail, hT[:, C:C + PAD])
                    side.step(STEPS["val2"])
                    if p % 2 == 0:
                        for name, dst, table in (("qr", qrT, cosT), ("qs", swapped, sinT)):
                            n = proj_e.place[p, name, 0] - 1
                            dve.wait_ge(proj, proj_e.value(t, p, name, 0))
                            dve.tensor_tensor(dst[:, :], bank[:, n % 2, :], table[:, :], ALU.mult).then_inc(taken, 1)
                        dve.wait_ge(taken, taken_e.value(t, p, "qs", 0))
                        dve.tensor_tensor(qrT[:, :], qrT[:, :], swapped[:, :], ALU.add).then_inc(roped, 1)
                    side.step(STEPS["q"])
                    conv_start(p)
                    k = taps(p, 0, EARLY_TAPS)
                    side.step(STEPS["conv"])
                    side.step(STEPS["kv"])
                    for j in range(SLOTS):
                        low_of(p, j)
                    side.step(STEPS["first"])
                    for j in QB:
                        inv_of(p, j)
                        k = taps(p, k, STEP_TAPS)
                        side.step(STEPS["turn"])
                        if j + SLOTS < CB:
                            low_of(p, j + SLOTS)
                        k = taps(p, k, STEP_TAPS)
                        side.step(STEPS["attend"])
                        k = taps(p, k, STEP_TAPS)
                        side.step(STEPS["tail"])
                    taps(p, k, V_TAPS)
                side.finish()


def mix(c, q, beside):
    split = c.split
    nc, bank, ident, ones = c.nc, c.bank, c.ident, c.ones
    aT, oT, acc = c.aT, c.oT, c.acc
    x4 = acc[:, :].rearrange("p (b d) -> p b d", b=CB)
    h1 = oT[:, :].rearrange("p (b d) -> p b d", b=CB)
    WR, SG, BANKS = 3, 4, 5
    LEAD = 3
    JOBS = [("mean", 0)]
    for d in range(KT):
        JOBS += [("ga", d), ("ya", d)]
    JOBS += [("gc", d) for d in range(LEAD)]
    for d in range(KT):
        JOBS += [("yc", d)] + [("gc", d + LEAD)] * (d + LEAD < KT)
    JOBS += [("o", d) for d in range(KT)]
    TILES = JOBS[1:]
    GATES = [j for j in JOBS if j[0] in ("ga", "gc")]
    assert len(TILES) == 5 * KT
    N = {j: n for n, j in enumerate(JOBS)}
    BY_ACT = [j for j in JOBS if j[0] in ("ga", "gc")]
    BY_DVE = [j for j in JOBS if j[0] not in ("ga", "gc")]

    with ExitStack() as ctx:
        sb, sem = scope(c, ctx, f"q{q}mix_")
        mixT = aT if split else sb("mixT", [P, KT, C])
        w = sb("w", [P, WR, D])
        if split:
            w_parts = sb("w_parts", [P, 2, HR, D], F32R)
            y_parts = sb("y_parts", [P, 2, KT * C], F32R)
        else:
            w_parts = y_parts = None
        a_parts = c.a_parts
        sig = sb("sig", [P, SG, C])
        sq = sb("sq", [P, 2, C])
        mu = sb("mu", [P, C])
        part = sq
        g_ffn = sb("g_ffn", [P, D])
        ss = sb("ss", [P, CB])
        rstd = sb("rstd", [P, CB])
        g_in = sem("g_in")
        x_in = sem("x_in")
        w_in = [sem(f"w_in{r}") for r in range(WR)]
        proj = sem("proj")
        gated = sem("gated")
        taken = sem("taken")
        centred = sem("centred")
        squared = sem("squared")
        summed = sem("summed")
        var_ready = sem("var_ready")
        root_ready = sem("root_ready")
        inv_ready = sem("inv_ready")
        scaled = sem("scaled")
        silued = sem("silued")
        parted = sem("parted")
        mixed = sem("mixed")
        energy = sem("energy")
        normed = sem("normed")
        chain = sem("chain")
        turned = sem("turned")
        turned_out = sem("turned_out")
        stored = sem("stored")
        w_hi_ready = sem("w_hi_ready")
        w_ready = sem("w_ready")
        x_hi_ready = sem("x_hi_ready")
        x_ready = sem("x_ready")
        block = ctx.enter_context(nc.Block())

        def weights_hi(act, i):
            act.wait_ge(w_in[i % WR], 16 * (i // WR + 1))
            if i >= HR:
                act.wait_ge(proj, i - HR + 2)
            act.activation(w_parts[:, 0, i % HR, :], w[:, i % WR, :], ACT.Copy).then_inc(w_hi_ready, 1)

        def weights_lo(dve, i):
            dve.wait_ge(w_hi_ready, i + 1)
            lo_of(dve, w[:, i % WR, :], parts(None, w_parts, i % HR, slice(None))).then_inc(w_ready, 1)

        def ahead(part, eng, *j):
            i = N[j] + 1
            if split and i < TILES.index(("o", 0)):
                part(eng, i)

        cols_of = lambda t, k: t[:, k * C:(k + 1) * C]
        tile_of = lambda k: slice(k * C, (k + 1) * C)
        SPLIT = [(aT[:, k, :], parts(None, a_parts, k, slice(None))) for k in range(KT)]
        SPLIT += [(cols_of(oT, k), parts(None, y_parts, tile_of(k))) for k in range(KT)]
        SPLIT += [(cols_of(acc, k), parts(None, y_parts, tile_of(k))) for k in range(KT)]
        A, Y, CONV = (g * KT for g in range(3))

        def split_hi(act, n):
            if split:
                x, both = SPLIT[n]
                act.activation(both[0], x, ACT.Copy).then_inc(x_hi_ready, 1)

        def split_lo(dve, n):
            if split:
                dve.wait_ge(x_hi_ready, n + 1)
                lo_of(dve, *SPLIT[n]).then_inc(x_ready, 1)

        def bank_free(pe, n):
            if n >= BANKS:
                j = JOBS[n - BANKS]
                if j in BY_ACT:
                    pe.wait_ge(gated, BY_ACT.index(j) + 1)
                else:
                    pe.wait_ge(taken, BY_DVE.index(j) + 1)

        def steps(front, side):
            front("mean", 0); side.step(7)
            for d in range(KT):
                front("a", d); side.step(15)
            front("lead", 0); side.step(7 * LEAD)
            for d in range(KT):
                front("c", d); side.step(14 if d + LEAD < KT else 7)
            for d in range(KT):
                front("o", d); side.step(7)
            front("norm", 0); side.step(2)
            for b in range(CB):
                front("turn", b); side.step(1)
            side.finish()

        WEIGHT = total_weight(steps)

        @block.sync
        def _(sp):
            sp.dma_start(g_ffn[:, :], c.dram["g_ffn"].broadcast_to([P, D])).then_inc(g_in, 16)
            for i, j in enumerate(TILES):
                if i >= WR and split and TILES[i - WR][0] != "o":
                    sp.wait_ge(w_ready, i - WR + 1)
                elif i >= WR:
                    sp.wait_ge(proj, i - WR + 2)
                if j == ("o", 3):
                    sp.wait_ge(proj, N["yc", KT - 1] + 1)
                    sp.dma_start(x4, c.dram["x"][q * C:(q + 1) * C, :].rearrange("(b p) d -> p b d", p=P)
                                 ).then_inc(x_in, 16)
                sp.dma_start(w[:, i % WR, :], c.dram["w_mix"][i]).then_inc(w_in[i % WR], 16)
            for b in range(CB):
                rows = slice((q * CB + b) * P, (q * CB + b + 1) * P)
                sp.wait_ge(taken, len(BY_DVE))
                sp.dma_start(c.h1_dram[rows, :], h1[:, b, :]).then_inc(stored, 16)
                sp.wait_ge(normed, b + 1)
                sp.dma_start(c.xn_dram[rows, :], x4[:, b, :]).then_inc(stored, 16)
            sp.wait_ge(stored, 2 * CB * 16)

        @block.gpsimd
        def _(pool):
            steps(lambda *_: None, beside("pool", pool, None, WEIGHT))

        @block.tensor
        def _(pe):
            def job(j, products):
                n = N[j]
                bank_free(pe, n)
                if n and split and j[0] != "o":
                    pe.wait_ge(w_ready, n)
                elif n:
                    pe.wait_ge(w_in[(n - 1) % WR], 16 * ((n - 1) // WR + 1))
                for lhs, rhs, lo, wd, a, b in products:
                    mm = product(pe, bank[:, n % BANKS, lo:lo + wd], lhs, rhs, a, b)
                mm.then_inc(proj, 1)

            def wt(j, k):
                i, cols = N[j] - 1, slice(k * P, (k + 1) * P)
                return parts(w[:, i % WR, cols], w_parts, i % HR, cols)

            def operand(first):
                return lambda k: SPLIT[first + k][split]

            def ready(first):
                if split:
                    pe.wait_ge(x_ready, first + KT)

            def full(j, x):
                job(j, [(wt(j, k), x(k), 0, C, k == 0, k == KT - 1) for k in range(KT)])

            def front(what, d):
                if what == "mean":
                    job(("mean", 0), [(ones[:, :], cols_of(acc, k), 0, C, k == 0, k == KT - 1) for k in range(KT)])
                if what == "a":
                    ready(A)
                    full(("ga", d), operand(A))
                    ready(Y)
                    full(("ya", d), operand(Y))
                    pe.wait_ge(squared, d + 1)
                    pe.matmul(bank[:, 5, :], ones[:, :], sq[:, d % 2, :], start=(d == 0), stop=(d == KT - 1)).then_inc(summed, 1)
                if what == "lead":
                    for i in range(LEAD):
                        full(("gc", i), operand(A))
                if what == "c":
                    if d == 0:
                        pe.wait_ge(silued, KT)
                        ready(CONV)
                    full(("yc", d), operand(CONV))
                    if d + LEAD < KT:
                        full(("gc", d + LEAD), operand(A))
                if what == "o":
                    if d == 0:
                        pe.wait_ge(mixed, KT)
                    i = (N["o", d] - 1) % WR
                    job(("o", d), [(mixT[:, k, b * P:(b + 1) * P], w[:, i, k * P:(k + 1) * P], b * P, P, k == 0, k == KT - 1)
                                   for b in range(CB) for k in range(KT)])
                if what == "turn":
                    pe.wait_ge(normed, d + 1)
                    for u in range(2):
                        n = 2 * d + u
                        if n < 2:
                            pe.wait_ge(taken, len(BY_DVE))
                        else:
                            pe.wait_ge(turned_out, n - 1)
                        for k in range(4):
                            mm = pe.transpose(bank[:, n % 2, k * P:(k + 1) * P],
                                              x4[:, d, (4 * u + k) * P:(4 * u + k + 1) * P], ident[:, :])
                        mm.then_inc(turned, 1)

            steps(front, beside("tensor", pe, None, WEIGHT))

        @block.scalar
        def _(act):
            def gate(j, g0):
                i = GATES.index(j)
                if i >= SG:
                    old = GATES[i - SG]
                    act.wait_ge(taken, BY_DVE.index(("y" + old[0][1], old[1])) + 1)
                act.wait_ge(proj, N[j] + 1)
                act.activation(sig[:, i % SG, :], bank[:, N[j] % BANKS, :], ACT.Sigmoid,
                               bias=c.gcols[:, g0 + j[1]:g0 + j[1] + 1]).then_inc(gated, 1)

            def front(what, d):
                if what == "mean" and split:
                    weights_hi(act, 0)
                    for k in range(2 * KT):
                        if k == KT:
                            weights_hi(act, 1)
                        split_hi(act, k)
                if what == "a":
                    ahead(weights_hi, act, "ga", d)
                    gate(("ga", d), G_BGATE + KT)
                    ahead(weights_hi, act, "ya", d)
                    act.wait_ge(centred, d + 1)
                    if d >= 2:
                        act.wait_ge(summed, d - 1)
                    act.activation(sq[:, d % 2, :], acc[:, d * C:(d + 1) * C], ACT.Square).then_inc(squared, 1)
                if what == "lead":
                    ahead(weights_hi, act, "gc", 0)
                    act.wait_ge(var_ready, 1)
                    act.activation(mu[:, :], mu[:, :], ACT.Sqrt).then_inc(root_ready, 1)
                    for k in range(KT):
                        t = acc[:, k * C:(k + 1) * C]
                        act.wait_ge(scaled, k + 1)
                        act.activation(t, t, ACT.Silu, bias=c.gcols[:, G_LNB + k:G_LNB + k + 1],
                                       scale=c.gcols[:, G_LNG + k:G_LNG + k + 1]).then_inc(silued, 1)
                    ahead(weights_hi, act, "gc", 1)
                    if split:
                        act.wait_ge(proj, N["ya", KT - 1] + 1)
                        act.wait_ge(silued, KT)
                    for k in range(KT):
                        split_hi(act, CONV + k)
                    for i in range(LEAD):
                        if i == LEAD - 1:
                            ahead(weights_hi, act, "gc", i)
                        gate(("gc", i), G_BGATE)
                if what == "c":
                    ahead(weights_hi, act, "yc", d)
                    if d + LEAD < KT:
                        ahead(weights_hi, act, "gc", d + LEAD)
                        gate(("gc", d + LEAD), G_BGATE)
                if what == "norm":
                    for b in range(CB):
                        act.wait_ge(taken, len(BY_DVE))
                        if b:
                            act.wait_ge(energy, b)
                        act.activation(sig[:, 0:2, :].rearrange("p a n -> p (a n)"), h1[:, b, :], ACT.Square,
                                       accum_out=ss[:, b:b + 1]).then_inc(energy, 1)
                    act.wait_ge(var_ready, 2)
                    act.activation(ss[:, :], ss[:, :], ACT.Sqrt).then_inc(root_ready, 1)
                if what == "turn":
                    for u in range(2):
                        n = 2 * d + u
                        act.wait_ge(turned, n + 1)
                        act.activation(aT[:, 4 * u:4 * u + 4, d * P:(d + 1) * P],
                                       bank[:, n % 2, :].rearrange("p (k n) -> p k n", k=4), ACT.Copy).then_inc(turned_out, 1)
                        if split:
                            act.wait_ge(turned_out, n + 1)
                            act.activation(a_parts[:, 0, 4 * u:4 * u + 4, d * P:(d + 1) * P],
                                           aT[:, 4 * u:4 * u + 4, d * P:(d + 1) * P], ACT.Copy).then_inc(x_hi_ready, 1)

            steps(front, beside("scalar", act, None, WEIGHT))

        @block.vector
        def _(dve):
            count = [0]

            def link(ins):
                count[0] += 1
                ins.then_inc(chain, 1)
                dve.wait_ge(chain, count[0])

            def out_of(j):
                dve.wait_ge(proj, N[j] + 1)
                return bank[:, N[j] % BANKS, :]

            def gated_y(dst, j):
                g = ("g" + j[0][1], j[1])
                dve.wait_ge(gated, BY_ACT.index(g) + 1)
                return dve.tensor_tensor(dst, out_of(j), sig[:, GATES.index(g) % SG, :], ALU.mult).then_inc(taken, 1)

            def front(what, d):
                if what == "mean":
                    if split:
                        weights_lo(dve, 0)
                        for k in range(2 * KT):
                            if k == KT:
                                weights_lo(dve, 1)
                            split_lo(dve, k)
                    dve.tensor_scalar(mu[:, :], out_of(("mean", 0)), 1.0 / D, None, ALU.mult).then_inc(taken, 1)
                    dve.wait_ge(taken, 1)
                if what == "a":
                    t = acc[:, d * C:(d + 1) * C]
                    ahead(weights_lo, dve, "ga", d)
                    if split:
                        dve.wait_ge(x_ready, 2 * KT)
                    dve.tensor_tensor(t, t, mu[:, :], ALU.subtract).then_inc(centred, 1)
                    ahead(weights_lo, dve, "ya", d)
                    gated_y(mixT[:, d, :], ("ya", d))
                if what == "lead":
                    ahead(weights_lo, dve, "gc", 0)
                    dve.wait_ge(summed, KT)
                    dve.wait_ge(centred, KT)
                    dve.tensor_scalar(mu[:, :], bank[:, 5, :], 1.0 / D, EPS, ALU.mult, ALU.add).then_inc(var_ready, 1)
                    dve.wait_ge(root_ready, 1)
                    link(dve.reciprocal(mu[:, :], mu[:, :]))
                    for k in range(KT):
                        t = acc[:, k * C:(k + 1) * C]
                        dve.tensor_tensor(t, t, mu[:, :], ALU.mult).then_inc(scaled, 1)
                    ahead(weights_lo, dve, "gc", 1)
                    for k in range(KT):
                        split_lo(dve, CONV + k)
                    ahead(weights_lo, dve, "gc", LEAD - 1)
                if what == "c":
                    ahead(weights_lo, dve, "yc", d)
                    if d + LEAD < KT:
                        ahead(weights_lo, dve, "gc", d + LEAD)
                    if d >= 2:
                        dve.wait_ge(mixed, d - 1)
                    gated_y(part[:, d % 2, :], ("yc", d))
                    dve.wait_ge(taken, BY_DVE.index(("yc", d)) + 1)
                    dve.tensor_tensor(mixT[:, d, :], mixT[:, d, :], part[:, d % 2, :], ALU.add).then_inc(mixed, 1)
                if what == "o":
                    if d == 0:
                        dve.wait_ge(x_in, 16)
                    cols = slice(d * P, (d + 1) * P)
                    dve.tensor_tensor(h1[:, :, cols], out_of(("o", d)).rearrange("p (b n) -> p b n", b=CB),
                                      x4[:, :, cols], ALU.add).then_inc(taken, 1)
                if what == "norm":
                    dve.wait_ge(energy, CB)
                    dve.tensor_scalar(ss[:, :], ss[:, :], 1.0 / D, EPS, ALU.mult, ALU.add).then_inc(var_ready, 1)
                    dve.wait_ge(root_ready, 2)
                    link(dve.reciprocal(rstd[:, :], ss[:, :]))
                    dve.wait_ge(taken, len(BY_DVE))
                    dve.wait_ge(g_in, 16)
                    for b in range(CB):
                        dve.scalar_tensor_tensor(out=x4[:, b, :], in0=h1[:, b, :], scalar=rstd[:, b:b + 1],
                                                 in1=g_ffn[:, :], op0=ALU.mult, op1=ALU.mult).then_inc(normed, 1)
                if what == "turn" and split:
                    for u in range(2):
                        at = slice(4 * u, 4 * u + 4), slice(d * P, (d + 1) * P)
                        dve.wait_ge(x_hi_ready, 3 * KT + 2 * d + u + 1)
                        lo_of(dve, aT[(slice(None),) + at], parts(None, a_parts, *at)).then_inc(x_ready, 1)

            steps(front, beside("vector", dve, None, WEIGHT))


def peer_scores(c, q, beside, peer):
    FIRST = q * CB
    nc, bank, xnT = c.nc, c.bank, c.aT
    HS = 2 * PH
    WR = 4
    split, a_parts = c.split, c.a_parts
    with ExitStack() as ctx:
        sb, sem = scope(c, ctx, f"q{q}scores_")
        w = sb("w", [P, WR, D])
        w_parts = sb("w_parts", [P, 2, HR, D], F32R) if split else None
        keysT = sb("keysT", [P, HS * NK])
        queryT = sb("queryT", [P, 2, C])
        out = sb("out", [P, 2, C])
        k_in = sem("k_in")
        w_in = [sem(f"w_in{r}") for r in range(WR)]
        proj = sem("proj")
        copied = sem("copied")
        scored = sem("scored")
        out_ready = sem("out_ready")
        w_hi_ready = sem("w_hi_ready")
        w_ready = sem("w_ready")
        fed = sem("fed")
        stored = [sem(f"stored{r}") for r in range(2)]
        block = ctx.enter_context(nc.Block())

        def steps(front, side):
            for i in range(HS + 1):
                front(i)
                side.step(8)
            front("end")
            side.finish()

        WEIGHT = total_weight(steps) * 9 // 8

        def store(sp, i):
            sp.wait_ge(out_ready, i + 1)
            dst = c.sc_dram[q * C + P:(q + 1) * C, i * NK:(i + 1) * NK].rearrange("(b p) n -> p b n", p=P)
            sp.dma_start(dst, out[:, i % 2, P:].rearrange("p (b n) -> p b n", b=CB - 1)).then_inc(stored[i % 2], 16)

        @block.sync
        def _(sp):
            for i in range(HS):
                if i >= WR:
                    sp.wait_ge(proj, i - WR + 1)
                sp.dma_start(w[:, i % WR, :], c.dram["w_peer"][i]).then_inc(w_in[i % WR], 16)
                if i == 0:
                    sp.dma_start(keysT[:, :], c.dram["keysT"]).then_inc(k_in, 16)
                if i >= 3:
                    store(sp, i - 3)
            for i in range(HS - 3, HS):
                store(sp, i)
            for r in range(2):
                sp.wait_ge(stored[r], 16 * (HS // 2))

        @block.gpsimd
        def _(pool):
            if q == 0:
                peer.before("pool", pool)
                pool.iota(peer.iota[:, :], pattern=[[1, TOPK]], base=0, channel_multiplier=0,
                          allow_small_or_imprecise_dtypes=True).then_inc(peer.ready, 1)
            steps(lambda i: None, beside("pool", pool, None, WEIGHT))

        @block.tensor
        def _(pe):
            if q == 0:
                peer.before("tensor", pe)

            def front(i):
                if i == "end":
                    return
                if i < HS:
                    if split:
                        pe.wait_ge(w_ready, i + 1)
                    else:
                        pe.wait_ge(w_in[i % WR], 16 * (i // WR + 1))
                    if i >= 2:
                        pe.wait_ge(copied, i - 1)
                    for k in range(KT):
                        cols = slice(k * P, (k + 1) * P)
                        mm = product(pe, bank[:, i % 2, :], parts(w[:, i % WR, cols], w_parts, i % HR, cols),
                                     parts(xnT[:, k, :], a_parts, k, slice(None)), k == 0, k == KT - 1)
                    mm.then_inc(proj, 1)
                if i:
                    i -= 1
                    if i == 0:
                        pe.wait_ge(k_in, 16)
                    pe.wait_ge(copied, i + 1)
                    if i >= 2:
                        pe.wait_ge(out_ready, i - 1)
                    for b in range(CB):
                        mm = pe.matmul(bank[:, 2 + i % 2, b * P:(b + 1) * P], queryT[:, i % 2, b * P:(b + 1) * P],
                                       keysT[:, i * NK:(i + 1) * NK], start=True, stop=True)
                    mm.then_inc(scored, 1)

            steps(front, beside("tensor", pe, None, WEIGHT))

        @block.scalar
        def _(act):
            def front(i):
                if i == "end":
                    act.sem_inc(peer.sc_in, 16)
                    peer.route_exp(act, FIRST)
                    return
                if split:
                    for n in range(2) if i == 0 else []:
                        weights_hi(act, n)
                    if i + 2 < HS:
                        weights_hi(act, i + 2)
                if i < HS:
                    act.wait_ge(proj, i + 1)
                    if i >= 2:
                        act.wait_ge(scored, i - 1)
                    act.activation(queryT[:, i % 2, :], bank[:, i % 2, :], ACT.Copy).then_inc(copied, 1)
                if i:
                    i -= 1
                    act.wait_ge(scored, i + 1)
                    act.activation(peer.sc[:, i * NK:(i + 1) * NK], bank[:, 2 + i % 2, 0:P], ACT.Copy).then_inc(fed, 1)
                    if i >= 2:
                        act.wait_ge(stored[i % 2], 16 * (i // 2))
                    act.activation(out[:, i % 2, P:], bank[:, 2 + i % 2, P:], ACT.Copy).then_inc(out_ready, 1)

            def weights_hi(act, i):
                act.wait_ge(w_in[i % WR], 16 * (i // WR + 1))
                if i >= HR:
                    act.wait_ge(proj, i - HR + 1)
                act.activation(w_parts[:, 0, i % HR, :], w[:, i % WR, :], ACT.Copy).then_inc(w_hi_ready, 1)

            if q == 0:
                peer.before("scalar", act)
                act.sem_inc(peer.y_out, 16)
            act.wait_ge(peer.routed, peer.ROUTE * (FIRST + 1))
            steps(front, beside("scalar", act, None, WEIGHT))

        @block.vector
        def _(dve):
            if q == 0:
                peer.before("vector", dve)
                dve.wait_ge(peer.ready, 1)
            routing, done = peer.route(dve, FIRST, fed), [0]

            def route_to(n):
                while done[0] < n:
                    next(routing)
                    done[0] += 1

            def front(i):
                for n in [] if i == "end" or not split else [0, 1, 2] if i == 0 else [i + 2]:
                    if n < HS:
                        dve.wait_ge(w_hi_ready, n + 1)
                        lo_of(dve, w[:, n % WR, :], parts(None, w_parts, n % HR, slice(None))).then_inc(w_ready, 1)
                if i == "end":
                    route_to(peer.ROUTE)
                elif i >= 2:
                    route_to(peer.ROUTE_HEAD // 2 * (i - 1))

            steps(front, beside("vector", dve, None, WEIGHT))


class Peer:

    ROUTE_HEAD = 24
    ROUTE = PH * ROUTE_HEAD + 4
    DIAGS = 4
    SPAN, OF_VECTOR = 4, (3,)
    V_PICKS = PICKS // SPAN * len(OF_VECTOR)
    PE_PICKS = PICKS - V_PICKS

    def __init__(self, c, ctx):
        sb, sem = scope(c, ctx, "peer_")
        self.c = c
        self.sc = sb("sc", [P, 2 * PH * NK])
        self.next_index = sb("next_index", [P, PICKS], I32)
        self.next_gates = sb("next_gates", [P, PICKS])
        self.best = sb("best", [P, PICKS])
        self.norm = sb("norm", [P, PH])
        self.top = sb("top", [P, 2, TOPK])
        self.top_at = sb("top_at", [P, 2, TOPK], U32)
        self.top_atf = sb("top_atf", [P, 2, TOPK])
        self.rest = sb("rest", [P, 2, NK])
        self.cand = sb("cand", [P, TOPK * TOPK])
        self.cand_rest = sb("cand_rest", [P, TOPK * TOPK])
        self.place = sb("place", [P, TOPK], U32)
        self.digits = sb("digits", [P, 2, TOPK], U32)
        self.digitsf = sb("digitsf", [P, 2, TOPK])
        self.hit = sb("hit", [P, 2 * TOPK * TOPK])
        self.side_at = sb("side_at", [P, 2 * TOPK])
        self.iota = sb("iota", [P, TOPK])
        self.got = [sem(f"got{r}") for r in range(RING)]
        self.xn_in, self.h1_in, self.sc_in, self.y_out = (sem(n) for n in ("xn_in", "h1_in", "sc_in", "y_out"))
        self.dotted = sem("dotted")
        self.gelued = sem("gelued")
        self.diag_ready = sem("diag_ready")
        self.added = sem("added")
        self.gates_set = sem("gates_set")
        self.index_set = sem("index_set")
        self.routed = sem("routed")
        self.exp_done = sem("exp_done")
        self.summed = sem("summed")
        self.ms_ready = sem("ms_ready")
        self.root_ready = sem("root_ready")
        self.inv_ready = sem("inv_ready")
        self.y_ready = sem("y_ready")
        self.carried = sem("carried")
        self.ready = sem("ready")
        self.coef_ready = sem("coef_ready")
        self.added_v = sem("added_v")
        self.vsum_ready = sem("vsum_ready")

    def rows_buffers(self, c, ctx):
        sb = lambda name, shape, dtype=F32: ctx.enter_context(c.nc.sbuf_tensor("peer_" + name, shape, dtype))
        self.ring = sb("ring", [P, RING, 2 * D])
        self.xn = sb("xn", [P, D])
        self.h1 = sb("h1", [P, D])
        self.vsum = sb("vsum", [P, D])
        self.g_final = sb("g_final", [P, D])
        self.diag = sb("diag", [P, self.DIAGS, P])
        self.dots = sb("dots", [P, PICKS])
        self.coefs = sb("coefs", [P, PICKS])
        self.gates = sb("gates", [P, PICKS])
        self.index = sb("index", [P, PICKS], I32)
        self.ms = sb("ms", [P, 1])
        self.root = sb("root", [P, 1])

    BEFORE = {"tensor": [("added", PE_PICKS)], "scalar": [("gelued", PICKS), ("coef_ready", PICKS), ("diag_ready", PE_PICKS), ("exp_done", 1), ("root_ready", 1)],
              "vector": [("dotted", PICKS), 
                         ("added_v", V_PICKS), ("vsum_ready", 1), ("gates_set", 1), ("routed", ROUTE), ("summed", 2),
                         ("ms_ready", 2), ("inv_ready", 1), ("y_ready", 1)],
              "pool": [("index_set", PH)]}

    def before(self, name, eng):
        for s_, n in self.BEFORE[name]:
            eng.sem_inc({"added": self.added, "gelued": self.gelued, "exp_done": self.exp_done,
                         "root_ready": self.root_ready, "dotted": self.dotted, "diag_ready": self.diag_ready,
                         "gates_set": self.gates_set, "routed": self.routed, "summed": self.summed,
                         "ms_ready": self.ms_ready, "inv_ready": self.inv_ready, "y_ready": self.y_ready,
                         "index_set": self.index_set, "coef_ready": self.coef_ready, "added_v": self.added_v,
                         "vsum_ready": self.vsum_ready}[s_], n)

    def by_vector(self, n):
        return n % self.SPAN in self.OF_VECTOR

    def v_place(self, n):
        return n // self.SPAN * len(self.OF_VECTOR) + sum(k < n % self.SPAN for k in self.OF_VECTOR)

    def pe_place(self, n):
        return n - self.v_place(n)

    def wait_used(self, eng, b, n):
        if self.by_vector(n):
            eng.wait_ge(self.added_v, self.V_PICKS * (b + 1) + self.v_place(n) + 1)
        else:
            eng.wait_ge(self.added, self.PE_PICKS * (b + 1) + self.pe_place(n) + 1)

    def route(self, dve, b, fed=None):
        base, n = self.ROUTE * (b + 1), [0]

        def step(ins):
            n[0] += 1
            ins.then_inc(self.routed, 1)

        def after(k=None):
            dve.wait_ge(self.routed, base + (n[0] if k is None else k))

        def carry():
            after()
            dve.sem_inc(self.carried, 1)

        if fed is None:
            dve.wait_ge(self.sc_in, 16 * (b + 1))
        for h in range(PH):
            if fed is not None:
                dve.wait_ge(fed, 2 * h + 2)
            side = [self.sc[:, (2 * h + i) * NK:(2 * h + i + 1) * NK] for i in range(2)]
            for lo in (0, TOPK // 2):
                of = side if lo == 0 else [self.rest[:, i, :] for i in range(2)]
                some = slice(lo, lo + TOPK // 2)
                for i in range(2):
                    carry()
                    step(dve.max(self.top[:, i, some], of[i])); yield
                for i in range(2):
                    carry()
                    step(dve.max_index(self.top_at[:, i, some], self.top[:, i, some], of[i])); yield
                if lo == 0:
                    for i in range(2):
                        carry()
                        step(dve.match_replace(self.rest[:, i, :], self.top[:, i, some], of[i], LOWEST)); yield
            grid = lambda t: t.rearrange("p (i j) -> p i j", i=TOPK)
            after()
            step(dve.tensor_tensor(grid(self.cand[:, :]), self.top[:, 0, :].unsqueeze(2).broadcast_to([P, TOPK, TOPK]),
                                   self.top[:, 1, :].unsqueeze(1).broadcast_to([P, TOPK, TOPK]), ALU.add)); yield
            best = self.best[:, h * TOPK:(h + 1) * TOPK]
            for lo in (0, TOPK // 2):
                some = slice(lo, lo + TOPK // 2)
                of = self.cand if lo == 0 else self.cand_rest
                carry()
                step(dve.max(best[:, some], of[:, :])); yield
                carry()
                step(dve.max_index(self.place[:, some], best[:, some], of[:, :])); yield
                if lo == 0:
                    carry()
                    step(dve.match_replace(self.cand_rest[:, :], best[:, some], of[:, :], LOWEST)); yield
            after()
            step(dve.tensor_single_scalar(self.digits[:, 0, :], self.place[:, :], 4, ALU.logical_shift_right)); yield
            step(dve.tensor_single_scalar(self.digits[:, 1, :], self.place[:, :], TOPK - 1, ALU.bitwise_and)); yield
            after()
            step(dve.tensor_copy(self.digitsf[:, :, :], self.digits[:, :, :])); yield
            step(dve.tensor_copy(self.top_atf[:, :, :], self.top_at[:, :, :])); yield
            hit3 = self.hit[:, :].rearrange("p (k a) -> p k a", a=TOPK)
            hit4 = self.hit[:, :].rearrange("p (s k a) -> p s k a", s=2, a=TOPK)
            after()
            step(dve.tensor_tensor(hit3, self.digitsf[:, :, :].rearrange("p s k -> p (s k)").unsqueeze(2)
                                   .broadcast_to([P, 2 * TOPK, TOPK]),
                                   self.iota[:, :].unsqueeze(1).broadcast_to([P, 2 * TOPK, TOPK]), ALU.is_equal)); yield
            after()
            step(dve.tensor_tensor(hit4, hit4, self.top_atf[:, :, :].unsqueeze(2)
                                   .broadcast_to([P, 2, TOPK, TOPK]), ALU.mult)); yield
            after()
            step(dve.tensor_reduce(self.side_at[:, :], hit3, AX.X, ALU.add)); yield
            after()
            dve.wait_ge(self.index_set, PH * b + h + 1)
            step(dve.scalar_tensor_tensor(out=self.next_index[:, h * TOPK:(h + 1) * TOPK], in0=self.side_at[:, 0:TOPK],
                                          scalar=float(NK), in1=self.side_at[:, TOPK:], op0=ALU.mult, op1=ALU.add)); yield
            assert n[0] == self.ROUTE_HEAD * (h + 1), n
        heads = lambda t: t[:, :].rearrange("p (h k) -> p h k", h=PH)
        after()
        dve.wait_ge(self.gates_set, b + 1)
        step(dve.tensor_tensor(heads(self.next_gates), heads(self.best),
                               heads(self.best)[:, :, 0:1].broadcast_to([P, PH, TOPK]), ALU.subtract)); yield
        dve.wait_ge(self.exp_done, b + 2)
        step(dve.tensor_reduce(self.norm[:, :], heads(self.next_gates), AX.X, ALU.add)); yield
        after()
        step(dve.reciprocal(self.norm[:, :], self.norm[:, :])); yield
        after()
        step(dve.tensor_tensor(heads(self.next_gates), heads(self.next_gates),
                               self.norm[:, :].unsqueeze(2).broadcast_to([P, PH, TOPK]), ALU.mult)); yield
        assert n[0] == self.ROUTE

    def route_exp(self, act, b):
        act.wait_ge(self.routed, self.ROUTE * (b + 1) + self.ROUTE - 3)
        act.activation(self.next_gates[:, :], self.next_gates[:, :], ACT.Exp).then_inc(self.exp_done, 1)

    def load_scores(self, eng, b):
        eng.wait_ge(self.routed, self.ROUTE * (b + 1))
        eng.dma_start(self.sc[:, :], self.rows("sc_dram", b)).then_inc(self.sc_in, 16)

    def rows(self, name, b):
        return {"sc_dram": self.c.sc_dram, "xn_dram": self.c.xn_dram, "h1_dram": self.c.h1_dram,
                "y": self.c.dram["y"]}[name][bass.ds(b * P, P), :]


class PeerBlock:

    AHEAD = {"pool": 3, "tensor": -5, "scalar": -1, "vector": 0}
    LAG = 2
    ROUTE_FROM = 4
    ROUTE_EXP = PICKS - 2 * RING

    def __init__(self, peer, name, eng, b, route, weight, start=0):
        self.p, self.name, self.eng, self.b, self.route = peer, name, eng, b, route
        self.weight, self.start = weight, start
        self.n = self.passed = self.done = 0
        self.part = {"pool": self.fetch, "tensor": self.add, "scalar": self.gelu, "vector": self.dot}[name]
        self.routing = peer.route(eng, b + 1) if route and name == "vector" else None
        if name == "scalar":
            self.loads()

    def step(self, weight):
        self.passed += weight
        self.upto(PICKS * (self.passed - self.start) // (self.weight - self.start) + self.AHEAD[self.name])

    def upto(self, n):
        while self.n < min(n, PICKS):
            self.part(self.n)
            self.n += 1

    def finish(self):
        assert self.passed <= self.weight
        self.upto(PICKS)
        if self.name == "vector":
            self.close()
        if self.name == "scalar":
            self.close_root()

    def fetch(self, n):
        p, pool, b, r = self.p, self.eng, self.b, n % RING
        if n % TOPK == 0:
            h = n // TOPK
            cols = slice(n, n + TOPK)
            pool.wait_ge(p.routed, p.ROUTE * (b + 2))
            pool.sem_inc(self.p.c.passed, 1)
            pool.tensor_copy(p.index[:, cols], p.next_index[:, cols]).then_inc(p.index_set, 1)
            pool.wait_ge(p.index_set, PH * (b + 1) + h + 1)
        p.wait_used(pool, b, n - RING)
        pool.sem_inc(self.p.c.passed, 1)
        pool.indirect_dma_start(out=p.ring[:, r, :], out_offset=None, in_=p.c.dram["uv"],
                                in_offset=bass.IndirectOffsetOnAxis(ap=p.index[:, n:n + 1], axis=0)).then_inc(p.got[r], 16)

    def dot(self, n):
        p, dve, b, r = self.p, self.eng, self.b, n % RING
        if n == 0:
            dve.wait_ge(p.routed, p.ROUTE * (b + 2))
            dve.wait_ge(p.coef_ready, PICKS * (b + 1))
            dve.tensor_copy(p.gates[:, :], p.next_gates[:, :]).then_inc(p.gates_set, 1)
            dve.wait_ge(p.xn_in, 16 * (b + 1))
        row = p.ring[:, r, 0:D]
        dve.wait_ge(p.got[r], 16 * (PICKS // RING) * b + 16 * (n // RING + 1))
        dve.tensor_tensor_reduce(row, row, p.xn[:, :], 1.0, 0.0, ALU.mult, ALU.add,
                                 p.dots[:, n:n + 1]).then_inc(p.dotted, 1)
        if n >= self.LAG:
            self.add_here(n - self.LAG)
        if self.routing and n >= self.ROUTE_FROM:
            todo = p.ROUTE if n >= self.ROUTE_EXP + 2 else min(
                p.ROUTE - 3, -(-p.ROUTE * (n + 1 - self.ROUTE_FROM) // (self.ROUTE_EXP - self.ROUTE_FROM)))
            while self.done < todo:
                next(self.routing)
                self.done += 1

    def add_here(self, n):
        p, dve, b = self.p, self.eng, self.b
        if not p.by_vector(n):
            return
        k = p.v_place(n)
        row, coef = p.ring[:, n % RING, D:], p.coefs[:, n:n + 1]
        dve.wait_ge(p.coef_ready, PICKS * (b + 1) + n + 1)
        if k == 0:
            dve.wait_ge(p.vsum_ready, b + 1)
            ins = dve.tensor_scalar(p.vsum[:, :], row, coef, None, ALU.mult)
        else:
            dve.wait_ge(p.added_v, p.V_PICKS * (b + 1) + k)
            ins = dve.scalar_tensor_tensor(out=p.vsum[:, :], in0=row, scalar=coef, in1=p.vsum[:, :],
                                           op0=ALU.mult, op1=ALU.add)
        ins.then_inc(p.added_v, 1)

    def close(self):
        p, dve, b = self.p, self.eng, self.b
        for n in range(PICKS - self.LAG, PICKS):
            self.add_here(n)
        dve.wait_ge(p.h1_in, 16 * (b + 1))
        dve.wait_ge(p.added_v, p.V_PICKS * (b + 2))
        dve.tensor_tensor(p.h1[:, :], p.h1[:, :], p.vsum[:, :], ALU.add).then_inc(p.vsum_ready, 1)
        dve.wait_ge(p.vsum_ready, b + 2)
        dve.wait_ge(p.added, p.PE_PICKS * (b + 2))
        for h in range(2):
            cols = slice(h * C, (h + 1) * C)
            dve.tensor_tensor(p.h1[:, cols], p.h1[:, cols], p.c.bank[:, 6 + h, :], ALU.add).then_inc(p.summed, 1)
        dve.wait_ge(p.summed, 2 * (b + 2))
        squares = p.c.bank[:, 6:8, :].rearrange("p a n -> p (a n)")
        dve.tensor_tensor_reduce(squares, p.h1[:, :], p.h1[:, :], 1.0, 0.0, ALU.mult, ALU.add,
                                 p.ms[:, :]).then_inc(p.ms_ready, 1)
        dve.wait_ge(p.ms_ready, 2 * (b + 1) + 1)
        dve.tensor_scalar(p.ms[:, :], p.ms[:, :], 1.0 / D, EPS, ALU.mult, ALU.add).then_inc(p.ms_ready, 1)
        dve.wait_ge(p.root_ready, b + 2)
        dve.reciprocal(p.root[:, :], p.root[:, :]).then_inc(p.inv_ready, 1)
        dve.wait_ge(p.inv_ready, b + 2)
        dve.scalar_tensor_tensor(out=p.h1[:, :], in0=p.h1[:, :], scalar=p.root[:, 0:1], in1=p.g_final[:, :],
                                 op0=ALU.mult, op1=ALU.mult).then_inc(p.y_ready, 1)

    def loads(self):
        p, act, b = self.p, self.eng, self.b
        act.wait_ge(p.dotted, PICKS * (b + 1))
        act.dma_start(p.xn[:, :], p.rows("xn_dram", b)).then_inc(p.xn_in, 16)
        if self.route:
            p.load_scores(act, b + 1)

    def gelu(self, n):
        p, act, b = self.p, self.eng, self.b
        if n == 8:
            act.wait_ge(p.y_out, 16 * (b + 1))
            act.dma_start(p.h1[:, :], p.rows("h1_dram", b)).then_inc(p.h1_in, 16)
        if self.route and n == self.ROUTE_EXP:
            p.route_exp(act, b + 1)
        if n == 0:
            act.wait_ge(p.added_v, p.V_PICKS * (b + 1))
            act.wait_ge(p.gates_set, b + 2)
        coef = p.coefs[:, n:n + 1]
        act.wait_ge(p.dotted, PICKS * (b + 1) + n + 1)
        act.activation(coef, p.dots[:, n:n + 1], ACT.Gelu).then_inc(p.gelued, 1)
        act.wait_ge(p.gelued, PICKS * (b + 1) + n + 1)
        act.activation(coef, coef, ACT.Copy, scale=p.gates[:, n:n + 1]).then_inc(p.coef_ready, 1)
        if not p.by_vector(n):
            m = p.pe_place(n)
            act.wait_ge(p.coef_ready, PICKS * (b + 1) + n + 1)
            act.wait_ge(p.added, p.PE_PICKS * (b + 1) + m + 1 - p.DIAGS)
            act.activation(p.diag[:, m % p.DIAGS, :], p.c.ident[:, :], ACT.Copy, scale=coef).then_inc(p.diag_ready, 1)

    def close_root(self):
        p, act, b = self.p, self.eng, self.b
        act.wait_ge(p.ms_ready, 2 * (b + 2))
        act.activation(p.root[:, :], p.ms[:, :], ACT.Sqrt).then_inc(p.root_ready, 1)
        act.wait_ge(p.y_ready, b + 2)
        act.dma_start(p.rows("y", b), p.h1[:, :]).then_inc(p.y_out, 16)

    def add(self, n):
        p, pe, b, r = self.p, self.eng, self.b, n % RING
        if p.by_vector(n):
            return
        m = p.pe_place(n)
        if n == 0:
            pe.wait_ge(p.ms_ready, 2 * b + 1 + 1)
        pe.wait_ge(p.diag_ready, p.PE_PICKS * (b + 1) + m + 1)
        for h in range(2):
            mm = pe.matmul(p.c.bank[:, 6 + h, :], p.diag[:, m % p.DIAGS, :], p.ring[:, r, D + h * C:D + (h + 1) * C],
                           start=(n == 0), stop=(m == p.PE_PICKS - 1))
        mm.then_inc(p.added, 1)


def peer_blocks(c, peer, b0):
    nc, last = c.nc, S // P - 1
    with ExitStack() as ctx:
        block = ctx.enter_context(nc.Block())

        def run(name, eng):
            with eng.Fori(b0, last) as b:
                PeerBlock(peer, name, eng, b, True, 1).finish()
            PeerBlock(peer, name, eng, last, False, 1).finish()

        @block.gpsimd
        def _(pool):
            run("pool", pool)

        @block.tensor
        def _(pe):
            run("tensor", pe)

        @block.scalar
        def _(act):
            run("scalar", act)
            act.wait_ge(peer.y_out, 16 * (last + 2))

        @block.vector
        def _(dve):
            run("vector", dve)


def build(nc, dram):
    c = Chip()
    c.nc, c.dram = nc, dram
    with ExitStack() as ctx:
        sb = lambda n, s, d=F32: ctx.enter_context(nc.sbuf_tensor(n, s, d))
        c.bank = ctx.enter_context(nc.psum_tensor("bank", [P, 8, C], F32))
        c.passed = ctx.enter_context(nc.semaphore("passed"))
        scratch = lambda n, s: nc.dram_tensor(n, s, F32, kind="Internal").ap()
        c.h1_dram = scratch("h1_dram", [S, D])
        c.xn_dram = scratch("xn_dram", [S, D])
        c.sc_dram = scratch("sc_dram", [S, 2 * PH * NK])
        c.ident = sb("ident", [P, P])
        c.ones = sb("ones", [P, P])
        c.gcols = sb("gcols", [P, G_COLS])
        c.mask = sb("mask", [P, P])
        c.wdw = sb("wdw", [P, KT * (TAPS + 1)])
        c.tails = sb("tails", [P, KT * PAD])
        c.ckvT = sb("ckvT", [P, S])
        c.krT = sb("krT", [P, S])
        with ExitStack() as rest:
            peer = Peer(c, rest)
            front(c, 0, peer)
            peer.rows_buffers(c, rest)
            front(c, 1, peer)
            peer_blocks(c, peer, CB)


def front(c, q, peer):
    nc = c.nc

    def beside(b, route):
        if q == 0:
            return lambda *_: Alone()
        return lambda name, eng, t, weight: PeerBlock(peer, name, eng, b if t is None else t + b, route, weight,
                                                      weight // 16 if t is None else 0)

    with ExitStack() as ctx:
        sb = lambda n, s, d=F32: ctx.enter_context(nc.sbuf_tensor(f"q{q}_{n}", s, d))
        c.aT = sb("aT", [P, KT, C])
        c.oT = sb("oT", [P, HEADS * C])
        c.acc = sb("acc", [P, KT * C])
        with ExitStack() as ctx2:
            sb = lambda n, s, d=F32: ctx2.enter_context(nc.sbuf_tensor(f"q{q}_{n}", s, d))
            c.cqT = sb("cqT", [P, QT, C])
            c.cosT = sb("cosT", [P, C])
            c.sinT = sb("sinT", [P, C])
            mixer_inputs(c, q, peer)
            mixers(c, q, beside(0, True))
        c.split = q == 0
        c.a_parts = ctx.enter_context(nc.sbuf_tensor(f"q{q}_a_parts", [P, 2, KT, C], F32R)) if c.split else None
        mix(c, q, beside(2, True))
        peer_scores(c, q, beside(3, False), peer)


def lay_out(i):
    tile = lambda w: w.reshape(w.shape[0] // P, P, -1).transpose(1, 0, 2)
    cols = lambda v: v.reshape(-1, P).T
    w_in, r = i["w_in"][0], np.arange(ROPE)
    swap = (r + ROPE // 2) % ROPE
    o_gate, o_q, o_kv = D, 2 * D, 2 * D + QL
    o_kr = o_kv + P
    o_mix = o_kr + ROPE
    kr = np.concatenate([r, r])
    pick = lambda cs: tile(w_in[:, cs]).reshape(P, -1)
    at = lambda o: np.arange(o, o + P)
    w_uq = tile(i["w_uq"][0]).reshape(P, QT, HEADS, NOPE + ROPE)
    w_ukv = i["w_ukv"][0].reshape(P, HEADS, NOPE + VDIM)
    by_tile = lambda w: np.stack([tile(w[:, o:o + P]).reshape(P, -1) for o in range(0, w.shape[1], P)])
    ga, gc = by_tile(w_in[:, o_mix + D:]), by_tile(w_in[:, o_mix:o_mix + D])
    ya, yc, yo = by_tile(i["w_attn_out"][0]), by_tile(i["w_conv_out"][0]), by_tile(i["w_o"][0])
    lead = 3
    w_mix = [t for d in range(KT) for t in (ga[d], ya[d])] + [gc[d] for d in range(lead)]
    for d in range(KT):
        w_mix += [yc[d]] + ([gc[d + lead]] if d + lead < KT else [])
    w_mix = np.stack(w_mix + list(yo))
    half = ROPE // 2
    freq = np.float32(ROPE_BASE) ** (-np.arange(half, dtype=np.float32) / np.float32(half))
    sign = np.repeat(np.array([-1, 1, -1, 1], np.float32), half)
    return {
        "x": i["x"][0],
        "xT": i["x"][0].T.reshape(KT, P, S),
        "pos": i["positions"],
        "rope": np.stack([np.tile(freq, 4), sign], 1).astype(np.float32),
        "gcols": np.concatenate([cols(i[n][0]) for n in ("mix_norm_g", "q_norm_g", "kv_norm_g", "conv_ln_g",
                                                          "conv_ln_b", "b_gate")], 1),
        "wdw": np.concatenate([i["w_dw"][0, :, 0], i["b_dw"]], 0).reshape(TAPS + 1, KT, P)
                 .transpose(2, 1, 0).reshape(P, -1),
        "w_pre": np.stack([pick(at(o_q)), pick(at(o_q + P)), pick(at(o_kv)), pick(o_kr + kr),
                           pick(o_kr + swap[kr])]),
        "w_vg": np.stack([pick(at(o + h * P)) for h in range(KT) for o in (o_gate, 0)]),
        "w_head": np.stack([np.concatenate([w_uq[:, :, h, :NOPE].reshape(P, -1), w_ukv[:, h, :NOPE],
                                            w_ukv[:, h, NOPE:]], 1) for h in range(HEADS)]),
        "w_rope": np.stack([np.concatenate([w_uq[:, :, h:h + 2, NOPE + rs].reshape(P, -1) for rs in (r, swap)], 1)
                            for h in range(0, HEADS, 2)]),
        "w_mix": w_mix,
        "g_ffn": i["ffn_norm_g"],
        "w_peer": by_tile(i["w_peer_q"][0]),
        "keysT": i["peer_sub_keys"][0].transpose(3, 0, 1, 2).reshape(P, -1),
        "uv": np.concatenate([i["peer_u"][0], i["peer_v"][0]], 1),
        "g_final": i["final_norm_g"][None],
    }


def kernel(**inputs):
    import concourse.bacc as bacc
    from concourse.bass_utils import run_bass_kernel_spmd

    nc = bacc.Bacc("TRN2", target_bir_lowering=False, num_devices=1)
    arrays, dram = {}, {}
    for name, a in lay_out({k: np.asarray(v) for k, v in inputs.items()}).items():
        arrays["in_" + name] = np.ascontiguousarray(a)
        dram[name] = nc.dram_tensor("in_" + name, a.shape, mybir.dt.from_np(a.dtype), kind="ExternalInput").ap()
    dram["y"] = nc.dram_tensor("out_y", (S, D), F32, kind="ExternalOutput").ap()
    build(nc, dram)
    return run_bass_kernel_spmd(nc, [arrays], core_ids=[0]).results[0]["out_y"].reshape(1, S, D)
```
